# Optimizing a Trainium2 kernel written in Bass

```python
import math
import jax, jax.numpy as jnp
from jax import lax
import numpy as np

D_MODEL = 1024
BATCH = 1
SEQ = 128
DEPTH = 2
DEC_BATCH = 1
DEC_SEQ = 256
PAST_LEN = 128

GRID_W = 64
N_EVEN = (DEPTH + 1) // 2
N_ODD = DEPTH // 2
H_A = 4
DK_A = D_MODEL // 16
DV_A = D_MODEL // 8
GK_RANK = 16
GATE_TEMP = 16.0
H_B = 4
DK_B = D_MODEL // 16
DV_B = D_MODEL // 8
CHUNK = 64
REC_SIZES = (H_A * DK_A, H_A * DK_A, H_A * DV_A, H_A * DV_A, H_B * DK_B, H_B * DK_B, H_B * DV_B, H_B * DV_B, 2 * GK_RANK, 4 * H_B)
REC_IN = sum(REC_SIZES)
REC_OUT = H_A * DV_A + H_B * DV_B
HY_ORDER = 2
HY_EMB = 33
HY_BANDS = (HY_EMB - 1) // 2
HY_FFN = 64
HY_TARGET = 1e-2
HY_FAST_PCT = 0.3
HY_SLOW_PCT = 1.5
HY_MAX_DECAY = abs(math.log(HY_TARGET)) / HY_FAST_PCT
HY_MIN_DECAY = abs(math.log(HY_TARGET)) / HY_SLOW_PCT
N_GROUPS = 4
EXP_PER_GROUP = 4
N_EXPERTS = N_GROUPS * EXP_PER_GROUP
TOP_K = 2
D_EXPERT = D_MODEL // 2
N_MOD = 6
POS_THETA = 10000.0
EPS = 1e-6

kernel_name = 'hybrid_prefix_diffusion_gla_mlstm_hyena_hmoe'

def _rmsnorm(x, w):
    x32 = x.astype(jnp.float32)
    y = x32 * lax.rsqrt(jnp.mean(x32 * x32, axis=-1, keepdims=True) + EPS)
    return (y * w.astype(jnp.float32)).astype(x.dtype)

def _modulate(x, w, shift, scale):
    return _rmsnorm(x, w) * (1.0 + scale) + shift

def _ada(cvec, w, b):
    m = jax.nn.silu(cvec) @ w + b
    return jnp.split(m[:, None, :], N_MOD, axis=-1)

def _grid_pos_embed(L):
    f32 = jnp.float32
    rows = L // GRID_W
    r, cl = jnp.meshgrid(jnp.arange(rows, dtype=f32), jnp.arange(GRID_W, dtype=f32), indexing='ij')
    quarter = D_MODEL // 4
    omega = POS_THETA ** (-jnp.arange(quarter, dtype=f32) / quarter)
    def enc(pos):
        a = pos.reshape(-1, 1) * omega[None, :]
        return jnp.concatenate([jnp.sin(a), jnp.cos(a)], axis=-1)
    return jnp.concatenate([enc(r), enc(cl)], axis=-1)

def _to_chunks(t):
    b, l = t.shape[0], t.shape[1]
    return jnp.moveaxis(t.reshape((b, l // CHUNK, CHUNK) + t.shape[2:]), 1, 0)

def _from_chunks(t):
    t = jnp.moveaxis(t, 0, 1)
    return t.reshape((t.shape[0], t.shape[1] * t.shape[2]) + t.shape[3:])

def _gla_scan(q, k, v, g, s0):
    mask = jnp.tril(jnp.ones((CHUNK, CHUNK), dtype=bool))
    def step(S, inp):
        qc, kc, vc, gc = inp
        b = jnp.cumsum(gc, axis=1)
        qe = qc * jnp.exp(b)
        ke = kc * jnp.exp(-b)
        A = jnp.where(mask, jnp.einsum('bthk,bshk->bhts', qe, ke), 0.0)
        o = jnp.einsum('bhts,bshv->bthv', A, vc) + jnp.einsum('bthk,bhkv->bthv', qe, S)
        b_end = b[:, -1]
        S = jnp.exp(b_end)[..., None] * S + jnp.einsum('bshk,bshv->bhkv', kc * jnp.exp(b_end[:, None] - b), vc)
        return S, o
    s_fin, o = lax.scan(step, s0.astype(jnp.float32), (_to_chunks(q), _to_chunks(k), _to_chunks(v), _to_chunks(g)))
    return _from_chunks(o), s_fin

def _mlstm_scan(q, k, v, ig, lf, c0, n0, m0):
    mask = jnp.tril(jnp.ones((CHUNK, CHUNK), dtype=bool))
    def step(carry, inp):
        Cm, n, m = carry
        qc, kc, vc, ic, fc = inp
        b = jnp.cumsum(fc, axis=1).transpose(0, 2, 1)
        it = ic.transpose(0, 2, 1)
        dlog = jnp.where(mask, b[..., :, None] - b[..., None, :] + it[..., None, :], -jnp.inf)
        inter = b + m[..., None]
        m_t = jnp.maximum(inter, jnp.max(dlog, axis=-1))
        w = jnp.exp(dlog - m_t[..., None])
        a_in = jnp.exp(inter - m_t).transpose(0, 2, 1)[..., None]
        s = jnp.einsum('bthk,bshk->bhts', qc, kc) * w
        num = jnp.einsum('bhts,bshv->bthv', s, vc) + a_in * jnp.einsum('bthk,bhkv->bthv', qc, Cm)
        den = jnp.sum(s, axis=-1).transpose(0, 2, 1)[..., None] + a_in * jnp.einsum('bthk,bhk->bth', qc, n)[..., None]
        h = num / jnp.maximum(jnp.abs(den), jnp.exp(-m_t).transpose(0, 2, 1)[..., None])
        b_end = b[..., -1]
        dend = b_end[..., None] - b + it
        m_new = jnp.maximum(b_end + m, jnp.max(dend, axis=-1))
        w_end = jnp.exp(dend - m_new[..., None])
        decay = jnp.exp(b_end + m - m_new)
        Cm = decay[..., None, None] * Cm + jnp.einsum('bhs,bshk,bshv->bhkv', w_end, kc, vc)
        n = decay[..., None] * n + jnp.einsum('bhs,bshk->bhk', w_end, kc)
        return (Cm, n, m_new), h
    f32 = jnp.float32
    fin, h = lax.scan(step, (c0.astype(f32), n0.astype(f32), m0.astype(f32)),
                      (_to_chunks(q), _to_chunks(k), _to_chunks(v), _to_chunks(ig), _to_chunks(lf)))
    return _from_chunks(h), fin

def _rec_mixer(u, st_gla, st_c, st_n, st_m, p, j):
    f32 = jnp.float32
    bsz, L, _ = u.shape
    proj = (u @ p['rec_w_in'][j]).astype(f32)
    offs = np.cumsum(REC_SIZES)[:-1].tolist()
    qa, ka, va, ra, qb, kb, vb, ob, gk_lr, mg = jnp.split(proj, offs, axis=-1)
    qa = qa.reshape(bsz, L, H_A, DK_A) * (DK_A ** -0.5)
    ka = ka.reshape(bsz, L, H_A, DK_A)
    va = va.reshape(bsz, L, H_A, DV_A)
    glog = jax.nn.log_sigmoid(jnp.einsum('bldr,drk->bldk', gk_lr.reshape(bsz, L, 2, GK_RANK), p['gla_gk_w'][j].astype(f32))
                              + p['gla_gk_b'][j].astype(f32)) / GATE_TEMP
    glog = glog.reshape(bsz, L, 2, H_A, DK_A)
    qb = qb.reshape(bsz, L, H_B, DK_B) * (DK_B ** -0.5)
    kb = kb.reshape(bsz, L, H_B, DK_B)
    vb = vb.reshape(bsz, L, H_B, DV_B)
    mg = mg.reshape(bsz, L, 2, 2, H_B) + p['mlstm_gate_b'][j].astype(f32)
    ig = mg[:, :, :, 0]
    lf = jax.nn.log_sigmoid(mg[:, :, :, 1])
    rev = lambda t: t[:, ::-1]
    oa_f, sa_f = _gla_scan(qa, ka, va, glog[:, :, 0], st_gla[:, 0])
    oa_b, sa_b = _gla_scan(rev(qa), rev(ka), rev(va), rev(glog[:, :, 1]), st_gla[:, 1])
    hb_f, (c_f, n_f, m_f) = _mlstm_scan(qb, kb, vb, ig[:, :, 0], lf[:, :, 0], st_c[:, 0], st_n[:, 0], st_m[:, 0])
    hb_b, (c_b, n_b, m_b) = _mlstm_scan(rev(qb), rev(kb), rev(vb), rev(ig[:, :, 1]), rev(lf[:, :, 1]), st_c[:, 1], st_n[:, 1], st_m[:, 1])
    out_a = _rmsnorm(oa_f + rev(oa_b), p['gla_norm_w'][j]).reshape(bsz, L, H_A * DV_A) * jax.nn.silu(ra)
    out_b = _rmsnorm(hb_f + rev(hb_b), p['mlstm_norm_w'][j]).reshape(bsz, L, H_B * DV_B) * jax.nn.sigmoid(ob)
    mix = jnp.concatenate([out_a, out_b], axis=-1).astype(u.dtype) @ p['rec_w_out'][j]
    states = (jnp.stack([sa_f, sa_b], axis=1), jnp.stack([c_f, c_b], axis=1),
              jnp.stack([n_f, n_b], axis=1), jnp.stack([m_f, m_b], axis=1))
    return mix, states

def _hyena_filters(L, p, j):
    f32 = jnp.float32
    t = jnp.linspace(0.0, 1.0, L, dtype=f32)[:, None]
    w = 2.0 * math.pi * jnp.arange(L, dtype=f32)[:, None] / L
    f = jnp.linspace(1e-4, HY_BANDS - 1, HY_BANDS, dtype=f32)[None, :]
    emb = jnp.concatenate([t, jnp.cos(f * w), -jnp.sin(f * w)], axis=-1)
    h = jnp.sin(p['hy_f_freq1'][j].astype(f32) * (emb @ p['hy_f_w1'][j].astype(f32) + p['hy_f_b1'][j].astype(f32)))
    h = jnp.sin(p['hy_f_freq2'][j].astype(f32) * (h @ p['hy_f_w2'][j].astype(f32) + p['hy_f_b2'][j].astype(f32)))
    h = (h @ p['hy_f_w3'][j].astype(f32)).reshape(L, HY_ORDER, 2, D_MODEL)
    decay = jnp.exp(-t * jnp.linspace(HY_MIN_DECAY, HY_MAX_DECAY, D_MODEL, dtype=f32)[None, :])
    h = h * decay[:, None, None, :]
    h_fwd, h_bwd = h[:, :, 0], h[:, :, 1]
    k = jnp.concatenate([h_fwd, jnp.zeros((1, HY_ORDER, D_MODEL), f32), h_bwd[1:][::-1]], axis=0)
    return jnp.fft.rfft(k, axis=0)

def _hyena_mixer(u, p, j):
    f32 = jnp.float32
    L = u.shape[1]
    z = u @ p['hy_w_in'][j]
    z = lax.conv_general_dilated(z, p['hy_conv_w'][j][:, None, :], window_strides=(1,), padding='SAME',
                                 dimension_numbers=('NWC', 'WIO', 'NWC'), feature_group_count=3 * D_MODEL)
    v, x1, x2 = jnp.split(z.astype(f32), 3, axis=-1)
    kf = _hyena_filters(L, p, j)
    bias = p['hy_f_bias'][j].astype(f32)
    def long_conv(s, o):
        y = jnp.fft.irfft(jnp.fft.rfft(s, n=2 * L, axis=1) * kf[None, :, o], n=2 * L, axis=1)[:, :L]
        return y + bias[o] * s
    y = x2 * long_conv(x1 * long_conv(v, 0), 1)
    return y.astype(u.dtype) @ p['hy_w_out'][j]

def _hier_moe(u, p, l):
    f32 = jnp.float32
    g_logits = (u @ p['moe_w_group'][l] + p['moe_b_group'][l]).astype(f32)
    g_idx = jnp.argmax(g_logits, axis=-1)
    g_oh = jax.nn.one_hot(g_idx, N_GROUPS, dtype=f32)
    p_group = jnp.sum(jax.nn.softmax(g_logits, axis=-1) * g_oh, axis=-1)
    e_logits = (u @ p['moe_w_router'][l] + p['moe_b_router'][l]).astype(f32)
    e_logits = e_logits.reshape(u.shape[:2] + (N_GROUPS, EXP_PER_GROUP))
    e_in = jnp.einsum('blge,blg->ble', e_logits, g_oh)
    top_v, top_i = lax.top_k(e_in, TOP_K)
    w = jax.nn.softmax(top_v, axis=-1) * p_group[..., None]
    ids = g_idx[..., None] * EXP_PER_GROUP + top_i
    gates = jnp.einsum('blke,blk->ble', jax.nn.one_hot(ids, N_EXPERTS, dtype=f32), w)
    hg = jnp.einsum('bld,edf->blef', u, p['moe_w_gate'][l])
    hu = jnp.einsum('bld,edf->blef', u, p['moe_w_up'][l])
    h = jax.nn.silu(hg) * hu * gates.astype(u.dtype)[..., None]
    return jnp.einsum('blef,efd->bld', h, p['moe_w_down'][l])

def _trunk(x, cvec, init_states, p):
    finals = []
    for l in range(DEPTH):
        j = l // 2
        sh1, sc1, g1, sh2, sc2, g2 = _ada(cvec, p['ada_w'][l], p['ada_b'][l])
        h = _modulate(x, p['norm1_w'][l], sh1, sc1)
        if l % 2 == 0:
            mix, st = _rec_mixer(h, *init_states[j], p, j)
            finals.append(st)
        else:
            mix = _hyena_mixer(h, p, j)
        x = x + g1 * mix
        h = _modulate(x, p['norm2_w'][l], sh2, sc2)
        x = x + g2 * _hier_moe(h, p, l)
    return _rmsnorm(x, p['norm_f_w']), finals

def setup_inputs(seed: int = 0) -> dict:
    key = jax.random.key(seed)
    ks = iter(jax.random.split(key, 48))
    f32 = jnp.float32
    def nrm(shape, scale):
        return jax.random.normal(next(ks), shape, f32) * scale
    gate_b = nrm((N_EVEN, 2, 2, H_B), 0.1) + jnp.array([0.0, 3.0], f32)[None, None, :, None]
    return {
        'x_prompt': nrm((BATCH, SEQ, D_MODEL), 1.0),
        'x_sample': nrm((DEC_BATCH, DEC_SEQ, D_MODEL), 1.0),
        'state_gla': nrm((DEC_BATCH, N_EVEN, 2, H_A, DK_A, DV_A), 0.5),
        'state_mlstm_c': nrm((DEC_BATCH, N_EVEN, 2, H_B, DK_B, DV_B), 0.5),
        'state_mlstm_n': nrm((DEC_BATCH, N_EVEN, 2, H_B, DK_B), 0.5),
        'state_mlstm_m': nrm((DEC_BATCH, N_EVEN, 2, H_B), 1.0),
        'c': nrm((DEC_BATCH, D_MODEL), 1.0),
        'c_ctx': nrm((D_MODEL,), 1.0),
        'norm1_w': 1.0 + nrm((DEPTH, D_MODEL), 0.02),
        'norm2_w': 1.0 + nrm((DEPTH, D_MODEL), 0.02),
        'norm_f_w': 1.0 + nrm((D_MODEL,), 0.02),
        'ada_w': nrm((DEPTH, D_MODEL, N_MOD * D_MODEL), D_MODEL ** -0.5),
        'ada_b': nrm((DEPTH, N_MOD * D_MODEL), 0.02),
        'rec_w_in': nrm((N_EVEN, D_MODEL, REC_IN), D_MODEL ** -0.5),
        'gla_gk_w': nrm((N_EVEN, 2, GK_RANK, H_A * DK_A), GK_RANK ** -0.5),
        'gla_gk_b': nrm((N_EVEN, 2, H_A * DK_A), 0.1),
        'mlstm_gate_b': gate_b,
        'gla_norm_w': 1.0 + nrm((N_EVEN, DV_A), 0.02),
        'mlstm_norm_w': 1.0 + nrm((N_EVEN, DV_B), 0.02),
        'rec_w_out': nrm((N_EVEN, REC_OUT, D_MODEL), REC_OUT ** -0.5),
        'hy_w_in': nrm((N_ODD, D_MODEL, 3 * D_MODEL), D_MODEL ** -0.5),
        'hy_conv_w': nrm((N_ODD, 3, 3 * D_MODEL), 3 ** -0.5),
        'hy_f_w1': nrm((N_ODD, HY_EMB, HY_FFN), HY_EMB ** -0.5),
        'hy_f_b1': nrm((N_ODD, HY_FFN), 0.1),
        'hy_f_freq1': 1.0 + nrm((N_ODD, HY_FFN), 0.1),
        'hy_f_w2': nrm((N_ODD, HY_FFN, HY_FFN), HY_FFN ** -0.5),
        'hy_f_b2': nrm((N_ODD, HY_FFN), 0.1),
        'hy_f_freq2': 1.0 + nrm((N_ODD, HY_FFN), 0.1),
        'hy_f_w3': nrm((N_ODD, HY_FFN, HY_ORDER * 2 * D_MODEL), 0.01),
        'hy_f_bias': nrm((N_ODD, HY_ORDER, D_MODEL), 0.5),
        'hy_w_out': nrm((N_ODD, D_MODEL, D_MODEL), D_MODEL ** -0.5),
        'moe_w_group': nrm((DEPTH, D_MODEL, N_GROUPS), D_MODEL ** -0.5),
        'moe_b_group': nrm((DEPTH, N_GROUPS), 0.01),
        'moe_w_router': nrm((DEPTH, D_MODEL, N_EXPERTS), D_MODEL ** -0.5),
        'moe_b_router': nrm((DEPTH, N_EXPERTS), 0.01),
        'moe_w_gate': nrm((DEPTH, N_EXPERTS, D_MODEL, D_EXPERT), D_MODEL ** -0.5),
        'moe_w_up': nrm((DEPTH, N_EXPERTS, D_MODEL, D_EXPERT), D_MODEL ** -0.5),
        'moe_w_down': nrm((DEPTH, N_EXPERTS, D_EXPERT, D_MODEL), D_EXPERT ** -0.5),
    }

def reference(x_prompt, x_sample, state_gla, state_mlstm_c, state_mlstm_n, state_mlstm_m, c, c_ctx,
              norm1_w, norm2_w, norm_f_w, ada_w, ada_b, rec_w_in, gla_gk_w, gla_gk_b, mlstm_gate_b,
              gla_norm_w, mlstm_norm_w, rec_w_out, hy_w_in, hy_conv_w, hy_f_w1, hy_f_b1, hy_f_freq1,
              hy_f_w2, hy_f_b2, hy_f_freq2, hy_f_w3, hy_f_bias, hy_w_out, moe_w_group, moe_b_group,
              moe_w_router, moe_b_router, moe_w_gate, moe_w_up, moe_w_down):
    p = dict(norm1_w=norm1_w, norm2_w=norm2_w, norm_f_w=norm_f_w, ada_w=ada_w, ada_b=ada_b,
             rec_w_in=rec_w_in, gla_gk_w=gla_gk_w, gla_gk_b=gla_gk_b, mlstm_gate_b=mlstm_gate_b,
             gla_norm_w=gla_norm_w, mlstm_norm_w=mlstm_norm_w, rec_w_out=rec_w_out,
             hy_w_in=hy_w_in, hy_conv_w=hy_conv_w, hy_f_w1=hy_f_w1, hy_f_b1=hy_f_b1, hy_f_freq1=hy_f_freq1,
             hy_f_w2=hy_f_w2, hy_f_b2=hy_f_b2, hy_f_freq2=hy_f_freq2, hy_f_w3=hy_f_w3, hy_f_bias=hy_f_bias,
             hy_w_out=hy_w_out, moe_w_group=moe_w_group, moe_b_group=moe_b_group,
             moe_w_router=moe_w_router, moe_b_router=moe_b_router, moe_w_gate=moe_w_gate,
             moe_w_up=moe_w_up, moe_w_down=moe_w_down)
    f32 = jnp.float32
    bp = x_prompt.shape[0]
    zero_states = [(jnp.zeros((bp, 2, H_A, DK_A, DV_A), f32), jnp.zeros((bp, 2, H_B, DK_B, DV_B), f32),
                    jnp.zeros((bp, 2, H_B, DK_B), f32), jnp.zeros((bp, 2, H_B), f32)) for _ in range(N_EVEN)]
    y_prompt, ctx_states = _trunk(x_prompt, c_ctx[None, :], zero_states, p)
    cached = [(state_gla[:, j], state_mlstm_c[:, j], state_mlstm_n[:, j], state_mlstm_m[:, j]) for j in range(N_EVEN)]
    x_lat = x_sample + _grid_pos_embed(x_sample.shape[1]).astype(x_sample.dtype)
    y_sample, _ = _trunk(x_lat, c, cached, p)
    new_state_gla = jnp.stack([s[0] for s in ctx_states], axis=1)
    new_state_mlstm_c = jnp.stack([s[1] for s in ctx_states], axis=1)
    new_state_mlstm_n = jnp.stack([s[2] for s in ctx_states], axis=1)
    new_state_mlstm_m = jnp.stack([s[3] for s in ctx_states], axis=1)
    return (y_prompt, y_sample, new_state_gla, new_state_mlstm_c, new_state_mlstm_n, new_state_mlstm_m)


_drawn_inputs = setup_inputs


def setup_inputs(seed=0):
    import zlib

    import numpy as np

    out = dict(_drawn_inputs(seed))
    spreads = {}
    factors = {'state_gla': 3.197,
     'state_mlstm_n': 4.787,
     'state_mlstm_m': 2.669,
     'norm_f_w': 8.077,
     'gla_norm_w': 3.657,
     'mlstm_norm_w': 11.53,
     'moe_b_group': 5.476,
     'moe_b_router': 6.674,
     'norm2_w': 2.712}
    for name, (base, spread) in spreads.items():
        noise = np.random.default_rng([zlib.crc32(name.encode()), seed]).standard_normal(out[name].shape)
        drawn = base * np.exp(spread * noise) if base else spread * noise
        out[name] = __import__('jax').numpy.asarray(drawn.astype(out[name].dtype))
    for name, factor in factors.items():
        out[name] = (out[name] * factor).astype(out[name].dtype)
    return out
```

```python
import math
from contextlib import ExitStack

import numpy as np

import concourse.bass as bass
from concourse import mybir

F32 = mybir.dt.float32
U32 = mybir.dt.uint32
I32 = mybir.dt.int32
ALU = mybir.AluOpType
ACT = mybir.ActivationFunctionType
AX = mybir.AxisListType

P = 128
D = 1024
DC = D // P
LP, LS = 128, 256
T = LP + LS
NT = T // P
SEQS = [(0, LP), (LP, T)]
H = 4
DK, DV = 64, 128
RANK = 16
NMOD = 6
NG, EPG = 4, 4
NE = NG * EPG
DE = D // 2
EPS = 1e-6
RING = 6
SLOT = 4096
NEG = -1.0e30
BIG = 1.0e4

V_CTX, V_C, V_N1, V_N2, V_NF, V_GKB, V_ADA, V_CONV = 0, 8, 16, 32, 48, 56, 60, 156
V_ALL = V_CONV + 72


def tables():
    i = np.arange(P)
    common = np.concatenate([
        np.eye(P), (i[:, None] < i[None, :]), np.tile(i, (P, 1)),
        i[:, None] + P * np.arange(NT)[None, :], np.tile([4, 3, 2, 1], (P, 1)),
        np.tile(P * np.arange(NE), (P, 1)), (i[:, None] > 0)], axis=1).astype(np.float32)
    le, ge = i[:, None] <= i[None, :], i[:, None] >= i[None, :]
    zero = np.zeros((P, P))
    nf, nb = np.where(le, 0.0, NEG), np.where(ge, 0.0, NEG)
    rec = np.concatenate([nf, nf, zero, nf, nb, nb, zero, nb, le, ge], axis=1).astype(np.float32)

    def dft(L):
        t, f = np.arange(L)[:, None], np.arange(L)[None, :]
        w = math.pi * ((t * f) % (2 * L)) / L
        c, s = np.cos(w), -np.sin(w)
        alt = (-1.0) ** np.arange(L)
        s_nyq, c_nyq = s.copy(), c.copy()
        s_nyq[:, 0] = alt
        c_nyq[:, 0] = alt
        gr, gi = 2 * c.T / (2 * L), 2 * s.T / (2 * L)
        gr[0] = 1.0 / (2 * L)
        gi[0] = alt / (2 * L)
        return c, s_nyq, s, c_nyq, gr, gi

    def rows(m):
        return m.reshape(-1, P, m.shape[1]).transpose(1, 0, 2).reshape(P, -1)

    cp, snp, sp_, c3p, grp, gip = dft(LP)
    cs, sns, ss, c3s, grs, gis = dft(LS)
    hy = np.concatenate([cp, snp, sp_, c3p, grp, gip, rows(cs), rows(sns), rows(ss[:, :P]),
                         rows(c3s[:, :P]), rows(grs), rows(gis)], axis=1).astype(np.float32)

    def linspace(a, b, n):
        return np.linspace(np.float32(a), np.float32(b), n, dtype=np.float32)

    emb, dec = [], []
    lo, hi = abs(math.log(1e-2)) / 1.5, abs(math.log(1e-2)) / 0.3
    for L in (LP, LS):
        t = linspace(0.0, 1.0, L)[:, None]
        w = (2.0 * math.pi * np.arange(L)[:, None] / L)
        f = linspace(1e-4, 15, 16)[None, :].astype(np.float64)
        emb.append(np.concatenate([t, np.cos(f * w), -np.sin(f * w)], axis=1))
        dec.append(np.exp(-t * linspace(lo, hi, D)[None, :]))
    emb = np.concatenate(emb).T.astype(np.float32)
    dec = np.concatenate(dec).astype(np.float32)
    r, cl = np.meshgrid(np.arange(LS // 64), np.arange(64), indexing="ij")
    omega = 10000.0 ** (-np.arange(D // 4) / (D // 4))
    pos = []
    for q in (r, cl):
        a = q.reshape(-1, 1) * omega[None, :]
        pos += [np.sin(a), np.cos(a)]
    pos = np.concatenate(pos, axis=1).astype(np.float32)
    return dict(t_common=common, t_rec=rec, t_hy=hy, t_emb=np.ascontiguousarray(emb), t_decay=dec, t_pos=pos)


def build(nc, A, O):
    ctx = ExitStack()
    with ctx:
        def sb(name, shape, dt=F32):
            return ctx.enter_context(nc.sbuf_tensor(name, shape, dt))

        semaphores = {}

        def S(name):
            if name not in semaphores:
                semaphores[name] = ctx.enter_context(nc.semaphore(name))
            return semaphores[name]

        ring = sb("ring", [P, RING, SLOT])
        xT = sb("xT", [P, DC, T])
        uT = sb("uT", [P, DC, T])
        tc_ = sb("tab_common", [P, 3 * P + NT + 4 + NE + 1])
        ident, strict, iota = tc_[:, 0:P], tc_[:, P:2 * P], tc_[:, 2 * P:3 * P]
        o = 3 * P
        tokid, w4, ebase = tc_[:, o:o + NT], tc_[:, o + NT:o + NT + 4], tc_[:, o + NT + 4:o + NT + 4 + NE]
        notfirst = tc_[:, o + NT + 4 + NE:o + NT + 5 + NE]
        ones = sb("ones", [P, P])
        eps = sb("eps", [P, 1])
        vecT = sb("vecT", [P, V_ALL])
        silc = sb("silc", [P, DC, 2])
        ada = sb("ada", [P, 2, NMOD * DC, 2])
        mA = sb("mA", [P, DC, 2])
        mB = sb("mB", [P, DC, 2])
        rstd = sb("rstd", [P, T])
        b20 = sb("b20", [P, 2, NG + NE])
        wr = sb("wr", [P, DC, 2, NG + NE])
        WORK = 19700
        work = sb("work", [P, WORK])
        ps = [ctx.enter_context(nc.psum_tensor(f"ps{b}", [P, 512], F32)) for b in range(8)]

        u_dram = nc.dram_tensor("u_rows", [T, D], F32).ap()
        y_dram = nc.dram_tensor("y_rows", [NT * NE * P, D], F32).ap()

        class Arena:

            def __init__(self):
                self.at, self.high = 0, 0

            def get(self, n, high=False, parts=P):
                if high:
                    a, self.high = self.high, self.high + n
                    assert self.high <= 2 * SLOT, self.high
                    return ring[0:parts, 4:6, :].rearrange("p a b -> p (a b)")[:, a:a + n]
                a, self.at = self.at, self.at + n
                assert self.at <= WORK, self.at
                return work[0:parts, a:a + n]

        bank_uses = [0] * 8
        jobs = {}
        turn = [0]

        def claim(key, bank=None, keep=None):
            if bank is None:
                if turn[0] % 8 == keep:
                    turn[0] += 1
                bank = turn[0] % 8
                turn[0] += 1
            bank_uses[bank] += 1
            jobs[key] = (bank, bank_uses[bank], 0)
            return bank

        def claim_loop(n, body):
            per = [sum(b == bank for _, b in body) for bank in range(8)]
            seen = [0] * 8
            for key, bank in body:
                seen[bank] += 1
                jobs[key] = (bank, bank_uses[bank] + seen[bank], per[bank])
            for bank in range(8):
                bank_uses[bank] += n * per[bank]

        bank_full = [S(f"bank{b}_full") for b in range(8)]
        bank_free = [S(f"bank{b}_free") for b in range(8)]

        def bank(key):
            return ps[jobs[key][0]]

        def opened(eng, key, it=0):
            b, use, per = jobs[key]
            if isinstance(it, int) and use - 1 + it * per == 0:
                return
            eng.wait_ge(bank_free[b], it * per + (use - 1))

        def full(eng, key, it=0):
            b, use, per = jobs[key]
            eng.wait_ge(bank_full[b], it * per + use)

        def done(ins, key):
            ins.then_inc(bank_full[jobs[key][0]], 1)

        def free(ins, key):
            ins.then_inc(bank_free[jobs[key][0]], 1)

        claim("vec", 7)
        for j in range(NT):
            for hf in range(2):
                claim(("x", j, hf))
        MODS = ["rec", "moe0", "hy", "moe1", "fin"]

        claim(("ada", 0))
        claim(("ss", "rec"))
        for m in range(4):
            claim(("qka", m))
        claim("gk")
        claim("mg")
        for m in range(4):
            claim(("qkb", m))
        for n in ("va", "vb", "ra", "ob"):
            for j in range(NT):
                claim((n, j))
        for m in range(4):
            claim(("glog", m))
        for k in range(4):
            claim(("keT", k))
        for d in range(2):
            for j in range(NT):
                claim(("A", d, j))
        for d in range(2):
            claim(("kv", d, 0))
        for d in range(2):
            claim(("kv", d, 1))
        for j in range(NT):
            claim(("oa", j))
        claim("mtok")
        claim("qk0", 7)
        claim("kbt", keep=7)
        for h in range(H):
            claim(("qk", h), keep=7)
            for d in range(2):
                claim(("nM", d, h), keep=7)
        for d in range(2):
            claim(("C", d))
        for j in range(NT):
            for d in range(2):
                for hp in range(2):
                    claim(("num", j, d, hp))
        for j in range(NT):
            for hf in range(2):
                claim(("mixT", j, hf))
        for m in range(DC):
            claim(("ro", m))

        BODY = [("X", 0), ("X", 1), ("G",), ("U",), ("HT",), ("Y", 0), ("Y", 1)]

        def claim_moe(l):
            claim(("ss", f"moe{l}"))
            claim(("route", l))
            claim(("pos", l))
            claim(("cnt", l))
            for j in range(NT):
                for hf in range(2):
                    claim(("ut", l, j, hf))
            claim(("idx", l))
            body = []
            for u in range(2):
                for k, name in enumerate(BODY):
                    body.append(((l, u) + name, k))
            claim_loop(NE // 2, body)
            if l == 0:
                claim(("ada", 1))
            for j in range(NT):
                for hf in range(2):
                    claim(("yT", l, j, hf))

        claim_moe(0)
        claim(("ss", "hy"))
        claim("f1")
        claim("f2")
        for m in range(3 * DC):
            claim(("z", m))
            if 1 <= m <= 2 * DC:
                claim(("zt", m - 1))
        for c in range(2):
            for od in range(2):
                for j in range(NT):
                    for d in range(2):
                        claim(("filt", c, od, j, d))
                for q in range(8):
                    claim(("K", c, od, q))
                for q in range(6):
                    claim(("F", c, od, q))
                for q in range(NT if od == 0 else 4):
                    claim(("inv", c, od, q))
        for m in range(DC):
            claim(("ho", m))
        claim_moe(1)
        claim(("ss", "fin"))
        for j in range(NT):
            for hf in range(2):
                claim(("out", j, hf))

        loads = {}
        slot_uses = [0] * RING
        order = []

        def cols(w, j):
            return w.rearrange("(k p) n -> p k n", p=P)[:, :, j * 512:(j + 1) * 512]

        def add_load(key, slot, src, last, wait=None):
            slot_uses[slot] += 1
            loads[key] = (slot, slot_uses[slot], 0)
            order.append(("load", slot, src, last, wait))

        for j in range(12):
            add_load(("ada", 0, j), j % 6, cols(A["ada_w"][0], j), ("ada", 0, j) if j < 11 else ("ada", 0))
        REC_ORDER = [(0, ("qka", 3)), (3, ("qkb", 3)), (1, ("va", 2)), (4, ("vb", 2)), (2, ("ra", 2)), (5, ("ob", 2))]
        for n, (j, last) in enumerate(REC_ORDER):
            add_load(("rec", j), n % 4, cols(A["rec_w_in"][0], j), last)
        for j in range(2):
            add_load(("ro", j), (2 + j) % 4, cols(A["rec_w_out"][0], j), ("ro", 4 * j + 3))

        def add_moe(l):
            order.append(("moe", l, [slot_uses[s] for s in range(RING)]))
            for s in range(RING):
                slot_uses[s] += NE // 2

        moe_base = {}
        moe_base[0] = list(slot_uses)
        add_moe(0)
        for j in range(12):
            add_load(("ada", 1, j), j % 6, cols(A["ada_w"][1], j), ("ada", 1, j) if j < 11 else ("ada", 1))
        add_load("w3", 0, A["hy_f_w3"][0], ("filt", 1, 1, NT - 1, 1))
        for j in range(6):
            add_load(("hin", j), 1 + j % 3, cols(A["hy_w_in"][0], j), ("z", 4 * j + 3))
        for j in range(2):
            add_load(("ho", j), 1 + j, cols(A["hy_w_out"][0], j), ("ho", 4 * j + 3))
        moe_base[1] = list(slot_uses)
        add_moe(1)

        ada_no = {("ada", l, j): 11 * l + j for l in range(2) for j in range(11)}

        def released(eng, last, it=0):
            if last in ada_no:
                eng.wait_ge(S("ada_slot_read"), ada_no[last] + 1)
            else:
                full(eng, last, it)

        def loaded(eng, key):
            slot, use, _ = loads[key]
            eng.wait_ge(S(f"slot{slot}_loaded"), 16 * use)
            return ring[:, slot, :]

        def moe_src(l, kind, e):
            if kind < 2:
                w = (A["moe_w_gate"], A["moe_w_up"])[kind]
                return w[l, e].rearrange("(k p) n -> p k n", p=P)
            return A["moe_w_down"][l, e].rearrange("(k p) n -> p k n", p=P)

        a = Arena()
        x_in = a.get(NT * D).rearrange("p (j d) -> p j d", j=NT)
        pos_in = a.get(2 * D).rearrange("p (j d) -> p j d", j=2)
        vrows = a.get(3 * P).rearrange("p (a b) -> p a b", a=3)
        c_exp = a.get(2 * DC)
        a = Arena()
        sq = a.get(DC * T).rearrange("p (k t) -> p k t", k=DC)
        a.at = 0
        B_ = a.get(4 * T).rearrange("p (m t) -> p m t", m=4)
        gt = a.get(4 * T).rearrange("p (m t) -> p m t", m=4)
        mix_tok = a.get(NT * D).rearrange("p (j d) -> p j d", j=NT)
        qka = a.get(4 * T).rearrange("p (m t) -> p m t", m=4)
        qkb = a.get(4 * T).rearrange("p (m t) -> p m t", m=4)
        va = a.get(NT * H * DV).rearrange("p (j n) -> p j n", j=NT)
        vb = a.get(NT * H * (DV + 1)).rearrange("p (j h n) -> p j h n", j=NT, h=H)
        gkT = a.get(T, parts=32)
        trec = a.get(10 * P)
        mneg = [trec[:, 0:512], trec[:, 512:1024]]
        amask = [trec[:, 1024:1152].bitcast(U32), trec[:, 1152:1280].bitcast(U32)]
        wg = trec.rearrange("p (k n) -> p k n", k=DC)
        gkw = a.get(512, parts=32)
        gnw = a.get(2 * DV)
        S0 = a.get(2 * 2 * DV).rearrange("p (d k v) -> p d k v", d=2, k=2)
        C0 = a.get(2 * 2 * (DV + 1)).rearrange("p (d k v) -> p d k v", d=2, k=2)
        refs = a.get(4 * NT).rearrange("p (m j) -> p m j", m=4)
        fcol = a.get(4 * 3).rearrange("p (m c) -> p m c", m=4)
        fexp = a.get(4 * 3).rearrange("p (m c) -> p m c", m=4)
        m0b = a.get(8)
        mcol = a.get(4)
        atok = a.get(NT * 36).rearrange("p (j c) -> p j c", j=NT)
        emt = a.get(NT * 36).rearrange("p (j c) -> p j c", j=NT)
        dn = a.get(8)
        rms = a.get(3 * NT * 8).rearrange("p (a j c) -> p a j c", a=3, j=NT)
        g36 = a.get(7 * T, parts=36).rearrange("p (a t) -> p a t", a=7)
        Dq = gt
        eq = a.get(4 * T, high=True).rearrange("p (m t) -> p m t", m=4)
        ek = a.get(4 * T, high=True).rearrange("p (m t) -> p m t", m=4)
        A_sb = a.get(2 * NT * 512, high=True).rearrange("p (d j n) -> p d j n", d=2, j=NT)
        ke_s = a.get(4 * 2 * P, high=True).rearrange("p (q n) -> p q n", q=8)
        S1 = a.get(2 * 2 * DV, high=True).rearrange("p (d k v) -> p d k v", d=2, k=2)
        S3 = a.get(2 * 2 * DV, high=True).rearrange("p (d k v) -> p d k v", d=2, k=2)
        hm_ = Arena()
        Wm = hm_.get(8 * 512, high=True).rearrange("p (c n) -> p c n", c=8)
        Cout = hm_.get(2 * 2 * (DV + 1), high=True).rearrange("p (d n) -> p d n", d=2)
        qin = hm_.get(2 * 2 * LS, high=True).rearrange("p (d k t) -> p d k t", d=2, k=2)
        kbt = hm_.get(2 * P, high=True).rearrange("p (a n) -> p a n", a=2)
        kw = hm_.get(8 * DK, high=True).rearrange("p (c n) -> p c n", c=8)
        hs = gt.rearrange("p m t -> p (m t)").rearrange("p (j n) -> p j n", j=NT)
        osq = B_.rearrange("p m t -> p (m t)").rearrange("p (j n) -> p j n", j=NT)
        a = Arena()
        msq = a.get(DC * T).rearrange("p (k t) -> p k t", k=DC)
        a.at = 0
        pall = a.get(NT * NE * P).rearrange("p (j e s) -> p j e s", j=NT, e=NE)
        utok = a.get(NT * D).rearrange("p (j d) -> p j d", j=NT)
        lg = a.get(NT * 20).rearrange("p (j c) -> p j c", j=NT)
        R4 = [a.get(NT * 4).rearrange("p (j c) -> p j c", j=NT) for _ in range(12)]
        R1 = [a.get(NT) for _ in range(10)]
        R5 = [a.get(NT * 5).rearrange("p (j c) -> p j c", j=NT) for _ in range(2)]
        R16 = [a.get(NT * 16).rearrange("p (j c) -> p j c", j=NT) for _ in range(8)]
        gid = a.get(NT * NE * 2).rearrange("p (j e c) -> p j e c", j=NT, e=NE)
        idxf = a.get(NE * 2).rearrange("p (e c) -> p e c", e=NE)
        idxu = a.get(NE).bitcast(U32)
        gslot = a.get(NE)
        ridx = a.get(NT * 2).bitcast(U32).rearrange("p (j c) -> p j c", j=NT)
        flag = a.get(1).bitcast(I32)
        cmax = a.get(2)
        oidx = a.get(NE).bitcast(U32)
        ogate = a.get(NE)
        gcol = a.get(2)
        b = Arena()
        ug = b.get(2 * D).rearrange("p (u d) -> p u d", u=2)
        xg = b.get(2 * D).rearrange("p (u k s) -> p u k s", u=2, k=DC)
        sg = b.get(2 * DE).rearrange("p (u n) -> p u n", u=2)
        assert b.at <= NT * NE * P
        b = Arena()
        b.at = 2 * D + 2 * D + 2 * DE
        hh = b.get(DE)
        hT = b.get(DE)
        ysb = utok.rearrange("p j d -> p (j d)")[:, 0:2 * D].rearrange("p (u d) -> p u d", u=2)
        assert b.at <= NT * NE * P
        x_out = utok
        cmb = work[:, 0:2 * NT * D].rearrange("p (c j d) -> p c j d", c=2, j=NT)
        a = Arena()
        hsq = a.get(DC * T).rearrange("p (k t) -> p k t", k=DC)
        a.at = 0
        v_tok = a.get(NT * D).rearrange("p (j d) -> p j d", j=NT)
        x1_tok = a.get(NT * D).rearrange("p (j d) -> p j d", j=NT)
        x2T = a.get(DC * T).rearrange("p (k t) -> p k t", k=DC)
        thy = a.get(3328)
        Yf = a.get(6 * 512).rearrange("p (q n) -> p q n", q=6)
        dcy = a.get(NT * 512).rearrange("p (j n) -> p j n", j=NT)
        embT = a.get(T, parts=33)
        h1T = a.get(T, parts=64)
        h2T = a.get(T, parts=65)
        fprm = a.get(4, parts=64)
        hw1 = a.get(64, parts=33)
        hw2 = a.get(64, parts=64)
        zall = a.get(2 * T)
        zc = zall.rearrange("p (u t) -> p u t", u=2)
        srt = zall[0:64, :].rearrange("p (u t) -> p u t", u=2)
        htmp = zall[:, 0:512]
        Kf = a.get(8 * 512, high=True).rearrange("p (q n) -> p q n", q=8)
        hpm = a.get(6 * 512, high=True).rearrange("p (j s n) -> p j s n", j=NT, s=2)
        ptmp = hpm.rearrange("p j s n -> p (j s) n")

        def col(i):
            return vecT[:, i:i + 1]

        def mod(l, part, m, v):
            return ada[:, l, part * DC + m, v:v + 1]

        def bc(ap, shape):
            return ap.to_broadcast(shape)

        def x_ready(eng, name):
            if name == "rec":
                for j in range(NT):
                    for hf in range(2):
                        evacuated(eng, ("x", j, hf))
            elif name in ("moe0", "moe1"):
                for m in range(DC):
                    evacuated(eng, ("ro" if name == "moe0" else "ho", m))
            else:
                for j in range(NT):
                    for hf in range(2):
                        evacuated(eng, ("yT", 0 if name == "hy" else 1, j, hf))

        def evacuated(eng, key, it=0):
            b, use, per = jobs[key]
            eng.wait_ge(bank_free[b], it * per + use)

        REC_SMALL = 2 + 6 + 3 + 12
        OVF = NT - 1
        squares = {"rec": sq, "moe0": msq, "hy": hsq, "moe1": msq, "fin": msq}
        MODV = {"rec": (0, 0), "moe0": (0, 3), "hy": (1, 0), "moe1": (1, 3)}
        NVEC = {"rec": V_N1, "moe0": V_N2, "hy": V_N1 + DC, "moe1": V_N2 + DC, "fin": V_NF}
        block = ctx.enter_context(nc.Block())

        @block.sync
        def _(sp):
            slot_last = [None] * RING

            def load(item):
                _, slot, src, last, _ = item
                if slot_last[slot] is not None:
                    released(sp, slot_last[slot])
                if src.shape[0] == P:
                    dst = ring[:, slot, :].rearrange("p (k n) -> p k n", k=src.shape[1])
                else:
                    dst = ring[0:src.shape[0], slot, :]
                sp.dma_start(dst, src).then_inc(S(f"slot{slot}_loaded"), 16)
                slot_last[slot] = last

            def moe_loads(l, base):
                def pair(it, first):
                    for u in range(2):
                        for kind, name in ((0, ("G",)), (1, ("U",)), (2, ("Y", 1))):
                            slot = 3 * u + kind
                            if first:
                                if slot_last[slot] is not None:
                                    released(sp, slot_last[slot])
                            else:
                                full(sp, (l, u) + name, it - 1)
                            k = 8 if kind < 2 else 4
                            sp.dma_start(ring[:, slot, :].rearrange("p (k n) -> p k n", k=k),
                                         moe_src(l, kind, 2 * it + u)).then_inc(S(f"slot{slot}_loaded"), 16)
                        if not first:
                            store(it - 1, u)

                def store(it, u):
                    evacuated(sp, (l, u, "Y", 0), it)
                    evacuated(sp, (l, u, "Y", 1), it)
                    sp.dma_start(y_dram.rearrange("(e s) d -> e s d", s=P)[2 * it + u],
                                 ysb[:, u, :]).then_inc(S(f"y{u}_stored"), 16)

                if l == 0:
                    sp.wait_ge(S("states_stored"), 16 * 14)
                for m in range(DC):
                    full(sp, ("ro" if l == 0 else "ho", m))
                pair(0, True)
                with sp.Fori(1, NE // 2) as it:
                    pair(it, False)
                store(NE // 2 - 1, 0)
                store(NE // 2 - 1, 1)
                for u in range(2):
                    slot_last[3 * u], slot_last[3 * u + 1], slot_last[3 * u + 2] = None, None, None
                full(sp, (l, 1, "Y", 1), NE // 2 - 1)
                overflow_sp(l)

            def overflow_sp(l):
                sp.wait_ge(S("overflow_flag"), l + 1)
                over = sp.value_load(flag[0:1, 0:1], min_val=0, max_val=T)
                with sp.If(over > P):
                    sp.nop().then_inc(S(f"over{l}_y_stored"), 16)
                    for c in range(1, NT):
                        with sp.Fori(0, NE) as e:
                            n = e + NE * (c - 1)
                            sp.wait_ge(S(f"over{l}_y_stored"), 16 * n + 16)
                            for kind in range(3):
                                k = 8 if kind < 2 else 4
                                sp.dma_start(ring[:, kind, :].rearrange("p (k n) -> p k n", k=k),
                                             moe_src(l, kind, e)).then_inc(S(f"over{l}_loaded{kind}"), 16)
                            sp.wait_ge(S(f"over{l}_y"), n + 1)
                            sp.dma_start(y_dram.rearrange("(e s) d -> e s d", s=P)[e + c * NE],
                                         ysb[:, 0, :]).then_inc(S(f"over{l}_y_stored"), 16)
                    sp.wait_ge(S(f"over{l}_y_stored"), 16 * NE * OVF + 16)
                with sp.Else():
                    sp.nop()
                sp.nop()

            for item in order:
                if item[0] == "load":
                    load(item)
                else:
                    moe_loads(item[1], item[2])
            for j in range(NT):
                for hf in range(2):
                    evacuated(sp, ("out", j, hf))
                dst = O[0][0] if j == 0 else O[1][0, (j - 1) * P:j * P, :]
                sp.dma_start(dst, x_out[:, j, :]).then_inc(S("y_out_stored"), 16)
            sp.wait_ge(S("y_out_stored"), 16 * NT)

        @block.gpsimd
        def _(pool):
            def clear(ap, name):
                pool.memset(ap, 0.0).then_inc(S(name), 1)

            for dst, src in (
                (vrows[0:8, 0, :], A["c_ctx"].rearrange("(a b) -> a b", b=P)),
                (vrows[8:16, 0, :], A["c"].rearrange("o (a b) -> (o a) b", b=P)),
                (vrows[16:32, 0, :], A["norm1_w"].rearrange("l (a b) -> (l a) b", b=P)),
                (vrows[32:48, 0, :], A["norm2_w"].rearrange("l (a b) -> (l a) b", b=P)),
                (vrows[48:56, 0, :], A["norm_f_w"].rearrange("(a b) -> a b", b=P)),
                (vrows[56:60, 0, :], A["gla_gk_b"].rearrange("o d (a b) -> (o d a) b", b=P)),
                (vrows[0:96, 1, :], A["ada_b"].rearrange("l (a b) -> (l a) b", b=P)),
                (vrows[0:72, 2, :], A["hy_conv_w"].rearrange("o t (a b) -> (o t a) b", b=P)),
            ):
                pool.dma_start(dst, src).then_inc(S("vec_rows_loaded"), 16)
            for l in range(2):
                pool.dma_start(wr[:, :, l, 0:NG], A["moe_w_group"][l].rearrange("(k p) n -> p k n", p=P)).then_inc(S("router_loaded"), 16)
                pool.dma_start(wr[:, :, l, NG:], A["moe_w_router"][l].rearrange("(k p) n -> p k n", p=P)).then_inc(S("router_loaded"), 16)
                pool.dma_start(b20[:, l, 0:NG], A["moe_b_group"][l].partition_broadcast(P)).then_inc(S("router_loaded"), 16)
                pool.dma_start(b20[:, l, NG:], A["moe_b_router"][l].partition_broadcast(P)).then_inc(S("router_loaded"), 16)

            for m in range(DC):
                evacuated(pool, ("x", m % NT, m % 2))
            evacuated(pool, "vec")
            clear(wg, "wg_cleared")
            clear(gkw, "gkw_cleared")
            clear(g36, "g36_cleared")
            clear(mcol, "mcol_cleared")
            pool.memset(vb[:, :, :, DV:DV + 1], 1.0).then_inc(S("vb_ones"), 1)
            pool.wait_ge(S("wg_cleared"), 1)
            w_in = A["rec_w_in"][0].rearrange("(k p) n -> p k n", p=P)
            base = w_in.shape[2] - 16
            pool.dma_start(wg[:, :, 0:32], w_in[:, :, base - 32:base]).then_inc(S("wg_loaded"), 16)
            for q in range(4):
                typ, d = q // 2, q % 2
                pool.dma_start(wg[:, :, 32 + 32 * q:36 + 32 * q],
                               w_in[:, :, base + 8 * d + 4 * typ:base + 8 * d + 4 * typ + 4]).then_inc(S("wg_loaded"), 16)
            pool.wait_ge(S("gkw_cleared"), 1)
            for d in range(2):
                pool.dma_start(gkw[16 * d:16 * d + 16, 256 * d:256 * d + 256], A["gla_gk_w"][0, d]).then_inc(S("rec_small_loaded"), 16)
            pool.wait_ge(S("mcol_cleared"), 1)
            for d in range(2):
                for typ in range(2):
                    pool.dma_start(mcol[32 * d:32 * d + 4, typ:typ + 1],
                                   A["mlstm_gate_b"][0, d, typ].rearrange("(h o) -> h o", o=1)).then_inc(S("rec_small_loaded"), 16)
                pool.dma_start(mcol[32 * d:32 * d + 4, 2:3],
                               A["state_mlstm_m"][0, 0, d].rearrange("(h o) -> h o", o=1)).then_inc(S("rec_small_loaded"), 16)
            pool.dma_start(m0b, A["state_mlstm_m"][0, 0].rearrange("d h -> (d h)").partition_broadcast(P)).then_inc(S("rec_small_loaded"), 16)
            pool.dma_start(gnw[:, 0:DV], A["gla_norm_w"][0].partition_broadcast(P)).then_inc(S("rec_small_loaded"), 16)
            pool.dma_start(gnw[:, DV:], A["mlstm_norm_w"][0].partition_broadcast(P)).then_inc(S("rec_small_loaded"), 16)
            for d in range(2):
                for kc in range(2):
                    pool.dma_start(S0[:, d, kc, :], A["state_gla"][0, 0, d, 2 * kc:2 * kc + 2].rearrange("h k v -> (h k) v")).then_inc(S("rec_small_loaded"), 16)
                    pool.dma_start(C0[:, d, kc, 0:DV], A["state_mlstm_c"][0, 0, d, 2 * kc:2 * kc + 2].rearrange("h k v -> (h k) v")).then_inc(S("rec_small_loaded"), 16)
                    pool.dma_start(C0[:, d, kc, DV:], A["state_mlstm_n"][0, 0, d, 2 * kc:2 * kc + 2].rearrange("h (k o) -> (h k) o", o=1)).then_inc(S("rec_small_loaded"), 16)
            full(pool, ("ada", 0))
            clear(A_sb, "A_cleared")
            full(pool, "mg")
            pool.dma_start(trec, A["t_rec"]).then_inc(S("rec_tables_loaded"), 16)

            pool.wait_ge(S("gla_exp"), 2)
            evacuated(pool, ("qka", 3))
            for d in range(2):
                pool.tensor_tensor(ek[:, 2 * d:2 * d + 2, :], ek[:, 2 * d:2 * d + 2, :], qka[:, 2:4, :],
                                   ALU.mult).then_inc(S("ke"), 1)
            for d in range(2):
                evacuated(pool, ("kv", d, 0))
                for kc in range(2):
                    pool.dma_start(O[2][0, 0, d, 2 * kc:2 * kc + 2].rearrange("h k v -> (h k) v"), S1[:, d, kc, :]).then_inc(S("states_stored"), 16)
            pool.wait_ge(S("qin_exp"), 8)
            evacuated(pool, ("qkb", 1))
            for d in range(2):
                pool.tensor_tensor(qin[:, d, :, :], qin[:, d, :, :], qkb[:, 0:2, P:T], ALU.mult).then_inc(S("qin"), 1)
            for d in range(2):
                evacuated(pool, ("C", d))
                for kc in range(2):
                    pool.dma_start(O[3][0, 0, d, 2 * kc:2 * kc + 2].rearrange("h k v -> (h k) v"), Cout[:, d, kc * 129:kc * 129 + DV]).then_inc(S("states_stored"), 16)
                    pool.dma_start(O[4][0, 0, d, 2 * kc:2 * kc + 2].rearrange("h (k o) -> (h k) o", o=1), Cout[:, d, kc * 129 + DV:kc * 129 + DV + 1]).then_inc(S("states_stored"), 16)
                at = (LP - 1, 0)[d]
                pool.wait_ge(S("m_rows"), 1)
                pool.dma_start(O[5][0, 0, d].rearrange("(h o) -> h o", o=1), g36[32 * d:32 * d + 4, 2, at:at + 1]).then_inc(S("states_stored"), 16)
            pool.wait_ge(S("states_stored"), 16 * 14)

            def moe(l):
                for j in range(NT):
                    for hf in range(2):
                        evacuated(pool, ("ut", l, j, hf))
                    pool.dma_start(u_dram[j * P:(j + 1) * P, :], utok[:, j, :]).then_inc(S("u_rows_stored"), 16)
                pool.wait_ge(S("u_rows_stored"), 16 * NT * (l + 1))
                evacuated(pool, ("idx", l))
                for e in range(NE):
                    it, u = e // 2, e % 2
                    if e >= 2:
                        full(pool, (l, u, "X", 1), it - 1)
                    pool.indirect_dma_start(ug[:, u, :], None, u_dram,
                                            bass.IndirectOffsetOnAxis(ap=idxu[:, e:e + 1], axis=0)).then_inc(S(f"rows{u}_gathered"), 16)
                def token_rows(written):
                    for u in range(2):
                        pool.wait_ge(S(f"y{u}_stored"), 16 * (NE // 2) * (l + 1))
                    full(pool, (l, 1, "Y", 1), NE // 2 - 1)
                    for j in range(NT):
                        for q in range(2):
                            pool.indirect_dma_start(cmb[:, q, j, :], None, written,
                                                    bass.IndirectOffsetOnAxis(ap=ridx[:, j, q:q + 1], axis=0)).then_inc(S(f"token_rows_{j}"), 16)

                pool.wait_ge(S("overflow_flag"), l + 1)
                over = pool.value_load(flag[0:1, 0:1], min_val=0, max_val=T)
                with pool.If(over > P):
                    for c in range(1, NT):
                        pool.wait_ge(S(f"over{l}_idx"), c)
                        for e in range(NE):
                            n = e + NE * (c - 1)
                            if n:
                                pool.wait_ge(S(f"over{l}_y"), n)
                            pool.indirect_dma_start(ug[:, 0, :], None, u_dram,
                                                    bass.IndirectOffsetOnAxis(ap=oidx[:, e:e + 1], axis=0)).then_inc(S(f"over{l}_rows"), 16)
                    pool.wait_ge(S(f"over{l}_y_stored"), 16 * NE * OVF + 16)
                    token_rows(y_dram)
                with pool.Else():
                    token_rows(y_dram[0:NE * P, :])
                pool.nop()

            moe(0)
            for j in range(NT):
                for hf in range(2):
                    evacuated(pool, ("yT", 0, j, hf))
            pool.wait_ge(S("hy_u"), DC)
            for dst, src in (
                (thy, A["t_hy"]), (embT, A["t_emb"]), (hw1, A["hy_f_w1"][0]), (hw2, A["hy_f_w2"][0]),
                (fprm[:, 0:1], A["hy_f_b1"].rearrange("o (n c) -> (o n) c", c=1)),
                (fprm[:, 1:2], A["hy_f_freq1"].rearrange("o (n c) -> (o n) c", c=1)),
                (fprm[:, 2:3], A["hy_f_b2"].rearrange("o (n c) -> (o n) c", c=1)),
                (fprm[:, 3:4], A["hy_f_freq2"].rearrange("o (n c) -> (o n) c", c=1)),
            ):
                pool.dma_start(dst, src).then_inc(S("hy_small_loaded"), 16)
            pool.memset(h2T[64:65, :], 0.0).then_inc(S("h2_row"), 1)
            pool.wait_ge(S("h2_row"), 1)
            for a0, _ in SEQS:
                pool.memset(h2T[64:65, a0:a0 + 1], 1.0).then_inc(S("h2_row"), 1)
            full(pool, ("ada", 1))
            pool.memset(ring[64:65, 0, :], 0.0).then_inc(S("w3_row_cleared"), 1)
            pool.wait_ge(S("w3_row_cleared"), 1)
            for od in range(2):
                pool.dma_start(ring[64:65, 0, 2 * od * D:(2 * od + 1) * D], A["hy_f_bias"][0, od:od + 1, :]).then_inc(S("w3_row_loaded"), 16)
            for c in range(2):
                if c == 1:
                    evacuated(pool, ("filt", 0, 1, NT - 1, 1))
                    pool.wait_ge(S("filters"), 2 * NT)
                pool.dma_start(dcy, A["t_decay"].rearrange("(j p) n -> p j n", p=P)[:, :, c * 512:(c + 1) * 512]).then_inc(S("decay_loaded"), 16)
                for od in range(2):
                    for pr in range(3):
                        n = (c * 2 + od) * 3 + pr
                        pool.wait_ge(S("products"), n + 1)
                        pool.tensor_tensor(Yf[:, 2 * pr, :], Yf[:, 2 * pr, :], ptmp[:, 2 * pr, :], ALU.subtract).then_inc(S("spectrum"), 1)
                        pool.tensor_tensor(Yf[:, 2 * pr + 1, :], Yf[:, 2 * pr + 1, :], ptmp[:, 2 * pr + 1, :], ALU.add).then_inc(S("spectrum"), 1)
            moe(1)

        @block.scalar
        def _(act):
            nchain = [0]

            def chain(ins):
                nchain[0] += 1
                ins.then_inc(S("act_chain"), 1)
                act.wait_ge(S("act_chain"), nchain[0])

            act.dma_start(tc_[:], A["t_common"]).then_inc(S("tables_loaded"), 16)
            act.dma_start(x_in[:, 0, :], A["x_prompt"][0]).then_inc(S("x_loaded"), 16)
            act.dma_start(x_in[:, 1:3, :], A["x_sample"][0].rearrange("(j p) d -> p j d", p=P)).then_inc(S("x_loaded"), 16)
            act.dma_start(pos_in, A["t_pos"].rearrange("(j p) d -> p j d", p=P)).then_inc(S("x_loaded"), 16)
            evacuated(act, "vec")
            act.activation(silc[:].rearrange("p k v -> p v k"), vecT[:, 0:2 * DC].rearrange("p (v k) -> p v k", v=2),
                           ACT.Silu).then_inc(S("silu_c"), 1)
            for j in range(NT):
                full(act, ("x", j, 0))
                free(act.copy(xT[:, 0:4, j * P:(j + 1) * P], bank(("x", j, 0))[:].rearrange("p (n t) -> p n t", n=4)), ("x", j, 0))

            def modulate(name):
                s = squares[name]
                x_ready(act, name)
                if name in ("moe0", "moe1", "hy", "fin"):
                    act.wait_ge(S("phase_over"), MODS.index(name))
                act.activation(s, xT[:], ACT.Square).then_inc(S("squares"), 1)
                full(act, ("ss", name))
                act.wait_ge(S("eps_set"), 1)
                free(act.activation(rstd[:], bank(("ss", name))[:, 0:T], ACT.Sqrt, bias=eps[:, 0:1], scale=1.0 / D), ("ss", name))
                for m in range(DC):
                    act.wait_ge(S("xn"), MODS.index(name) * 2 + 1 + m // 4)
                    if name == "fin":
                        act.activation(uT[:, m, :], s[:, m, :], ACT.Copy, scale=col(V_NF + m)).then_inc(S("fin_u"), 1)
                        continue
                    l, part = MODV[name]
                    for v, (a0, a1) in enumerate(SEQS):
                        ins = act.activation(uT[:, m, a0:a1], s[:, m, a0:a1], ACT.Identity,
                                             bias=mod(l, part, m, v), scale=mA[:, m, v:v + 1])
                    ins.then_inc(S(f"{name}_u"), 1)

            modulate("rec")
            for m in range(2):
                full(act, ("qka", m))
                free(act.activation(qka[:, m, :], bank(("qka", m))[:, 0:T], ACT.Copy, scale=DK ** -0.5), ("qka", m))
            for m in range(2):
                full(act, ("qkb", m))
                free(act.activation(qkb[:, m, :], bank(("qkb", m))[:, 0:T], ACT.Copy, scale=DK ** -0.5), ("qkb", m))
            for j in range(NT):
                full(act, ("ra", j))
                free(act.activation(mix_tok[:, j, 0:512], bank(("ra", j))[:], ACT.Silu), ("ra", j))
            for j in range(NT):
                full(act, ("ob", j))
                free(act.activation(mix_tok[:, j, 512:], bank(("ob", j))[:], ACT.Sigmoid), ("ob", j))
            for m in range(4):
                full(act, ("glog", m))
                act.activation(gt[:, m, :], bank(("glog", m))[:, 0:T], ACT.Abs, bias=col(V_GKB + m)).then_inc(S("glog_abs"), 1)
            act.wait_ge(S("mlstm_f"), 1)
            act.wait_ge(S("rec_small_loaded"), 16 * REC_SMALL)
            act.activation(g36[:, 2, :], g36[:, 1, :], ACT.Abs, bias=mcol[0:36, 1:2]).then_inc(S("f_abs"), 1)
            act.wait_ge(S("glog_abs"), 4)
            chain(act.activation(gt, gt, ACT.Exp, scale=-1.0))
            act.activation(gt, gt, ACT.Ln, bias=ones[:, 0:1]).then_inc(S("gla_ln"), 1)
            act.wait_ge(S("f_abs"), 1)
            chain(act.activation(g36[:, 2, :], g36[:, 2, :], ACT.Exp, scale=-1.0))
            act.activation(g36[:, 2, :], g36[:, 2, :], ACT.Ln, bias=ones[0:36, 0:1]).then_inc(S("mlstm_ln"), 1)
            act.wait_ge(S("gla_diff"), 1)
            full(act, ("ada", 0))
            act.activation(eq, gt, ACT.Exp, scale=1.0 / 16).then_inc(S("gla_exp"), 1)
            act.activation(ek, gt, ACT.Exp, scale=-1.0 / 16).then_inc(S("gla_exp"), 1)
            act.activation(fexp, fcol, ACT.Exp, scale=1.0 / 16).then_inc(S("gla_fexp"), 1)
            for k in range(4):
                full(act, ("keT", k))
                free(act.copy(ke_s[:, 2 * k:2 * k + 2, :], bank(("keT", k))[:, 0:2 * P].rearrange("p (a n) -> p a n", a=2)), ("keT", k))
            act.wait_ge(S("gla_fexp"), 1)
            for d in range(2):
                full(act, ("kv", d, 0))
                for kc in range(2):
                    ins = act.activation(S1[:, d, kc, :], bank(("kv", d, 0))[:, kc * DV:(kc + 1) * DV], ACT.Copy,
                                         scale=fexp[:, 2 * d + kc, 2:3])
                free(ins, ("kv", d, 0))
            for j in range(NT):
                full(act, ("oa", j))
                act.activation(osq[:, j, :], bank(("oa", j))[:], ACT.Square).then_inc(S("gla_squares"), 1)
            full(act, "mtok")
            act.copy(atok, bank("mtok")[:, 0:108].rearrange("p (j c) -> p j c", j=NT)).then_inc(S("atok"), 1)
            free(act.activation(emt, bank("mtok")[:, 108:216].rearrange("p (j c) -> p j c", j=NT), ACT.Exp), "mtok")
            for j in range(NT):
                full(act, ("oa", j))
            full(act, "kbt")
            free(act.copy(kbt, bank("kbt")[:, 0:2 * P].rearrange("p (a n) -> p a n", a=2)), "kbt")
            for h in range(H):
                kc, r0 = h // 2, (h % 2) * DK
                for d in range(2):
                    c = 4 * d + h
                    full(act, ("nM", d, h))
                    act.activation(qin[r0:r0 + DK, d, kc, :], bank(("nM", d, h))[r0:r0 + DK, P:T], ACT.Exp,
                                   bias=m0b[r0:r0 + DK, c:c + 1]).then_inc(S("qin_exp"), 1)
                    evacuated(act, ("nM", d, h))
                    act.activation(Wm[:, c, :], Wm[:, c, :], ACT.Exp).then_inc(S("weights"), 1)
            for d in range(2):
                full(act, ("C", d))
                free(act.copy(Cout[:, d, :], bank(("C", d))[:, 0:258]), ("C", d))
            n = 0
            for j in range(NT):
                for d in range(2):
                    for hp in range(2):
                        key = ("num", j, d, hp)
                        full(act, key)
                        if n >= 4:
                            act.wait_ge(S("den_read"), n - 3)
                        act.activation(dn[:, 2 * (n % 4):2 * (n % 4) + 2], bank(key)[:, DV:258:129], ACT.Abs).then_inc(S("den_abs"), 1)
                        n += 1
                act.wait_ge(S("h_sum"), 2 * (j + 1))
                act.wait_ge(S("gla_sums"), j + 1)
                act.activation(osq[:, j, :], hs[:, j, :], ACT.Square).then_inc(S("h_squares"), 1)
                act.wait_ge(S("sums"), j + 1)
                act.activation(rms[:, 1, j, :], rms[:, 0, j, :], ACT.Sqrt, bias=eps[:, 0:1], scale=1.0 / DV).then_inc(S("head_rms"), 1)
            for j in range(NT):
                for hf in range(2):
                    full(act, ("mixT", j, hf))
                    free(act.copy(uT[:, 4 * hf:4 * hf + 4, j * P:(j + 1) * P], bank(("mixT", j, hf))[:].rearrange("p (n t) -> p n t", n=4)), ("mixT", j, hf))

            def moe(l):
                modulate(f"moe{l}")
                act.wait_ge(S("exp_in"), l + 1)
                act.activation(R5[1], R5[0], ACT.Exp).then_inc(S("exp_out"), 1)
                for j in range(NT):
                    full(act, ("ut", l, j, 0))
                    free(act.copy(utok[:, j, 0:512], bank(("ut", l, j, 0))[:]), ("ut", l, j, 0))

                def pair(it):
                    for u in range(2):
                        full(act, (l, u, "X", 0), it)
                        free(act.copy(xg[:, u, 0:4, :], bank((l, u, "X", 0))[:].rearrange("p (k s) -> p k s", k=4)), (l, u, "X", 0))
                        full(act, (l, u, "G"), it)
                        free(act.activation(sg[:, u, :], bank((l, u, "G"))[:], ACT.Silu), (l, u, "G"))
                        full(act, (l, u, "Y", 0), it)
                        if not isinstance(it, int) or it + l:
                            act.wait_ge(S(f"y{u}_stored"), it * 16 + l * (NE // 2) * 16)
                        free(act.copy(ysb[:, u, 0:512], bank((l, u, "Y", 0))[:]), (l, u, "Y", 0))

                act.wait_ge(S("u_rows_stored"), 16 * NT * (l + 1))
                full(act, ("idx", l))
                pair(0)
                with act.Fori(1, NE // 2) as it:
                    pair(it)
                act.wait_ge(S("overflow_flag"), l + 1)
                over = act.value_load(flag[0:1, 0:1], min_val=0, max_val=T)
                with act.If(over > P):
                    for c in range(1, NT):
                        with act.Fori(0, NE) as e:
                            n = e + NE * (c - 1)
                            act.wait_ge(S(f"over{l}_x"), n + 1)
                            act.copy(xg[:, 0, 0:4, :], ps[0][:].rearrange("p (k s) -> p k s", k=4)).then_inc(S(f"over{l}_xa"), 1)
                            act.wait_ge(S(f"over{l}_gu"), n + 1)
                            act.activation(sg[:, 0, :], ps[2][:], ACT.Silu).then_inc(S(f"over{l}_silu"), 1)
                            act.wait_ge(S(f"over{l}_down"), n + 1)
                            act.copy(ysb[:, 0, 0:512], ps[5][:]).then_inc(S(f"over{l}_ya"), 1)
                    act.wait_ge(S(f"over{l}_y_stored"), 16 * NE * OVF + 16)
                with act.Else():
                    act.nop()
                act.nop()

            moe(0)
            modulate("hy")
            for n, key in enumerate(("f1", "f2")):
                act.wait_ge(S("sin_in"), n + 1)
                act.activation((h1T, h2T[0:64])[n], srt[:, 0, :], ACT.Sin).then_inc(S("sin_out"), 1)
            for m in range(3 * DC):
                full(act, ("z", m))
                if m < 2 * DC:
                    dst = zc[:, m % 2, :]
                    if m == 0:
                        act.wait_ge(S("sin_out"), 2)
                    if m >= 2:
                        full(act, ("zt", m - 2))
                else:
                    dst = x2T[:, m - 2 * DC, :]
                act.activation(dst, bank(("z", m))[:, 0:T], ACT.Copy, scale=col(V_CONV + 3 * DC + m)).then_inc(S("conv_mid"), 1)
                if 1 <= m <= 2 * DC:
                    q = m - 1
                    full(act, ("zt", q))
                    dst = (v_tok if q < DC else x1_tok)[:, :, (q % DC) * P:(q % DC + 1) * P]
                    free(act.copy(dst, bank(("zt", q))[:, 0:T].rearrange("p (j n) -> p j n", j=NT)), ("zt", q))
            for c in range(2):
                for od in range(2):
                    for q in range(8):
                        full(act, ("K", c, od, q))
                        free(act.copy(Kf[:, q, :], bank(("K", c, od, q))[:]), ("K", c, od, q))
            moe(1)
            modulate("fin")
            for j in range(NT):
                full(act, ("out", j, 0))
                free(act.copy(x_out[:, j, 0:512], bank(("out", j, 0))[:]), ("out", j, 0))

        @block.vector
        def _(v):
            nchain = [0]

            def chain(ins):
                nchain[0] += 1
                ins.then_inc(S("dve_chain"), 1)
                v.wait_ge(S("dve_chain"), nchain[0])

            v.memset(ones[:], 1.0).then_inc(S("ones_set"), 1)
            v.memset(eps[:], EPS).then_inc(S("eps_set"), 1)
            full(v, "vec")
            free(v.tensor_copy(vecT[:], bank("vec")[:, 0:V_ALL]), "vec")
            v.wait_ge(S("x_loaded"), 48)
            v.tensor_tensor(x_in[:, 1:3, :], x_in[:, 1:3, :], pos_in, ALU.add).then_inc(S("x_pos"), 1)
            for j in range(NT):
                full(v, ("x", j, 1))
                free(v.tensor_copy(xT[:, 4:8, j * P:(j + 1) * P], bank(("x", j, 1))[:].rearrange("p (n t) -> p n t", n=4)), ("x", j, 1))

            def ada_out(l):
                full(v, ("ada", l))
                n = NMOD * DC
                free(v.tensor_tensor(ada[:, l, :, :], bank(("ada", l))[:, 0:2 * n].rearrange("p (m v) -> p m v", v=2),
                                     bc(vecT[:, V_ADA + l * n:V_ADA + (l + 1) * n].unsqueeze(2), [P, n, 2]), ALU.add), ("ada", l))

            def modulate(name):
                s = squares[name]
                if name != "fin":
                    l, part = MODV[name]
                    evacuated(v, ("ada", l))
                    v.scalar_tensor_tensor(mA[:], ada[:, l, (part + 1) * DC:(part + 2) * DC, :], 1.0,
                                           bc(vecT[:, NVEC[name]:NVEC[name] + DC].unsqueeze(2), [P, DC, 2]),
                                           ALU.add, ALU.mult).then_inc(S("mA_ready"), 1)
                evacuated(v, ("ss", name))
                chain(v.reciprocal(rstd[:], rstd[:]))
                for hf in range(2):
                    v.tensor_tensor(s[:, 4 * hf:4 * hf + 4, :], xT[:, 4 * hf:4 * hf + 4, :],
                                    bc(rstd[:].unsqueeze(1), [P, 4, T]), ALU.mult).then_inc(S("xn"), 1)

            def residual(key, m, l, part):
                full(v, key)
                for q, (a0, a1) in enumerate(SEQS):
                    ins = v.scalar_tensor_tensor(xT[:, m, a0:a1], bank(key)[:, a0:a1], mod(l, part, m, q),
                                                 xT[:, m, a0:a1], ALU.mult, ALU.add)
                free(ins, key)

            ada_out(0)
            modulate("rec")
            for m in range(2, 4):
                full(v, ("qka", m))
                free(v.tensor_copy(qka[:, m, :], bank(("qka", m))[:, 0:T]), ("qka", m))
            full(v, "gk")
            v.wait_ge(S("gkw_cleared"), 1)
            free(v.tensor_copy(gkT, bank("gk")[0:32, 0:T]), "gk")
            full(v, "mg")
            v.wait_ge(S("g36_cleared"), 1)
            v.tensor_copy(g36[:, 0, :], bank("mg")[0:36, 0:T]).then_inc(S("mlstm_i"), 1)
            v.tensor_copy(g36[:, 1, :], bank("mg")[64:100, 0:T]).then_inc(S("mlstm_f"), 1)
            v.wait_ge(S("mlstm_f"), 1)
            v.wait_ge(S("rec_small_loaded"), 16 * REC_SMALL)
            free(v.tensor_scalar(g36[:, 0, :], g36[:, 0, :], mcol[0:36, 0:1], None, ALU.add), "mg")
            for m in range(2, 4):
                full(v, ("qkb", m))
                free(v.tensor_copy(qkb[:, m, :], bank(("qkb", m))[:, 0:T]), ("qkb", m))
            for j in range(NT):
                full(v, ("va", j))
                free(v.tensor_copy(va[:, j, :], bank(("va", j))[:]), ("va", j))
            for j in range(NT):
                full(v, ("vb", j))
                free(v.tensor_copy(vb[:, j, :, 0:DV], bank(("vb", j))[:].rearrange("p (h n) -> p h n", h=H)), ("vb", j))
            v.wait_ge(S("rec_u"), DC)
            for m in range(4):
                full(v, ("glog", m))
                v.wait_ge(S("glog_abs"), m + 1)
                free(v.tensor_scalar(B_[:, m, :], bank(("glog", m))[:, 0:T], col(V_GKB + m), 0.0, ALU.add, ALU.min), ("glog", m))
            v.wait_ge(S("gla_ln"), 1)
            evacuated(v, ("glog", 3))
            chain(v.tensor_tensor(B_, B_, gt, ALU.subtract))
            for m in range(4):
                for a0, a1 in SEQS:
                    src, dst = B_[:, m, a0:a1], gt[:, m, a0:a1]
                    if m >= 2:
                        src, dst = src[:, ::-1], dst[:, ::-1]
                    ins = v.tensor_tensor_scan(dst, bc(ones[:, 0:1], [P, a1 - a0]), src, 0.0, ALU.mult, ALU.add)
            chain(ins)
            v.tensor_copy(refs[:, 0:2, :], gt[:, 0:2, 63::P])
            chain(v.tensor_copy(refs[:, 2:4, :], gt[:, 2:4, 64::P]))
            for d, (first, second, end) in enumerate(((1, 2, LP - 1), (2, 1, 0))):
                r = refs[:, 2 * d:2 * d + 2, :]
                fc = fcol[:, 2 * d:2 * d + 2, :]
                v.tensor_copy(fc[:, :, 0:1], r[:, :, first:first + 1])
                v.tensor_tensor(fc[:, :, 1:2], r[:, :, second:second + 1], r[:, :, first:first + 1], ALU.subtract)
                ins = v.tensor_tensor(fc[:, :, 2:3], gt[:, 2 * d:2 * d + 2, end:end + 1], r[:, :, 0:1], ALU.subtract)
            chain(ins)
            v.tensor_tensor(gt.rearrange("p m (j t) -> p (m j) t", j=NT), gt.rearrange("p m (j t) -> p (m j) t", j=NT),
                            bc(refs.rearrange("p m j -> p (m j)").unsqueeze(2), [P, 4 * NT, P]),
                            ALU.subtract).then_inc(S("gla_diff"), 1)
            v.wait_ge(S("mlstm_ln"), 1)
            chain(v.tensor_scalar(g36[:, 1, :], g36[:, 1, :], mcol[0:36, 1:2], 0.0, ALU.add, ALU.min))
            chain(v.tensor_tensor(g36[:, 1, :], g36[:, 1, :], g36[:, 2, :], ALU.subtract))

            def scans(src, dst, op, init):
                for d in range(2):
                    for q, (a0, a1) in enumerate(SEQS):
                        r = slice(32 * d, 32 * d + 4)
                        s_, d_ = g36[r, src, a0:a1], g36[r, dst, a0:a1]
                        if d:
                            s_, d_ = s_[:, ::-1], d_[:, ::-1]
                        ins = v.tensor_tensor_scan(d_, bc(ones[r, 0:1], [4, a1 - a0]), s_, init(r, q), ALU.mult, op)
                chain(ins)

            scans(1, 3, ALU.add, lambda r, q: 0.0)
            chain(v.tensor_tensor(g36[:, 4, :], g36[:, 0, :], g36[:, 3, :], ALU.subtract))
            scans(4, 5, ALU.max, lambda r, q: 0.0 if q == 0 else mcol[r, 2:3])
            chain(v.tensor_scalar(g36[:, 5, :], g36[:, 5, :], -1.0, None, ALU.mult))
            v.tensor_tensor(g36[:, 2, :], g36[:, 3, :], g36[:, 5, :], ALU.subtract)
            v.tensor_tensor(g36[:, 6, :], g36[:, 5, :], g36[:, 3, :], ALU.subtract).then_inc(S("m_rows"), 1)
            v.wait_ge(S("gla_exp"), 1)
            evacuated(v, ("qka", 1))
            for d in range(2):
                v.tensor_tensor(eq[:, 2 * d:2 * d + 2, :], eq[:, 2 * d:2 * d + 2, :], qka[:, 0:2, :], ALU.mult).then_inc(S("qe"), 1)
            v.wait_ge(S("gla_fexp"), 1)
            for d in range(2):
                for kc in range(2):
                    ins = v.tensor_scalar(S0[:, d, kc, :], S0[:, d, kc, :], fexp[:, 2 * d + kc, 0:1], None, ALU.mult)
            ins.then_inc(S("state_first"), 1)
            v.wait_ge(S("A_cleared"), 1)
            v.wait_ge(S("rec_tables_loaded"), 16)
            for d in range(2):
                for j in range(NT):
                    full(v, ("A", d, j))
                    free(v.copy_predicated(A_sb[:, d, j, :].rearrange("p (h t) -> p h t", h=H), bc(amask[d].unsqueeze(1), [P, H, P]),
                                           bank(("A", d, j))[:].rearrange("p (h t) -> p h t", h=H)), ("A", d, j))
            v.wait_ge(S("state_first"), 1)
            for d in range(2):
                full(v, ("kv", d, 1))
                free(v.tensor_tensor(S3[:, d, :, :], bank(("kv", d, 1))[:, 0:2 * DV].rearrange("p (k v) -> p k v", k=2), S0[:, d, :, :], ALU.add), ("kv", d, 1))
                evacuated(v, ("kv", d, 1))
                for kc in range(2):
                    ins = v.tensor_scalar(S3[:, d, kc, :], S3[:, d, kc, :], fexp[:, 2 * d + kc, 1:2], None, ALU.mult)
                ins.then_inc(S("state_second"), 1)
            for j in range(NT):
                v.wait_ge(S("gla_squares"), j + 1)
                v.tensor_reduce(rms[:, 0, j, 0:4], osq[:, j, :].rearrange("p (h n) -> p h n", h=H), AX.X, ALU.add).then_inc(S("gla_sums"), 1)
                evacuated(v, ("ra", j))
                free(v.tensor_tensor(mix_tok[:, j, 0:512], mix_tok[:, j, 0:512], bank(("oa", j))[:], ALU.mult), ("oa", j))
            v.wait_ge(S("atok"), 1)
            evacuated(v, "kbt")
            SPAN = (((0, 0, P), (1, P, 3 * P), (2, 3 * P, 4 * P)), ((0, 0, P), (1, P, 2 * P), (2, 2 * P, 4 * P)))
            FROM = ((0, P, 2 * P), (0, P, P))
            def weigh(h, d):
                c = 4 * d + h
                v.wait_ge(S("qin_exp"), 2 * h + d + 1)
                full(v, ("nM", d, h))
                for (s, o0, o1), t0 in zip(SPAN[d], FROM[d]):
                    ins = v.scalar_tensor_tensor(Wm[:, c, o0:o1], bank(("nM", d, h))[:, t0:t0 + o1 - o0],
                                                 atok[:, s, 32 * d + h:32 * d + h + 1], mneg[d][:, o0:o1], ALU.add, ALU.min)
                free(ins, ("nM", d, h))

            def times_qk(h, d):
                c = 4 * d + h
                kc, r0 = h // 2, (h % 2) * DK
                v.wait_ge(S("weights"), 2 * h + d + 1)
                end = (LP - 1, 0)[d]
                chain(v.tensor_scalar(kw[:, c, :], kbt[:, kc, r0:r0 + DK], Wm[:, c, end:end + 1], None, ALU.mult))
                full(v, "qk0")
                ins = v.tensor_tensor(Wm[:, c, 0:P], Wm[:, c, 0:P], bank("qk0")[:, h * P:(h + 1) * P], ALU.mult)
                if h == H - 1 and d == 1:
                    free(ins, "qk0")
                full(v, ("qk", h))
                for s, o0, o1 in SPAN[d][1:]:
                    q0 = {(0, 1): 0, (0, 2): 384, (1, 1): 0, (1, 2): 256}[(d, s)]
                    ins = v.tensor_tensor(Wm[:, c, o0:o1], Wm[:, c, o0:o1], bank(("qk", h))[:, q0:q0 + o1 - o0], ALU.mult)
                    if d == 0 and s == 2:
                        ins.then_inc(S("P_fwd"), 1)
                    elif d == 1 and s == 2:
                        free(ins, ("qk", h))
            for h in range(H):
                for d in range(2):
                    weigh(h, d)
                for d in range(2):
                    times_qk(h, d)
            n = 0
            for j in range(NT):
                for d in range(2):
                    for hp in range(2):
                        key = ("num", j, d, hp)
                        den = dn[:, 2 * (n % 4):2 * (n % 4) + 2]
                        v.wait_ge(S("den_abs"), n + 1)
                        chain(v.tensor_tensor(den, den, emt[:, j, 32 * d + 2 * hp:32 * d + 2 * hp + 2], ALU.max))
                        chain(v.reciprocal(den, den))
                        full(v, key)
                        for hh_ in range(2):
                            dst = hs[:, j, (2 * hp + hh_) * DV:(2 * hp + hh_ + 1) * DV]
                            src = bank(key)[:, hh_ * 129:hh_ * 129 + DV]
                            if d == 0:
                                ins = v.tensor_scalar(dst, src, den[:, hh_:hh_ + 1], None, ALU.mult)
                            else:
                                ins = v.scalar_tensor_tensor(dst, src, den[:, hh_:hh_ + 1], dst, ALU.mult, ALU.add)
                            if hh_ == 0:
                                chain(ins)
                        free(ins, key)
                        evacuated(v, key)
                        n += 1
                        v.nop().then_inc(S("den_read"), 1)
                    v.nop().then_inc(S("h_sum"), 1)
                v.wait_ge(S("h_squares"), j + 1)
                v.tensor_reduce(rms[:, 0, j, 4:8], osq[:, j, :].rearrange("p (h n) -> p h n", h=H), AX.X, ALU.add).then_inc(S("sums"), 1)
                chain(v.tensor_tensor(mix_tok[:, j, 512:], mix_tok[:, j, 512:], hs[:, j, :], ALU.mult))
                v.wait_ge(S("head_rms"), j + 1)
                chain(v.reciprocal(rms[:, 2, j, :], rms[:, 1, j, :]))
                for h in range(2 * H):
                    w = gnw[:, 0:DV] if h < H else gnw[:, DV:]
                    y = mix_tok[:, j, h * DV:(h + 1) * DV]
                    ins = v.scalar_tensor_tensor(y, y, rms[:, 2, j, h:h + 1], w, ALU.mult, ALU.mult)
                ins.then_inc(S("mix"), 1)
            for m in range(DC):
                residual(("ro", m), m, 0, 2)

            def first_of(out, vals, tmp, top):
                chain(v.tensor_reduce(top, vals, AX.X, ALU.max))
                chain(v.tensor_tensor(tmp, vals, bc(top.unsqueeze(2), [P, NT, 4]), ALU.is_equal))
                chain(v.tensor_tensor(tmp, tmp, bc(w4.unsqueeze(1), [P, NT, 4]), ALU.mult))
                chain(v.tensor_reduce(R1[9], tmp, AX.X, ALU.max))
                chain(v.tensor_tensor(out, tmp, bc(R1[9].unsqueeze(2), [P, NT, 4]), ALU.is_equal))

            def moe(l):
                modulate(f"moe{l}")
                full(v, ("route", l))
                v.wait_ge(S("router_loaded"), 16 * 8)
                v.wait_ge(S(f"moe{l}_u"), DC)
                free(v.tensor_tensor(lg, bank(("route", l))[:, 0:60].rearrange("p (j c) -> p j c", j=NT),
                                     bc(b20[:, l, :].unsqueeze(1), [P, NT, 20]), ALU.add), ("route", l))
                evacuated(v, ("route", l))
                goh, tmp, ein, oh1, oh2, e2, gin, gmsk, t4 = R4[:9]
                gmax, m1, m2, esum, pg, w1, w2 = R1[:7]
                pl, mask, gate, o1, o2, posm, t16, rows = R16
                gl = lg[:, :, 0:NG]
                first_of(goh, gl, tmp, gmax)
                chain(v.tensor_tensor(R5[0][:, :, 0:4], gl, bc(gmax.unsqueeze(2), [P, NT, 4]), ALU.subtract))
                el = lg[:, :, NG:].rearrange("p j (g e) -> p j g e", g=NG)
                t44 = t16.rearrange("p j (g e) -> p j g e", g=NG)
                chain(v.tensor_tensor(t44, el, bc(goh.unsqueeze(3), [P, NT, NG, EPG]), ALU.mult))
                chain(v.tensor_reduce(ein, t16.rearrange("p j (g e) -> p j e g", g=NG), AX.X, ALU.add))
                first_of(oh1, ein, tmp, m1)
                chain(v.scalar_tensor_tensor(e2, oh1, NEG, ein, ALU.mult, ALU.add))
                first_of(oh2, e2, tmp, m2)
                v.tensor_tensor(R5[0][:, :, 4:5], m2.unsqueeze(2), m1.unsqueeze(2), ALU.subtract).then_inc(S("exp_in"), 1)
                g4 = goh.unsqueeze(3)
                for oh, dst in ((oh1, o1), (oh2, o2)):
                    chain(v.tensor_tensor(dst.rearrange("p j (g e) -> p j g e", g=NG), bc(g4, [P, NT, NG, EPG]),
                                          bc(oh.unsqueeze(2), [P, NT, NG, EPG]), ALU.mult))
                v.tensor_tensor(mask, o1, o2, ALU.add).then_inc(S("mask"), 1)
                v.wait_ge(S("exp_out"), l + 1)
                chain(v.tensor_reduce(esum, R5[1][:, :, 0:4], AX.X, ALU.add))
                e5 = R5[1][:, :, 4:5]
                chain(v.tensor_scalar(w1.unsqueeze(2), e5, 1.0, None, ALU.add))
                chain(v.tensor_tensor(w1, w1, esum, ALU.mult))
                chain(v.reciprocal(w1, w1))
                chain(v.tensor_tensor(w2.unsqueeze(2), w1.unsqueeze(2), e5, ALU.mult))
                chain(v.tensor_tensor(gate, o1, bc(w1.unsqueeze(2), [P, NT, NE]), ALU.mult))
                chain(v.tensor_tensor(t16, o2, bc(w2.unsqueeze(2), [P, NT, NE]), ALU.mult))
                chain(v.tensor_tensor(gid[:, :, :, 1:2], gate.unsqueeze(3), t16.unsqueeze(3), ALU.add))
                chain(v.tensor_copy(gid[:, :, :, 0:1], bc(tokid.unsqueeze(2).unsqueeze(3), [P, NT, NE, 1])))
                full(v, ("pos", l))
                chain(v.tensor_scalar(posm, mask, -BIG, BIG, ALU.mult, ALU.add))
                chain(v.tensor_copy(pl, bank(("pos", l))[:, 0:48].rearrange("p (j e) -> p j e", j=NT)))
                free(v.tensor_tensor(posm, posm, pl, ALU.add), ("pos", l))
                evacuated(v, ("pos", l))
                full(v, ("cnt", l))
                chain(v.tensor_reduce(cmax[:, 0:1], bank(("cnt", l))[:, 0:NE], AX.X, ALU.max))
                free(v.tensor_copy(flag, cmax[:, 0:1]), ("cnt", l))
                evacuated(v, ("cnt", l))
                v.nop().then_inc(S("overflow_flag"), 1)
                for j in range(NT):
                    v.tensor_tensor(pall[:, j, :, :], bc(iota.unsqueeze(1), [P, NE, P]),
                                    bc(posm[:, j, :].unsqueeze(2), [P, NE, P]), ALU.is_equal).then_inc(S("slot_lists"), 1)
                chain(v.tensor_scalar(rows, pl, float(P), float(NE * P - P), ALU.is_ge, ALU.mult))
                chain(v.tensor_tensor(rows, rows, pl, ALU.add))
                chain(v.tensor_scalar(t16, pl, float(2 * P), float(NE * P - P), ALU.is_ge, ALU.mult))
                chain(v.tensor_tensor(rows, rows, t16, ALU.add))
                chain(v.tensor_tensor(rows, rows, bc(ebase.unsqueeze(1), [P, NT, NE]), ALU.add))
                for q, oh in ((0, o1), (1, o2)):
                    chain(v.tensor_tensor(t16, rows, oh, ALU.mult))
                    chain(v.tensor_reduce(R1[7 + q], t16, AX.X, ALU.add))
                    chain(v.tensor_copy(ridx[:, :, q:q + 1], R1[7 + q].unsqueeze(2)))
                for j in range(NT):
                    full(v, ("ut", l, j, 1))
                    free(v.tensor_copy(utok[:, j, 512:], bank(("ut", l, j, 1))[:]), ("ut", l, j, 1))
                full(v, ("idx", l))
                chain(v.tensor_copy(gslot.unsqueeze(2), bank(("idx", l))[:, 0:32].rearrange("p (e c) -> p e c", c=2)[:, :, 1:2]))
                free(v.tensor_copy(idxu.unsqueeze(2), bank(("idx", l))[:, 0:32].rearrange("p (e c) -> p e c", c=2)[:, :, 0:1]), ("idx", l))

                def pair(it):
                    for u in range(2):
                        full(v, (l, u, "X", 1), it)
                        free(v.tensor_copy(xg[:, u, 4:8, :], bank((l, u, "X", 1))[:].rearrange("p (k s) -> p k s", k=4)), (l, u, "X", 1))
                        v.tensor_copy(gcol[:, u:u + 1], gslot[:, bass.ds(2 * it + u, 1)]).then_inc(S(f"gate{u}_ready"), 1)
                        full(v, (l, u, "U"), it)
                        evacuated(v, (l, u, "G"), it)
                        v.wait_ge(S(f"gate{u}_ready"), it + 1 + l * (NE // 2))
                        free(v.scalar_tensor_tensor(hh, bank((l, u, "U"))[:], gcol[:, u:u + 1], sg[:, u, :], ALU.mult, ALU.mult), (l, u, "U"))
                        full(v, (l, u, "HT"), it)
                        free(v.tensor_copy(hT, bank((l, u, "HT"))[:]), (l, u, "HT"))
                        full(v, (l, u, "Y", 1), it)
                        if not isinstance(it, int) or it + l:
                            v.wait_ge(S(f"y{u}_stored"), it * 16 + l * (NE // 2) * 16)
                        free(v.tensor_copy(ysb[:, u, 512:], bank((l, u, "Y", 1))[:]), (l, u, "Y", 1))

                v.wait_ge(S("u_rows_stored"), 16 * NT * (l + 1))
                pair(0)
                with v.Fori(1, NE // 2) as it:
                    pair(it)
                over = v.value_load(flag[0:1, 0:1], min_val=0, max_val=T)
                with v.If(over > P):
                    full(v, (l, 1, "Y", 1), NE // 2 - 1)
                    for c in range(1, NT):
                        v.wait_ge(S(f"over{l}_y_stored"), 16 * NE * (c - 1) + 16)
                        v.tensor_scalar(t16, posm, float(-P * c), None, ALU.add).then_inc(S(f"over{l}_pos"), 1)
                        v.wait_ge(S(f"over{l}_pos"), c)
                        for j in range(NT):
                            v.tensor_tensor(pall[:, j, :, :], bc(iota.unsqueeze(1), [P, NE, P]),
                                            bc(t16[:, j, :].unsqueeze(2), [P, NE, P]), ALU.is_equal).then_inc(S(f"over{l}_lists"), 1)
                        v.wait_ge(S(f"over{l}_idx_mm"), c)
                        pi = ps[7][:, 0:32].rearrange("p (e c) -> p e c", c=2)
                        v.tensor_copy(ogate.unsqueeze(2), pi[:, :, 1:2]).then_inc(S(f"over{l}_gates"), 1)
                        v.tensor_copy(oidx.unsqueeze(2), pi[:, :, 0:1]).then_inc(S(f"over{l}_idx"), 1)
                        v.wait_ge(S(f"over{l}_idx"), c)
                        with v.Fori(0, NE) as e:
                            n = e + NE * (c - 1)
                            v.wait_ge(S(f"over{l}_x"), n + 1)
                            v.tensor_copy(xg[:, 0, 4:8, :], ps[1][:].rearrange("p (k s) -> p k s", k=4)).then_inc(S(f"over{l}_xb"), 1)
                            v.tensor_copy(gcol[:, 0:1], ogate[:, bass.ds(e, 1)]).then_inc(S(f"over{l}_gcol"), 1)
                            v.wait_ge(S(f"over{l}_silu"), n + 1)
                            v.wait_ge(S(f"over{l}_gcol"), n + 1)
                            v.scalar_tensor_tensor(hh, ps[3][:], gcol[:, 0:1], sg[:, 0, :], ALU.mult, ALU.mult).then_inc(S(f"over{l}_h"), 1)
                            v.wait_ge(S(f"over{l}_ht"), n + 1)
                            v.tensor_copy(hT, ps[4][:]).then_inc(S(f"over{l}_hT"), 1)
                            v.wait_ge(S(f"over{l}_ya"), n + 1)
                            v.tensor_copy(ysb[:, 0, 512:], ps[6][:]).then_inc(S(f"over{l}_y"), 1)
                    v.wait_ge(S(f"over{l}_y_stored"), 16 * NE * OVF + 16)
                with v.Else():
                    v.nop()
                if l == 0:
                    ada_out(1)
                for j in range(NT):
                    v.wait_ge(S(f"token_rows_{j}"), 32 * (l + 1))
                    v.tensor_tensor(cmb[:, 0, j, :], cmb[:, 0, j, :], cmb[:, 1, j, :], ALU.add).then_inc(S("y_sum"), 1)
                for j in range(NT):
                    for hf in range(2):
                        key = ("yT", l, j, hf)
                        full(v, key)
                        for n in range(4):
                            m = 4 * hf + n
                            x = xT[:, m, j * P:(j + 1) * P]
                            ins = v.scalar_tensor_tensor(x, bank(key)[:, n * P:(n + 1) * P], mod(l, 5, m, min(j, 1)), x, ALU.mult, ALU.add)
                        free(ins, key)

            v.nop().then_inc(S("phase_over"), 1)
            moe(0)
            v.nop().then_inc(S("phase_over"), 1)
            modulate("hy")
            v.wait_ge(S("hy_small_loaded"), 16 * 8)
            TWO_PI_HI, MAGIC = 6.28125, 1.5 * 2 ** 23
            for n, key in enumerate(("f1", "f2")):
                full(v, key)
                if n == 1:
                    v.wait_ge(S("sin_out"), 1)
                free(v.tensor_scalar(srt[:, 0, :], bank(key)[0:64, 0:T], fprm[:, 2 * n:2 * n + 1], fprm[:, 2 * n + 1:2 * n + 2],
                                     ALU.add, ALU.mult), key)
                evacuated(v, key)
                chain(v.tensor_scalar(srt[:, 1, :], srt[:, 0, :], 1.0 / (2 * math.pi), MAGIC, ALU.mult, ALU.add))
                chain(v.tensor_scalar(srt[:, 1, :], srt[:, 1, :], MAGIC, None, ALU.subtract))
                chain(v.scalar_tensor_tensor(srt[:, 0, :], srt[:, 1, :], -TWO_PI_HI, srt[:, 0, :], ALU.mult, ALU.add))
                chain(v.scalar_tensor_tensor(srt[:, 0, :], srt[:, 1, :], -(2 * math.pi - TWO_PI_HI), srt[:, 0, :], ALU.mult, ALU.add))
                v.tensor_scalar(srt[:, 0, :], srt[:, 0, :], 3.1415925, -3.1415925, ALU.min, ALU.max).then_inc(S("sin_in"), 1)
            for m in range(3 * DC):
                dst = zc[:, m % 2, :] if m < 2 * DC else x2T[:, m - 2 * DC, :]
                src = bank(("z", m))
                full(v, ("z", m))
                v.wait_ge(S("conv_mid"), m + 1)
                for tap, so, do in ((0, 0, 1), (2, 1, 0)):
                    w = col(V_CONV + tap * 3 * DC + m)
                    for a0, a1 in SEQS:
                        n = a1 - a0 - 1
                        ins = v.scalar_tensor_tensor(dst[:, a0 + do:a0 + do + n], src[:, a0 + so:a0 + so + n], w,
                                                     dst[:, a0 + do:a0 + do + n], ALU.mult, ALU.add)
                    if tap == 0:
                        chain(ins)
                free(ins, ("z", m))
            for c in range(2):
                v.wait_ge(S("decay_loaded"), 16 * (c + 1))
                for od in range(2):
                    if c or od:
                        v.wait_ge(S("spectrum"), 6 * (2 * c + od))
                    if c == 0 and od == 0:
                        full(v, ("zt", 2 * DC - 1))
                    for j in range(NT):
                        kf, kb_ = ("filt", c, od, j, 0), ("filt", c, od, j, 1)
                        full(v, kf)
                        full(v, kb_)
                        if c or od or j:
                            v.wait_ge(S("filters"), NT * (2 * c + od) + j)
                        free(v.tensor_tensor(htmp, bank(kf)[:], dcy[:, j, :], ALU.mult), kf)
                        free(v.scalar_tensor_tensor(hpm[:, j, 1, :], bank(kb_)[:], notfirst if j < 2 else ones[:, 0:1],
                                                    dcy[:, j, :], ALU.mult, ALU.mult), kb_)
                        evacuated(v, kb_)
                        v.tensor_tensor(hpm[:, j, 0, :], htmp, hpm[:, j, 1, :], ALU.add)
                        v.tensor_tensor(hpm[:, j, 1, :], htmp, hpm[:, j, 1, :], ALU.subtract).then_inc(S("filters"), 1)
                    full(v, ("K", c, od, 7))
                    for q in range(8):
                        evacuated(v, ("K", c, od, q))
                    for pr, (p1, p2, p3) in enumerate(((0, 1, 2), (3, 5, 7), (4, 6, 4))):
                        re, im = ("F", c, od, 2 * pr), ("F", c, od, 2 * pr + 1)
                        full(v, im)
                        v.tensor_tensor(Yf[:, 2 * pr, :], Kf[:, p1, :], bank(re)[:], ALU.mult)
                        free(v.tensor_tensor(Yf[:, 2 * pr + 1, :], Kf[:, p2, :], bank(re)[:], ALU.mult), re)
                        v.tensor_tensor(ptmp[:, 2 * pr, :], Kf[:, p2, :], bank(im)[:], ALU.mult).then_inc(S("im_used"), 1)
                        free(v.tensor_tensor(ptmp[:, 2 * pr + 1, :], Kf[:, p3, :], bank(im)[:], ALU.mult), im)
                        evacuated(v, im)
                        v.nop().then_inc(S("products"), 1)
                    for q in range(NT if od == 0 else 4):
                        key = ("inv", c, od, q)
                        full(v, key)
                        if od == 0:
                            w = x1_tok[:, q, c * 512:(c + 1) * 512]
                            free(v.tensor_tensor(w, w, bank(key)[:], ALU.mult), key)
                        else:
                            m = 4 * c + q
                            free(v.tensor_tensor(uT[:, m, :], x2T[:, m, :], bank(key)[:, 0:T], ALU.mult), key)
            for m in range(DC):
                residual(("ho", m), m, 1, 2)
            v.nop().then_inc(S("phase_over"), 1)
            moe(1)
            v.nop().then_inc(S("phase_over"), 1)
            modulate("fin")
            for j in range(NT):
                full(v, ("out", j, 1))
                free(v.tensor_copy(x_out[:, j, 512:], bank(("out", j, 1))[:]), ("out", j, 1))

        @block.tensor
        def _(pe):
            def transposes(key, blocks):
                opened(pe, key)
                for at, src in blocks:
                    p, n = src.shape
                    ins = pe.transpose(bank(key)[0:n, at:at + p], src, ident[0:p, 0:p])
                done(ins, key)

            def accumulate(key, out, pairs):
                n = len(pairs)
                for i, (lhsT, rhs) in enumerate(pairs):
                    ins = pe.matmul(out, lhsT, rhs, start=(i == 0), stop=(i == n - 1))
                return ins

            pe.wait_ge(S("vec_rows_loaded"), 16 * 8)
            pe.wait_ge(S("tables_loaded"), 16)
            transposes("vec", [(0, vrows[0:60, 0, :]), (V_ADA, vrows[0:96, 1, :]), (V_CONV, vrows[0:72, 2, :])])
            pe.wait_ge(S("x_loaded"), 48)
            for j in range(NT):
                if j == 1:
                    pe.wait_ge(S("x_pos"), 1)
                for hf in range(2):
                    transposes(("x", j, hf), [(n * P, x_in[:, j, (4 * hf + n) * P:(4 * hf + n + 1) * P]) for n in range(4)])

            nturn = [0]

            def settle(ins):
                nturn[0] += 1
                ins.then_inc(S("row_half_done"), 1)
                pe.wait_ge(S("row_half_done"), nturn[0])

            def ada_mm(l):
                key = ("ada", l)
                opened(pe, key)
                for j in range(12):
                    w = loaded(pe, ("ada", l, j)).rearrange("p (k n) -> p k n", k=DC)
                    for mm in range(4):
                        m = 4 * j + mm
                        ins = accumulate(key, bank(key)[:, 2 * m:2 * m + 2],
                                         [(w[:, k, mm * P:(mm + 1) * P], silc[:, k, :]) for k in range(DC)])
                    if j < 11:
                        ins.then_inc(S("ada_slot_read"), 1)
                done(ins, key)

            def sumsq(name):
                key = ("ss", name)
                opened(pe, key)
                pe.wait_ge(S("squares"), MODS.index(name) + 1)
                pe.wait_ge(S("ones_set"), 1)
                done(accumulate(key, bank(key)[:, 0:T], [(ones[:], squares[name][:, k, :]) for k in range(DC)]), key)

            def wide(key, w, rows=P):
                opened(pe, key)
                done(accumulate(key, bank(key)[0:rows, 0:T], [(w(k), uT[:, k, :]) for k in range(DC)]), key)

            pe.wait_ge(S("silu_c"), 1)
            ada_mm(0)
            sumsq("rec")
            pe.wait_ge(S("rec_u"), DC)
            w = loaded(pe, ("rec", 0)).rearrange("p (k n) -> p k n", k=DC)
            for m in range(4):
                wide(("qka", m), lambda k: w[:, k, m * P:(m + 1) * P])
            pe.wait_ge(S("wg_loaded"), 16 * 5)
            wide("gk", lambda k: wg[:, k, 0:32], 32)
            wide("mg", lambda k: wg[:, k, 32:160])
            w = loaded(pe, ("rec", 3)).rearrange("p (k n) -> p k n", k=DC)
            for m in range(4):
                wide(("qkb", m), lambda k: w[:, k, m * P:(m + 1) * P])
            for name, jb in (("va", 1), ("vb", 4), ("ra", 2), ("ob", 5)):
                w = loaded(pe, ("rec", jb)).rearrange("p (k n) -> p k n", k=DC)
                for j in range(NT):
                    key = (name, j)
                    opened(pe, key)
                    done(accumulate(key, bank(key)[:], [(uT[:, k, j * P:(j + 1) * P], w[:, k, :]) for k in range(DC)]), key)
            evacuated(pe, "gk")
            pe.wait_ge(S("rec_small_loaded"), 16 * REC_SMALL)
            for m in range(4):
                opened(pe, ("glog", m))
                done(pe.matmul(bank(("glog", m))[:, 0:T], gkw[:, m * P:(m + 1) * P], gkT, start=True, stop=True), ("glog", m))
            def head(h):
                return h // 2, (h % 2) * DK
            pe.wait_ge(S("ke"), 2)
            for k in range(4):
                d = k // 2
                j = (0, 1 + d)[k % 2]
                transposes(("keT", k), [(kc * P, ek[:, 2 * d + kc, j * P:(j + 1) * P]) for kc in range(2)])
            pe.wait_ge(S("qe"), 2)
            for d in range(2):
                for j in range(NT):
                    key = ("A", d, j)
                    opened(pe, key)
                    t = slice(j * P, (j + 1) * P)
                    for h in (0, 2, 1, 3):
                        kc, r0 = head(h)
                        if h == 1:
                            settle(ins)
                        ins = pe.matmul(bank(key)[:, h * P:(h + 1) * P], ek[r0:r0 + DK, 2 * d + kc, t],
                                        eq[r0:r0 + DK, 2 * d + kc, t], start=True, stop=True)
                    done(ins, key)
            for w_ in range(2):
                for d in range(2):
                    key = ("kv", d, w_)
                    k = 2 * d + w_
                    j = (0, (1, 2)[d])[w_]
                    evacuated(pe, ("keT", k))
                    evacuated(pe, ("va", j))
                    opened(pe, key)
                    for h in range(H):
                        kc, r0 = head(h)
                        ins = pe.matmul(bank(key)[r0:r0 + DK, kc * DV:(kc + 1) * DV], ke_s[:, 2 * k + kc, r0:r0 + DK],
                                        va[:, j, h * DV:(h + 1) * DV], start=True, stop=True)
                    done(ins, key)
            for j in range(NT):
                key = ("oa", j)
                evacuated(pe, ("va", j))
                for d in range(2):
                    evacuated(pe, ("A", d, j))
                if j:
                    pe.wait_ge(S("state_first"), 1)
                    pe.wait_ge(S("state_second"), 2)
                opened(pe, key)
                for h in (0, 2, 1, 3):
                    kc, r0 = head(h)
                    if h == 1 and j:
                        settle(ins)
                    pairs = [(A_sb[:, d, j, h * P:(h + 1) * P], va[:, j, h * DV:(h + 1) * DV]) for d in range(2)]
                    if j:
                        for d in range(2):
                            first = j == (1, 2)[d]
                            st = (S0 if first else S3)[r0:r0 + DK, d, kc, :]
                            pairs.append((eq[r0:r0 + DK, 2 * d + kc, j * P:(j + 1) * P], st))
                    ins = accumulate(key, bank(key)[:, h * DV:(h + 1) * DV], pairs)
                done(ins, key)
            pe.wait_ge(S("m_rows"), 1)
            transposes("mtok", [((q * NT + j) * 36, g36[:, row, j * P:(j + 1) * P]) for q, row in enumerate((4, 6)) for j in range(NT)])
            for m in range(4):
                evacuated(pe, ("qkb", m))
            opened(pe, "qk0")
            for h in (0, 2, 1, 3):
                kc, r0 = head(h)
                if h == 1:
                    settle(ins)
                ins = pe.matmul(bank("qk0")[:, h * P:(h + 1) * P], qkb[r0:r0 + DK, 2 + kc, 0:P], qkb[r0:r0 + DK, kc, 0:P], start=True, stop=True)
            done(ins, "qk0")
            transposes("kbt", [(kc * P, qkb[:, 2 + kc, 0:P]) for kc in range(2)])
            for h in range(H):
                kc, r0 = head(h)
                opened(pe, ("qk", h))
                for s in range(2):
                    ins = pe.matmul(bank(("qk", h))[:, s * LS:(s + 1) * LS], qkb[r0:r0 + DK, 2 + kc, (s + 1) * P:(s + 2) * P],
                                    qkb[r0:r0 + DK, kc, P:T], start=True, stop=True)
                done(ins, ("qk", h))
                for d in range(2):
                    key = ("nM", d, h)
                    opened(pe, key)
                    r = 32 * d + h
                    done(pe.matmul(bank(key)[:, 0:T], bc(ident[0:36, r:r + 1], [36, P]), g36[:, 5, :], start=True, stop=True), key)
            evacuated(pe, ("qk", H - 1))
            evacuated(pe, ("vb", NT - 1))
            pe.wait_ge(S("vb_ones"), 1)
            for d in range(2):
                key = ("C", d)
                opened(pe, key)
                for h in range(H):
                    kc, r0 = head(h)
                    ins = pe.matmul(bank(key)[r0:r0 + DK, kc * 129:(kc + 1) * 129], kw[:, 4 * d + h, :], vb[:, 0, h, :], start=True, stop=True)
                done(ins, key)
            pe.wait_ge(S("qin"), 2)
            PB = {(0, 0): [(0, 0)], (0, 1): [(1, P)], (0, 2): [(1, 2 * P), (2, 3 * P)],
                  (1, 0): [(0, 0)], (1, 1): [(1, P), (2, 2 * P)], (1, 2): [(2, 3 * P)]}
            for j in range(NT):
                for d in range(2):
                    for hp in range(2):
                        key = ("num", j, d, hp)
                        opened(pe, key)
                        for hh_ in range(2):
                            h = 2 * hp + hh_
                            kc, r0 = head(h)
                            if j and hh_:
                                settle(ins)
                            pairs = [(Wm[:, 4 * d + h, o0:o0 + P], vb[:, s, h, :]) for s, o0 in PB[(d, j)]]
                            if j:
                                pairs.append((qin[r0:r0 + DK, d, kc, (j - 1) * P:j * P], C0[r0:r0 + DK, d, kc, :]))
                            ins = accumulate(key, bank(key)[:, hh_ * 129:(hh_ + 1) * 129], pairs)
                        done(ins, key)
            for j in range(NT):
                pe.wait_ge(S("mix"), j + 1)
                for hf in range(2):
                    transposes(("mixT", j, hf), [(n * P, mix_tok[:, j, (4 * hf + n) * P:(4 * hf + n + 1) * P]) for n in range(4)])
            for j in range(NT):
                for hf in range(2):
                    evacuated(pe, ("mixT", j, hf))
            for jb in range(2):
                w = loaded(pe, ("ro", jb)).rearrange("p (k n) -> p k n", k=DC)
                for mm in range(4):
                    wide(("ro", 4 * jb + mm), lambda k: w[:, k, mm * P:(mm + 1) * P])

            def moe(l):
                sumsq(f"moe{l}")
                pe.wait_ge(S(f"moe{l}_u"), DC)
                pe.wait_ge(S("router_loaded"), 16 * 8)
                key = ("route", l)
                opened(pe, key)
                for j in range(NT):
                    ins = accumulate(key, bank(key)[:, 20 * j:20 * j + 20], [(uT[:, k, j * P:(j + 1) * P], wr[:, k, l, :]) for k in range(DC)])
                done(ins, key)
                mask = R16[1]
                pe.wait_ge(S("mask"), l + 1)
                key = ("pos", l)
                opened(pe, key)
                for j in range(NT):
                    pairs = [(ones[:], mask[:, q, :]) for q in range(j)] + [(strict, mask[:, j, :])]
                    ins = accumulate(key, bank(key)[:, 16 * j:16 * j + 16], pairs)
                done(ins, key)
                key = ("cnt", l)
                opened(pe, key)
                done(accumulate(key, bank(key)[:, 0:NE], [(ones[:], mask[:, q, :]) for q in range(NT)]), key)
                for j in range(NT):
                    for hf in range(2):
                        transposes(("ut", l, j, hf), [(n * P, uT[:, 4 * hf + n, j * P:(j + 1) * P]) for n in range(4)])
                key = ("idx", l)
                opened(pe, key)
                pe.wait_ge(S("slot_lists"), NT * (l + 1))
                for e in range(NE):
                    ins = accumulate(key, bank(key)[:, 2 * e:2 * e + 2], [(pall[:, j, e, :], gid[:, j, e, :]) for j in range(NT)])
                done(ins, key)
                evacuated(pe, key)
                base = moe_base[l]

                def t8(key, it, n0, u):
                    opened(pe, key, it)
                    for n in range(4):
                        ins = pe.transpose(bank(key)[:, n * P:(n + 1) * P], ug[:, u, (n0 + n) * P:(n0 + n + 1) * P], ident)
                    done(ins, key)

                def gathered(it, u):
                    pe.wait_ge(S(f"rows{u}_gathered"), (it + l * (NE // 2)) * 16 + 16)
                    t8((l, u, "X", 0), it, 0, u)
                    t8((l, u, "X", 1), it, 4, u)

                def slot(it, u, kind):
                    n = 3 * u + kind
                    pe.wait_ge(S(f"slot{n}_loaded"), 16 * base[n] + 16 + it * 16)
                    return ring[:, n, :]

                def pair(it, last):
                    for u in range(2):
                        evacuated(pe, (l, u, "X", 0), it)
                        evacuated(pe, (l, u, "X", 1), it)
                        for kind, name in ((0, "G"), (1, "U")):
                            key = (l, u, name)
                            w = slot(it, u, kind).rearrange("p (k n) -> p k n", k=DC)
                            opened(pe, key, it)
                            done(accumulate(key, bank(key)[:], [(xg[:, u, k, :], w[:, k, :]) for k in range(DC)]), key)
                        if u == 0:
                            gathered(it, 1)
                        elif not last:
                            gathered(it + 1, 0)
                        key = (l, u, "HT")
                        opened(pe, key, it)
                        evacuated(pe, (l, u, "U"), it)
                        for n in range(4):
                            ins = pe.transpose(bank(key)[:, n * P:(n + 1) * P], hh[:, n * P:(n + 1) * P], ident)
                        done(ins, key)
                        evacuated(pe, key, it)
                        w = slot(it, u, 2).rearrange("p (k n) -> p k n", k=4)
                        for q in range(2):
                            key = (l, u, "Y", q)
                            opened(pe, key, it)
                            done(accumulate(key, bank(key)[:], [(hT[:, k * P:(k + 1) * P], w[:, k, q * 512:(q + 1) * 512]) for k in range(4)]), key)

                gathered(0, 0)
                with pe.Fori(0, NE // 2 - 1) as it:
                    pair(it, False)
                pair(NE // 2 - 1, True)
                pe.wait_ge(S("overflow_flag"), l + 1)
                over = pe.value_load(flag[0:1, 0:1], min_val=0, max_val=T)
                with pe.If(over > P):
                    for q in range(2):
                        evacuated(pe, (l, 1, "Y", q), NE // 2 - 1)
                    for c in range(1, NT):
                        pe.wait_ge(S(f"over{l}_lists"), NT * c)
                        for e in range(NE):
                            ins = accumulate(None, ps[7][:, 2 * e:2 * e + 2], [(pall[:, j, e, :], gid[:, j, e, :]) for j in range(NT)])
                        ins.then_inc(S(f"over{l}_idx_mm"), 1)
                        with pe.Fori(0, NE) as e:
                            n = e + NE * (c - 1)
                            pe.wait_ge(S(f"over{l}_rows"), 16 * n + 16)
                            for k in range(DC):
                                ins = pe.transpose(ps[k // 4][:, (k % 4) * P:(k % 4 + 1) * P], ug[:, 0, k * P:(k + 1) * P], ident)
                            ins.then_inc(S(f"over{l}_x"), 1)
                            pe.wait_ge(S(f"over{l}_xa"), n + 1)
                            pe.wait_ge(S(f"over{l}_xb"), n + 1)
                            for kind in range(2):
                                pe.wait_ge(S(f"over{l}_loaded{kind}"), 16 * n + 16)
                                w = ring[:, kind, :].rearrange("p (k n) -> p k n", k=DC)
                                ins = accumulate(None, ps[2 + kind][:], [(xg[:, 0, k, :], w[:, k, :]) for k in range(DC)])
                            ins.then_inc(S(f"over{l}_gu"), 1)
                            pe.wait_ge(S(f"over{l}_h"), n + 1)
                            for k in range(4):
                                ins = pe.transpose(ps[4][:, k * P:(k + 1) * P], hh[:, k * P:(k + 1) * P], ident)
                            ins.then_inc(S(f"over{l}_ht"), 1)
                            pe.wait_ge(S(f"over{l}_hT"), n + 1)
                            pe.wait_ge(S(f"over{l}_loaded2"), 16 * n + 16)
                            w = ring[:, 2, :].rearrange("p (k n) -> p k n", k=4)
                            for q in range(2):
                                ins = accumulate(None, ps[5 + q][:], [(hT[:, k * P:(k + 1) * P], w[:, k, q * 512:(q + 1) * 512]) for k in range(4)])
                            ins.then_inc(S(f"over{l}_down"), 1)
                    pe.wait_ge(S(f"over{l}_y_stored"), 16 * NE * OVF + 16)
                with pe.Else():
                    pe.nop()
                pe.nop()
                if l == 0:
                    ada_mm(1)
                for j in range(NT):
                    pe.wait_ge(S("y_sum"), NT * l + j + 1)
                    for hf in range(2):
                        transposes(("yT", l, j, hf), [(n * P, cmb[:, 0, j, (4 * hf + n) * P:(4 * hf + n + 1) * P]) for n in range(4)])

            moe(0)
            sumsq("hy")
            pe.wait_ge(S("hy_small_loaded"), 16 * 8)
            opened(pe, "f1")
            done(pe.matmul(bank("f1")[0:64, 0:T], hw1, embT, start=True, stop=True), "f1")
            pe.wait_ge(S("sin_out"), 1)
            opened(pe, "f2")
            done(pe.matmul(bank("f2")[0:64, 0:T], hw2, h1T, start=True, stop=True), "f2")
            pe.wait_ge(S("hy_u"), DC)

            def zt(m):
                evacuated(pe, ("z", m))
                transposes(("zt", m), [(j * P, zc[:, m % 2, j * P:(j + 1) * P]) for j in range(NT)])

            for m in range(3 * DC):
                if m % 4 == 0:
                    w = loaded(pe, ("hin", m // 4)).rearrange("p (k n) -> p k n", k=DC)
                wide(("z", m), lambda k: w[:, k, (m % 4) * P:(m % 4 + 1) * P])
                if 1 <= m <= 2 * DC:
                    zt(m - 1)
            CP, SNP, SP, C3P, GRP, GIP = (thy[:, i * P:(i + 1) * P] for i in range(6))
            tab = [thy[:, 768 + 512 * i:1280 + 512 * i].rearrange("p (a f) -> p a f", a=2) for i in range(2)]
            CS, SNS = tab
            SS, C3S = (thy[:, 1792 + 256 * i:2048 + 256 * i].rearrange("p (a f) -> p a f", a=2) for i in range(2))
            GRS, GIS = (thy[:, 2304 + 512 * i:2816 + 512 * i].rearrange("p (a f) -> p a f", a=2) for i in range(2))
            w3 = loaded(pe, "w3")
            pe.wait_ge(S("w3_row_loaded"), 32)
            pe.wait_ge(S("h2_row"), 3)
            pe.wait_ge(S("sin_out"), 2)
            for c in range(2):
                for od in range(2):
                    for j in range(NT):
                        for d in range(2):
                            key = ("filt", c, od, j, d)
                            opened(pe, key)
                            at = (2 * od + d) * D + c * 512
                            done(pe.matmul(bank(key)[:], h2T[:, j * P:(j + 1) * P], w3[0:65, at:at + 512], start=True, stop=True), key)
                    pe.wait_ge(S("filters"), NT * (2 * c + od + 1))
                    if c or od:
                        pe.wait_ge(S("products"), 3 * (2 * c + od))
                    f1, f0 = slice(P, 2 * P), slice(0, P)
                    for q, (tabs, s) in enumerate((
                        (CP, 0), (SP, 1), (C3P, 0), ((CS, f0), 0), ((CS, f1), 0), ((SS, f0), 1), ((SNS, f1), 1), ((C3S, f0), 0),
                    )):
                        key = ("K", c, od, q)
                        opened(pe, key)
                        if q < 3:
                            pairs = [(tabs, hpm[:, 0, s, :])]
                        else:
                            pairs = [(tabs[0][:, tt, tabs[1]], hpm[:, 1 + tt, s, :]) for tt in range(2)]
                        done(accumulate(key, bank(key)[:], pairs), key)
                    sig = v_tok if od == 0 else x1_tok
                    if od == 0:
                        for m in range(2 * DC):
                            evacuated(pe, ("zt", m))
                    else:
                        for q in range(NT):
                            evacuated(pe, ("inv", c, 0, q))
                    for q in range(6):
                        key = ("F", c, od, q)
                        opened(pe, key)
                        if q < 2:
                            pairs = [((CP, SNP)[q], sig[:, 0, c * 512:(c + 1) * 512])]
                        else:
                            f = (f0, f1)[(q - 2) // 2]
                            pairs = [((CS, SNS)[q % 2][:, tt, f], sig[:, 1 + tt, c * 512:(c + 1) * 512]) for tt in range(2)]
                        done(accumulate(key, bank(key)[:], pairs), key)
                    pe.wait_ge(S("spectrum"), 6 * (2 * c + od + 1))
                    for q in range(NT if od == 0 else 4):
                        key = ("inv", c, od, q)
                        opened(pe, key)
                        if od == 0:
                            if q == 0:
                                pairs = [(GRP, Yf[:, 0, :]), (GIP, Yf[:, 1, :])]
                            else:
                                t = slice((q - 1) * P, q * P)
                                pairs = [(g[:, ft, t], Yf[:, 2 + 2 * ft + i, :]) for ft in range(2) for i, g in enumerate((GRS, GIS))]
                            done(accumulate(key, bank(key)[:], pairs), key)
                        else:
                            ch = slice(q * P, (q + 1) * P)
                            accumulate(key, bank(key)[:, 0:P], [(Yf[:, 0, ch], GRP), (Yf[:, 1, ch], GIP)])
                            done(accumulate(key, bank(key)[:, P:T], [(Yf[:, 2 + 2 * ft + i, ch], g[:, ft, :]) for ft in range(2)
                                                                     for i, g in enumerate((GRS, GIS))]), key)
            for q in range(4):
                evacuated(pe, ("inv", 0, 1, q))
                evacuated(pe, ("inv", 1, 1, q))
            for jb in range(2):
                w = loaded(pe, ("ho", jb)).rearrange("p (k n) -> p k n", k=DC)
                for mm in range(4):
                    wide(("ho", 4 * jb + mm), lambda k: w[:, k, mm * P:(mm + 1) * P])
            moe(1)
            sumsq("fin")
            pe.wait_ge(S("fin_u"), DC)
            for j in range(NT):
                for hf in range(2):
                    transposes(("out", j, hf), [(n * P, uT[:, 4 * hf + n, j * P:(j + 1) * P]) for n in range(4)])


_OUTS = [(1, LP, D), (1, LS, D), (1, 1, 2, H, DK, DV), (1, 1, 2, H, DK, DV), (1, 1, 2, H, DK), (1, 1, 2, H)]


def kernel(**inputs):
    import concourse.bacc as _bacc
    from concourse.bass_utils import run_bass_kernel_spmd as _run

    nc = _bacc.Bacc("TRN2", target_bir_lowering=False, num_devices=1)
    arrays, A = {}, {}
    for name, a in list(inputs.items()) + list(tables().items()):
        a = np.ascontiguousarray(a)
        arrays[f"in_{name}"] = a
        A[name] = nc.dram_tensor(f"in_{name}", a.shape, mybir.dt.from_np(a.dtype), kind="ExternalInput").ap()
    O = [nc.dram_tensor(f"out_{i}", shape, F32, kind="ExternalOutput").ap() for i, shape in enumerate(_OUTS)]
    build(nc, A, O)
    r = _run(nc, [arrays], core_ids=[0])
    return tuple(r.results[0][f"out_{i}"] for i in range(len(_OUTS)))
```

```python
import math
from contextlib import ExitStack

import numpy as np

import concourse.bass as bass
from concourse import mybir

F32 = mybir.dt.float32
U32 = mybir.dt.uint32
I32 = mybir.dt.int32
ALU = mybir.AluOpType
ACT = mybir.ActivationFunctionType
AX = mybir.AxisListType

P = 128
D = 1024
DC = D // P
LP, LS = 128, 256
T = LP + LS
NT = T // P
SEQS = [(0, LP), (LP, T)]
H = 4
DK, DV = 64, 128
RANK = 16
NMOD = 6
NG, EPG = 4, 4
NE = NG * EPG
DE = D // 2
EPS = 1e-6
RING = 6
SLOT = 4096
NEG = -1.0e30
BIG = 1.0e4

V_CTX, V_C, V_N1, V_N2, V_NF, V_GKB, V_ADA, V_CONV = 0, 8, 16, 32, 48, 56, 60, 156
V_ALL = V_CONV + 72


def tables():
    i = np.arange(P)
    common = np.concatenate([
        np.eye(P), (i[:, None] < i[None, :]), np.tile(i, (P, 1)),
        i[:, None] + P * np.arange(NT)[None, :], np.tile([4, 3, 2, 1], (P, 1)),
        np.tile(P * np.arange(NE), (P, 1)), (i[:, None] > 0)], axis=1).astype(np.float32)
    le, ge = i[:, None] <= i[None, :], i[:, None] >= i[None, :]
    zero = np.zeros((P, P))
    nf, nb = np.where(le, 0.0, NEG), np.where(ge, 0.0, NEG)
    rec = np.concatenate([nf, nf, zero, nf, nb, nb, zero, nb, le, ge], axis=1).astype(np.float32)

    def dft(L):
        t, f = np.arange(L)[:, None], np.arange(L)[None, :]
        w = math.pi * ((t * f) % (2 * L)) / L
        c, s = np.cos(w), -np.sin(w)
        alt = (-1.0) ** np.arange(L)
        s_nyq, c_nyq = s.copy(), c.copy()
        s_nyq[:, 0] = alt
        c_nyq[:, 0] = alt
        gr, gi = 2 * c.T / (2 * L), 2 * s.T / (2 * L)
        gr[0] = 1.0 / (2 * L)
        gi[0] = alt / (2 * L)
        return c, s_nyq, s, c_nyq, gr, gi

    def rows(m):
        return m.reshape(-1, P, m.shape[1]).transpose(1, 0, 2).reshape(P, -1)

    cp, snp, sp_, c3p, grp, gip = dft(LP)
    cs, sns, ss, c3s, grs, gis = dft(LS)
    hy = np.concatenate([cp, snp, sp_, c3p, grp, gip, rows(cs), rows(sns), rows(ss[:, :P]),
                         rows(c3s[:, :P]), rows(grs), rows(gis)], axis=1).astype(np.float32)

    def linspace(a, b, n):
        return np.linspace(np.float32(a), np.float32(b), n, dtype=np.float32)

    emb, dec = [], []
    lo, hi = abs(math.log(1e-2)) / 1.5, abs(math.log(1e-2)) / 0.3
    for L in (LP, LS):
        t = linspace(0.0, 1.0, L)[:, None]
        w = (2.0 * math.pi * np.arange(L)[:, None] / L)
        f = linspace(1e-4, 15, 16)[None, :].astype(np.float64)
        emb.append(np.concatenate([t, np.cos(f * w), -np.sin(f * w)], axis=1))
        dec.append(np.exp(-t * linspace(lo, hi, D)[None, :]))
    emb = np.concatenate(emb).T.astype(np.float32)
    dec = np.concatenate(dec).astype(np.float32)
    r, cl = np.meshgrid(np.arange(LS // 64), np.arange(64), indexing="ij")
    omega = 10000.0 ** (-np.arange(D // 4) / (D // 4))
    pos = []
    for q in (r, cl):
        a = q.reshape(-1, 1) * omega[None, :]
        pos += [np.sin(a), np.cos(a)]
    pos = np.concatenate(pos, axis=1).astype(np.float32)
    return dict(t_common=common, t_rec=rec, t_hy=hy, t_emb=np.ascontiguousarray(emb), t_decay=dec, t_pos=pos)


def build(nc, A, O):
    ctx = ExitStack()
    with ctx:
        def sb(name, shape, dt=F32):
            return ctx.enter_context(nc.sbuf_tensor(name, shape, dt))

        semaphores = {}

        def S(name):
            if name not in semaphores:
                semaphores[name] = ctx.enter_context(nc.semaphore(name))
            return semaphores[name]

        ring = sb("ring", [P, RING, SLOT])
        xT = sb("xT", [P, DC, T])
        uT = sb("uT", [P, DC, T])
        tc_ = sb("tab_common", [P, 3 * P + NT + 4 + NE + 1])
        ident, strict, iota = tc_[:, 0:P], tc_[:, P:2 * P], tc_[:, 2 * P:3 * P]
        o = 3 * P
        tokid, w4, ebase = tc_[:, o:o + NT], tc_[:, o + NT:o + NT + 4], tc_[:, o + NT + 4:o + NT + 4 + NE]
        notfirst = tc_[:, o + NT + 4 + NE:o + NT + 5 + NE]
        ones = sb("ones", [P, P])
        eps = sb("eps", [P, 1])
        vecT = sb("vecT", [P, V_ALL])
        silc = sb("silc", [P, DC, 2])
        ada = sb("ada", [P, 2, NMOD * DC, 2])
        flag = sb("flag", [P, 1])[:].bitcast(I32)
        mA = sb("mA", [P, DC, 2])
        rstd = sb("rstd", [P, T])
        b20 = sb("b20", [P, 2, NG + NE])
        wr = sb("wr", [P, DC, 2, NG + NE])
        WORK = 19716
        work = sb("work", [P, WORK])
        ps = [ctx.enter_context(nc.psum_tensor(f"ps{b}", [P, 512], F32)) for b in range(8)]

        u_dram = nc.dram_tensor("u_rows", [T, D], F32).ap()
        y_dram = nc.dram_tensor("y_rows", [NT * NE * P, D], F32).ap()

        class Arena:

            def __init__(self):
                self.at, self.high = 0, 0

            def get(self, n, high=False, parts=P):
                if high:
                    a, self.high = self.high, self.high + n
                    assert self.high <= 2 * SLOT, self.high
                    return ring[0:parts, 4:6, :].rearrange("p a b -> p (a b)")[:, a:a + n]
                a, self.at = self.at, self.at + n
                assert self.at <= WORK, self.at
                return work[0:parts, a:a + n]

        bank_uses = [0] * 8
        jobs = {}
        turn = [0]

        def claim(key, bank=None, keep=None):
            if bank is None:
                if turn[0] % 8 == keep:
                    turn[0] += 1
                bank = turn[0] % 8
                turn[0] += 1
            bank_uses[bank] += 1
            jobs[key] = (bank, bank_uses[bank], 0)
            return bank

        def claim_loop(n, body):
            per = [sum(b == bank for _, b in body) for bank in range(8)]
            seen = [0] * 8
            for key, bank in body:
                seen[bank] += 1
                jobs[key] = (bank, bank_uses[bank] + seen[bank], per[bank])
            for bank in range(8):
                bank_uses[bank] += n * per[bank]

        bank_full = [S(f"bank{b}_full") for b in range(8)]
        bank_free = [S(f"bank{b}_free") for b in range(8)]

        def bank(key):
            return ps[jobs[key][0]]

        def opened(eng, key, it=0):
            b, use, per = jobs[key]
            if isinstance(it, int) and use - 1 + it * per == 0:
                return
            eng.wait_ge(bank_free[b], it * per + (use - 1))

        def full(eng, key, it=0):
            b, use, per = jobs[key]
            eng.wait_ge(bank_full[b], it * per + use)

        def done(ins, key):
            ins.then_inc(bank_full[jobs[key][0]], 1)

        def free(ins, key):
            ins.then_inc(bank_free[jobs[key][0]], 1)

        claim("vec", 7)

        def claim_ada(l, first, last):
            if first == 0:
                claim(("ada", l), 7)
            for j in range(first, last):
                claim(("adam", l, j), 5 + j % 2)

        claim_ada(0, 0, 12)

        def claim_ada_step(j, rows=None, columns=None):
            claim(("adam", 1, j), rows)
            if j:
                claim(("adac", j - 1), columns)
            if j == 11:
                claim(("adac", 11), columns)

        for j in range(NT):
            for hf in range(2):
                claim(("x", j, hf), (2 * j + hf) % 5)
        MODS = ["rec", "moe0", "hy", "moe1", "fin"]

        claim(("ss", "rec"), 4)
        for m in range(4):
            claim(("qka", m))
        claim("gk")
        claim("mg")
        for m in range(4):
            claim(("qkb", m))
        for m in range(4):
            claim(("glog", m))
        for n in ("va", "vb", "ra", "ob"):
            for j in range(NT):
                claim((n, j))
        for k in range(4):
            claim(("keT", k))
        for d in range(2):
            for j in range(NT):
                claim(("A", d, j))
        for d in range(2):
            claim(("kv", d, 0))
        for d in range(2):
            claim(("kv", d, 1))
        for j in range(NT):
            claim(("oa", j))
        claim("mtok")
        claim("qk0", 7)
        claim("kbt", keep=7)
        for h in range(H):
            claim(("qk", h), keep=7)
            for d in range(2):
                claim(("nM", d, h), keep=7)
        for d in range(2):
            claim(("C", d))
        for j in range(NT):
            for d in range(2):
                for hp in range(2):
                    claim(("num", j, d, hp))
            claim_ada_step(j)
        for j in range(NT):
            for hf in range(2):
                claim(("mixT", j, hf))
            if j == 1:
                claim_ada_step(3)
        claim(("ss", "moe0"), 7)
        for m in range(DC):
            claim(("ro", m), m % 7)

        BODY = [("X", 0), ("X", 1), ("G",), ("U",), ("HT",), ("Y", 0), ("Y", 1)]
        ADA1 = (5, 7, 10, 12)
        claim_ada_step(4, 5, 7)

        def claim_moe(l):
            claim(("routeT", l), 0)
            for j in range(NT):
                for hf in range(2):
                    claim(("ut", l, j, hf), (1, 2, 3, 4, 1, 0)[2 * j + hf])
                if j == 1:
                    claim(("route", l), 7)
            if l == 0:
                for j in range(ADA1[0], ADA1[1]):
                    claim_ada_step(j, 5 + j % 2, 7)
            claim(("pos", l), 3)
            claim(("cnt", l), 1)
            if l == 0:
                for j in range(ADA1[1], ADA1[2]):
                    claim_ada_step(j, 5 + j % 2, 7)
            for g in range(4):
                claim(("idxT", l, g), (2, 4, 1, 3)[g])
            claim(("idx0", l), 0)
            claim(("idx", l), 2)
            if l == 0:
                for j in range(ADA1[2], ADA1[3]):
                    claim_ada_step(j, 5 + j % 2, 7)
            body = []
            for u in range(2):
                for k, name in enumerate(BODY):
                    body.append(((l, u) + name, k))
            claim_loop(NE // 2, body)
            for j in range(NT):
                for hf in range(2):
                    claim(("yT", l, j, hf), (2 * j + hf) % 6)
            claim(("ss", ("hy", "fin")[l]), 7)

        claim_moe(0)
        for m in range(3 * DC):
            claim(("z", m))
            if m in (1, 3):
                claim(("f1", None, "f2")[m - 1])
            if 1 <= m <= 2 * DC:
                claim(("zt", m - 1))
        NEXT = {(0, 0): (0, 1), (0, 1): (1, 0), (1, 0): (1, 1)}

        def claim_filters(c, od):
            for j in range(NT):
                for d in range(2):
                    claim(("filt", c, od, j, d))

        for c in range(2):
            for od in range(2):
                if c == 0 and od == 0:
                    claim_filters(0, 0)
                for q in range(8):
                    claim(("K", c, od, q))
                for q in range(6):
                    claim(("F", c, od, q))
                if (c, od) != (1, 1):
                    claim_filters(*NEXT[(c, od)])
                for q in range(NT if od == 0 else 4):
                    claim(("inv", c, od, q))
        claim(("ss", "moe1"), 7)
        for m in range(DC):
            claim(("ho", m), m % 7)
        claim_moe(1)
        for j in range(NT):
            for hf in range(2):
                claim(("out", j, hf))

        loads = {}
        slot_uses = [0] * RING
        order = []

        def cols(w, j):
            return w.rearrange("(k p) n -> p k n", p=P)[:, :, j * 512:(j + 1) * 512]

        def add_load(key, slot, src, last, wait=None):
            slot_uses[slot] += 1
            loads[key] = (slot, slot_uses[slot], 0)
            order.append(("load", slot, src, last, wait))

        for j in range(12):
            add_load(("ada", 0, j), j % 6, cols(A["ada_w"][0], j), ("adam", 0, j))
        REC_ORDER = [(0, ("qka", 3)), (3, ("qkb", 3)), (1, ("va", 2)), (4, ("vb", 2)), (2, ("ra", 2)), (5, ("ob", 2))]
        for n, (j, last) in enumerate(REC_ORDER):
            add_load(("rec", j), n % 4, cols(A["rec_w_in"][0], j), last)
        for j in range(2):
            add_load(("ro", j), (2 + j) % 4, cols(A["rec_w_out"][0], j), ("ro", 4 * j + 3))

        def add_moe(l):
            order.append(("moe", l, [slot_uses[s] for s in range(RING)]))
            for s in range(RING):
                slot_uses[s] += NE // 2

        moe_base = {}
        for j in range(12):
            add_load(("ada", 1, j), j % (2 if j < 4 else 4), cols(A["ada_w"][1], j), ("adam", 1, j))
        moe_base[0] = list(slot_uses)
        add_moe(0)
        HIN_SLOT = (3, 4, 1, 2, 3, 4)
        for j in range(6):
            if j == 3:
                add_load("w3", 0, A["hy_f_w3"][0], ("filt", 1, 1, NT - 1, 1))
            add_load(("hin", j), HIN_SLOT[j], cols(A["hy_w_in"][0], j), ("z", 4 * j + 3))
        ahead = {0: order[-7:-5], 1: []}
        del order[-7:-5]
        for j in range(2):
            add_load(("ho", j), 1 + j, cols(A["hy_w_out"][0], j), ("ho", 4 * j + 3))
        moe_base[1] = list(slot_uses)
        add_moe(1)

        def loaded(eng, key):
            slot, use, _ = loads[key]
            eng.wait_ge(S(f"slot{slot}_loaded"), 16 * use)
            return ring[:, slot, :]

        def moe_src(l, kind, e):
            if kind < 2:
                w = (A["moe_w_gate"], A["moe_w_up"])[kind]
                return w[l, e].rearrange("(k p) n -> p k n", p=P)
            return A["moe_w_down"][l, e].rearrange("(k p) n -> p k n", p=P)

        adar = work[0:2, 18800:18800 + 512]
        a = Arena()
        x_in = a.get(NT * D).rearrange("p (j d) -> p j d", j=NT)
        pos_in = a.get(2 * D).rearrange("p (j d) -> p j d", j=2)
        vrows = a.get(3 * P).rearrange("p (a b) -> p a b", a=3)
        a = Arena()
        sq = a.get(DC * T).rearrange("p (k t) -> p k t", k=DC)
        a.at = 0
        B_ = a.get(4 * T).rearrange("p (m t) -> p m t", m=4)
        gt = a.get(4 * T).rearrange("p (m t) -> p m t", m=4)
        mix_tok = a.get(NT * D).rearrange("p (j d) -> p j d", j=NT)
        qka = a.get(4 * T).rearrange("p (m t) -> p m t", m=4)
        qkb = a.get(4 * T).rearrange("p (m t) -> p m t", m=4)
        va = a.get(NT * H * DV).rearrange("p (j n) -> p j n", j=NT)
        vb = a.get(NT * H * (DV + 1)).rearrange("p (j h n) -> p j h n", j=NT, h=H)
        gkT = a.get(T, parts=32)
        trec = a.get(10 * P)
        mneg = [trec[:, 0:512], trec[:, 512:1024]]
        amask = [trec[:, 1024:1152].bitcast(U32), trec[:, 1152:1280].bitcast(U32)]
        wg = trec.rearrange("p (k n) -> p k n", k=DC)
        gkw = a.get(512, parts=32)
        gnw = a.get(2 * DV)
        S0 = a.get(2 * 2 * DV).rearrange("p (d k v) -> p d k v", d=2, k=2)
        C0 = a.get(2 * 2 * (DV + 1)).rearrange("p (d k v) -> p d k v", d=2, k=2)
        refs = a.get(4 * NT).rearrange("p (m j) -> p m j", m=4)
        fcol = a.get(4 * 3).rearrange("p (m c) -> p m c", m=4)
        fexp = a.get(4 * 3).rearrange("p (m c) -> p m c", m=4)
        m0b = a.get(8)
        mcol = a.get(4)
        atok = a.get(NT * 36).rearrange("p (j c) -> p j c", j=NT)
        emt = a.get(NT * 36).rearrange("p (j c) -> p j c", j=NT)
        dn = a.get(8)
        rms = a.get(3 * NT * 8).rearrange("p (a j c) -> p a j c", a=3, j=NT)
        g36 = a.get(7 * T, parts=36).rearrange("p (a t) -> p a t", a=7)
        Dq = gt
        eq = a.get(4 * T, high=True).rearrange("p (m t) -> p m t", m=4)
        ek = a.get(4 * T, high=True).rearrange("p (m t) -> p m t", m=4)
        A_sb = a.get(2 * NT * 512, high=True).rearrange("p (d j n) -> p d j n", d=2, j=NT)
        ke_s = a.get(4 * 2 * P, high=True).rearrange("p (q n) -> p q n", q=8)
        S1 = a.get(2 * 2 * DV, high=True).rearrange("p (d k v) -> p d k v", d=2, k=2)
        S3 = a.get(2 * 2 * DV, high=True).rearrange("p (d k v) -> p d k v", d=2, k=2)
        hm_ = Arena()
        Wm = hm_.get(8 * 512, high=True).rearrange("p (c n) -> p c n", c=8)
        Cout = hm_.get(2 * 2 * (DV + 1), high=True).rearrange("p (d n) -> p d n", d=2)
        qin = hm_.get(2 * 2 * LS, high=True).rearrange("p (d k t) -> p d k t", d=2, k=2)
        kbt = hm_.get(2 * P, high=True).rearrange("p (a n) -> p a n", a=2)
        kw = hm_.get(8 * DK, high=True).rearrange("p (c n) -> p c n", c=8)
        hs = gt.rearrange("p m t -> p (m t)").rearrange("p (j n) -> p j n", j=NT)
        osq = B_.rearrange("p m t -> p (m t)").rearrange("p (j n) -> p j n", j=NT)
        a = Arena()
        msq = a.get(DC * T).rearrange("p (k t) -> p k t", k=DC)
        a.at = 0
        pall = a.get(NT * NE * P).rearrange("p (j e s) -> p j e s", j=NT, e=NE)
        utok = a.get(NT * D).rearrange("p (j d) -> p j d", j=NT)
        lg = a.get(NT * 20).rearrange("p (j c) -> p j c", j=NT)
        R4 = [a.get(NT * 4).rearrange("p (j c) -> p j c", j=NT) for _ in range(12)]
        R1 = [a.get(NT) for _ in range(10)]
        R5 = [a.get(NT * 5).rearrange("p (j c) -> p j c", j=NT) for _ in range(2)]
        R16 = [a.get(NT * 16).rearrange("p (j c) -> p j c", j=NT) for _ in range(8)]
        gid = a.get(NT * NE * 2).rearrange("p (j e c) -> p j e c", j=NT, e=NE)
        idxf = a.get(NE * 2).rearrange("p (e c) -> p e c", e=NE)
        idxu = a.get(NE).bitcast(U32)
        gslot = a.get(NE)
        ridx = a.get(NT * 2).bitcast(U32).rearrange("p (j c) -> p j c", j=NT)
        cmax = a.get(2)
        oidx = a.get(NE).bitcast(U32)
        ogate = a.get(NE)
        gcol = a.get(2)
        logitT = a.get(T, parts=NG + NE)
        idxT = a.get(NE * P, parts=2)
        ug = a.get(2 * D).rearrange("p (u d) -> p u d", u=2)
        b = Arena()
        xg = b.get(2 * D).rearrange("p (u k s) -> p u k s", u=2, k=DC)
        sg = b.get(2 * DE).rearrange("p (u n) -> p u n", u=2)
        assert b.at <= NT * NE * P
        b = Arena()
        b.at = 2 * D + 2 * DE
        hh = b.get(DE)
        hT = b.get(DE)
        ysb = utok.rearrange("p j d -> p (j d)")[:, 0:2 * D].rearrange("p (u d) -> p u d", u=2)
        assert b.at <= NT * NE * P
        x_out = utok
        cmb = work[:, 0:2 * NT * D].rearrange("p (c j d) -> p c j d", c=2, j=NT)
        a = Arena()
        hsq = work[:, WORK - DC * T:].rearrange("p (k t) -> p k t", k=DC)
        v_tok = a.get(NT * D).rearrange("p (j d) -> p j d", j=NT)
        x1_tok = a.get(NT * D).rearrange("p (j d) -> p j d", j=NT)
        x2T = a.get(DC * T).rearrange("p (k t) -> p k t", k=DC)
        thy = a.get(3328)
        Yf = a.get(6 * 512).rearrange("p (q n) -> p q n", q=6)
        dcy = a.get(NT * 512).rearrange("p (j n) -> p j n", j=NT)
        embT = a.get(T, parts=33)
        h1T = a.get(T, parts=64)
        h2T = a.get(T, parts=65)
        fprm = a.get(4, parts=64)
        hw1 = a.get(64, parts=33)
        hw2 = a.get(64, parts=64)
        zall = a.get(2 * T)
        zc = zall.rearrange("p (u t) -> p u t", u=2)
        htmp2 = Yf.rearrange("p q n -> p (q n)")[:, 0:2 * T]
        srt = htmp2[0:64, :].rearrange("p (u t) -> p u t", u=2)
        htmp = zall[:, 0:512]
        Kf = a.get(8 * 512, high=True).rearrange("p (q n) -> p q n", q=8)
        hpm = a.get(6 * 512, high=True).rearrange("p (j s n) -> p j s n", j=NT, s=2)
        ptmp = hpm.rearrange("p j s n -> p (j s) n")

        def col(i):
            return vecT[:, i:i + 1]

        def mod(l, part, m, v):
            return ada[:, l, part * DC + m, v:v + 1]

        def bc(ap, shape):
            return ap.to_broadcast(shape)

        def x_ready(eng, name, m):
            if name in ("moe0", "moe1"):
                evacuated(eng, ("ro" if name == "moe0" else "ho", m))
            else:
                for j in range(NT):
                    key = ("x", j) if name == "rec" else ("yT", 0 if name == "hy" else 1, j)
                    evacuated(eng, key + (m // 4,))

        def u_ready(eng, name, m):
            eng.wait_ge(S("u_chunks"), MODS.index(name) * DC + m + 1)

        def add_shift(eng, name, m):
            l, part = MODV[name]
            eng.wait_ge(S("xn"), MODS.index(name) * DC + m + 1)
            for q, (a0, a1) in enumerate(SEQS):
                out, src, b_ = uT[:, m, a0:a1], squares[name][:, m, a0:a1], mod(l, part, m, q)
                ins = eng.activation(out, src, ACT.Identity, bias=b_)
            ins.then_inc(S("u_chunks"), 1)

        def evacuated(eng, key, it=0):
            b, use, per = jobs[key]
            eng.wait_ge(bank_free[b], it * per + use)

        REC_SMALL = 2 + 6 + 3 + 12
        OVF = NT - 1
        squares = {"rec": sq, "moe0": msq, "hy": hsq, "moe1": msq, "fin": hsq}
        MODV = {"rec": (0, 0), "moe0": (0, 3), "hy": (1, 0), "moe1": (1, 3)}
        NVEC = {"rec": V_N1, "moe0": V_N2, "hy": V_N1 + DC, "moe1": V_N2 + DC, "fin": V_NF}
        block = ctx.enter_context(nc.Block())

        @block.sync
        def _(sp):
            slot_last = [None] * RING
            last_expert = NE // 2 - 1

            def load(item):
                _, slot, src, last, _ = item
                if isinstance(slot_last[slot], int):
                    full(sp, (slot_last[slot], slot // 3, ("G", "U")[slot % 3]), last_expert)
                elif slot_last[slot] is not None:
                    full(sp, slot_last[slot])
                if src.shape[0] == P:
                    dst = ring[:, slot, :].rearrange("p (k n) -> p k n", k=src.shape[1])
                else:
                    dst = ring[0:src.shape[0], slot, :]
                sp.dma_start(dst, src).then_inc(S(f"slot{slot}_loaded"), 16)
                slot_last[slot] = last

            def moe_loads(l):
                def load_part(kind, e, it, u):
                    k = 8 if kind < 2 else 4
                    sp.dma_start(ring[:, 3 * u + kind, :].rearrange("p (k n) -> p k n", k=k),
                                 moe_src(l, kind, e)).then_inc(S(f"slot{3 * u + kind}_loaded"), 16)

                def store(it, u):
                    evacuated(sp, (l, u, "Y", 0), it)
                    evacuated(sp, (l, u, "Y", 1), it)
                    sp.dma_start(y_dram.rearrange("(e s) d -> e s d", s=P)[2 * it + u],
                                 ysb[:, u, :]).then_inc(S(f"y{u}_stored"), 16)

                def step(it, u):
                    full(sp, (l, u, "G"), it)
                    load_part(0, 2 * it + 2 + u, it + 1, u)
                    full(sp, (l, u, "U"), it)
                    load_part(1, 2 * it + 2 + u, it + 1, u)
                    down(it, u)

                def down(it, u):
                    e = 2 * it + u
                    if isinstance(it, int) and e == 0:
                        load_part(2, 1, 0, 1)
                        return
                    before = it - 1 if u == 0 else it
                    full(sp, (l, 1 - u, "Y", 1), before)
                    load_part(2, e + 1, it if u == 0 else it + 1, 1 - u)
                    store(before, 1 - u)

                if l == 0:
                    sp.wait_ge(S("states_stored"), 16 * 14)
                full(sp, ("ro" if l == 0 else "ho", DC - 1))
                for u in range(2):
                    for kind in range(3):
                        slot = 3 * u + kind
                        if slot_last[slot] is not None:
                            full(sp, slot_last[slot])
                            slot_last[slot] = None
                        if slot < 5:
                            load_part(kind, u, 0, u)
                step(0, 0)
                step(0, 1)
                with sp.Fori(1, NE // 2 - 1) as it:
                    step(it, 0)
                    step(it, 1)
                down(NE // 2 - 1, 0)
                for slot in (0, 1, 3, 4):
                    slot_last[slot] = l
                for item in ahead[l]:
                    load(item)
                store(NE // 2 - 1, 0)
                store(NE // 2 - 1, 1)
                overflow_sp(l)
                for j in range(NT):
                    sp.wait_ge(S(f"token_rows_{j}"), 32 * (l + 1))

            def overflow_sp(l):
                sp.wait_ge(S("overflow_flag"), l + 1)
                over = sp.value_load(flag[0:1, 0:1], min_val=0, max_val=T)
                with sp.If(over > P):
                    sp.nop().then_inc(S(f"over{l}_y_stored"), 16)
                    for c in range(1, NT):
                        with sp.Fori(0, NE) as e:
                            n = e + NE * (c - 1)
                            sp.wait_ge(S(f"over{l}_y_stored"), 16 * n + 16)
                            for kind in range(3):
                                k = 8 if kind < 2 else 4
                                sp.dma_start(ring[:, kind, :].rearrange("p (k n) -> p k n", k=k),
                                             moe_src(l, kind, e)).then_inc(S(f"over{l}_loaded"), 16)
                            sp.wait_ge(S(f"over{l}_y"), n + 1)
                            sp.dma_start(y_dram.rearrange("(e s) d -> e s d", s=P)[e + c * NE],
                                         ysb[:, 0, :]).then_inc(S(f"over{l}_y_stored"), 16)
                    sp.wait_ge(S(f"over{l}_y_stored"), 16 * NE * OVF + 16)
                with sp.Else():
                    sp.nop()
                sp.nop()

            for item in order:
                if item[0] == "load":
                    load(item)
                else:
                    moe_loads(item[1])
            for j in range(NT):
                for hf in range(2):
                    evacuated(sp, ("out", j, hf))
                dst = O[0][0] if j == 0 else O[1][0, (j - 1) * P:j * P, :]
                sp.dma_start(dst, x_out[:, j, :]).then_inc(S("y_out_stored"), 16)
            sp.wait_ge(S("y_out_stored"), 16 * NT)

        @block.gpsimd
        def _(pool):
            def clear(ap, name):
                pool.memset(ap, 0.0).then_inc(S(name), 1)

            clear(wg, "wg_cleared")
            clear(gkw, "gkw_cleared")
            clear(g36, "g36_cleared")
            clear(mcol, "mcol_cleared")
            pool.memset(vb[:, :, :, DV:DV + 1], 1.0).then_inc(S("vb_ones"), 1)
            pool.wait_ge(S("wg_cleared"), 1)
            w_in = A["rec_w_in"][0].rearrange("(k p) n -> p k n", p=P)
            base = w_in.shape[2] - 16
            pool.dma_start(wg[:, :, 0:32], w_in[:, :, base - 32:base]).then_inc(S("wg_loaded"), 16)
            for q in range(4):
                typ, d = q // 2, q % 2
                pool.dma_start(wg[:, :, 32 + 32 * q:36 + 32 * q],
                               w_in[:, :, base + 8 * d + 4 * typ:base + 8 * d + 4 * typ + 4]).then_inc(S("wg_loaded"), 16)
            pool.wait_ge(S("gkw_cleared"), 1)
            for d in range(2):
                pool.dma_start(gkw[16 * d:16 * d + 16, 256 * d:256 * d + 256], A["gla_gk_w"][0, d]).then_inc(S("rec_small_loaded"), 16)
            pool.wait_ge(S("mcol_cleared"), 1)
            for d in range(2):
                for typ in range(2):
                    pool.dma_start(mcol[32 * d:32 * d + 4, typ:typ + 1],
                                   A["mlstm_gate_b"][0, d, typ].rearrange("(h o) -> h o", o=1)).then_inc(S("rec_small_loaded"), 16)
                pool.dma_start(mcol[32 * d:32 * d + 4, 2:3],
                               A["state_mlstm_m"][0, 0, d].rearrange("(h o) -> h o", o=1)).then_inc(S("rec_small_loaded"), 16)
            pool.dma_start(m0b, A["state_mlstm_m"][0, 0].rearrange("d h -> (d h)").partition_broadcast(P)).then_inc(S("rec_small_loaded"), 16)
            pool.dma_start(gnw[:, 0:DV], A["gla_norm_w"][0].partition_broadcast(P)).then_inc(S("rec_small_loaded"), 16)
            pool.dma_start(gnw[:, DV:], A["mlstm_norm_w"][0].partition_broadcast(P)).then_inc(S("rec_small_loaded"), 16)
            for d in range(2):
                for kc in range(2):
                    pool.dma_start(S0[:, d, kc, :], A["state_gla"][0, 0, d, 2 * kc:2 * kc + 2].rearrange("h k v -> (h k) v")).then_inc(S("rec_small_loaded"), 16)
                    pool.dma_start(C0[:, d, kc, 0:DV], A["state_mlstm_c"][0, 0, d, 2 * kc:2 * kc + 2].rearrange("h k v -> (h k) v")).then_inc(S("rec_small_loaded"), 16)
                    pool.dma_start(C0[:, d, kc, DV:], A["state_mlstm_n"][0, 0, d, 2 * kc:2 * kc + 2].rearrange("h (k o) -> (h k) o", o=1)).then_inc(S("rec_small_loaded"), 16)
            for l in range(2):
                pool.dma_start(wr[:, :, l, 0:NG], A["moe_w_group"][l].rearrange("(k p) n -> p k n", p=P)).then_inc(S("router_loaded"), 16)
                pool.dma_start(wr[:, :, l, NG:], A["moe_w_router"][l].rearrange("(k p) n -> p k n", p=P)).then_inc(S("router_loaded"), 16)
                pool.dma_start(b20[:, l, 0:NG], A["moe_b_group"][l].partition_broadcast(P)).then_inc(S("router_loaded"), 16)
                pool.dma_start(b20[:, l, NG:], A["moe_b_router"][l].partition_broadcast(P)).then_inc(S("router_loaded"), 16)
            full(pool, ("adam", 0, 11))
            clear(A_sb, "A_cleared")
            evacuated(pool, ("ada", 0))
            full(pool, "mg")
            pool.dma_start(trec, A["t_rec"]).then_inc(S("rec_tables_loaded"), 16)

            pool.wait_ge(S("gla_exp"), 2)
            evacuated(pool, ("qka", 3))
            for d in range(2):
                pool.tensor_tensor(ek[:, 2 * d:2 * d + 2, :], ek[:, 2 * d:2 * d + 2, :], qka[:, 2:4, :],
                                   ALU.mult).then_inc(S("ke"), 1)
            for d in range(2):
                evacuated(pool, ("kv", d, 0))
                for kc in range(2):
                    pool.dma_start(O[2][0, 0, d, 2 * kc:2 * kc + 2].rearrange("h k v -> (h k) v"), S1[:, d, kc, :]).then_inc(S("states_stored"), 16)
            pool.wait_ge(S("qin_exp"), 8)
            evacuated(pool, ("qkb", 1))
            for d in range(2):
                pool.tensor_tensor(qin[:, d, :, :], qin[:, d, :, :], qkb[:, 0:2, P:T], ALU.mult).then_inc(S("qin"), 1)
            for d in range(2):
                evacuated(pool, ("C", d))
                for kc in range(2):
                    pool.dma_start(O[3][0, 0, d, 2 * kc:2 * kc + 2].rearrange("h k v -> (h k) v"), Cout[:, d, kc * 129:kc * 129 + DV]).then_inc(S("states_stored"), 16)
                    pool.dma_start(O[4][0, 0, d, 2 * kc:2 * kc + 2].rearrange("h (k o) -> (h k) o", o=1), Cout[:, d, kc * 129 + DV:kc * 129 + DV + 1]).then_inc(S("states_stored"), 16)
                at = (LP - 1, 0)[d]
                pool.wait_ge(S("m_rows"), 1)
                pool.dma_start(O[5][0, 0, d].rearrange("(h o) -> h o", o=1), g36[32 * d:32 * d + 4, 2, at:at + 1]).then_inc(S("states_stored"), 16)
            pool.wait_ge(S("states_stored"), 16 * 14)

            def moe(l):
                for j in range(NT):
                    for hf in range(2):
                        evacuated(pool, ("ut", l, j, hf))
                    pool.dma_start(u_dram[j * P:(j + 1) * P, :], utok[:, j, :]).then_inc(S("u_rows_stored"), 16)
                pool.wait_ge(S("u_rows_stored"), 16 * NT * (l + 1))
                evacuated(pool, ("idx0", l))
                for e in range(NE):
                    if e == 2:
                        evacuated(pool, ("idx", l))
                    it, u = e // 2, e % 2
                    if e >= 2:
                        full(pool, (l, u, "X", 1), it - 1)
                    pool.indirect_dma_start(ug[:, u, :], None, u_dram,
                                            bass.IndirectOffsetOnAxis(ap=idxu[:, e:e + 1], axis=0)).then_inc(S(f"rows{u}_gathered"), 16)
                def token_rows(written):
                    for u in range(2):
                        pool.wait_ge(S(f"y{u}_stored"), 16 * (NE // 2) * (l + 1))
                    full(pool, (l, 1, "Y", 1), NE // 2 - 1)
                    for j in range(NT):
                        for q in range(2):
                            pool.indirect_dma_start(cmb[:, q, j, :], None, written,
                                                    bass.IndirectOffsetOnAxis(ap=ridx[:, j, q:q + 1], axis=0)).then_inc(S(f"token_rows_{j}"), 16)

                pool.wait_ge(S("overflow_flag"), l + 1)
                over = pool.value_load(flag[0:1, 0:1], min_val=0, max_val=T)
                with pool.If(over > P):
                    for c in range(1, NT):
                        pool.wait_ge(S(f"over{l}_idx"), c)
                        for e in range(NE):
                            n = e + NE * (c - 1)
                            if n:
                                pool.wait_ge(S(f"over{l}_y"), n)
                            pool.indirect_dma_start(ug[:, 0, :], None, u_dram,
                                                    bass.IndirectOffsetOnAxis(ap=oidx[:, e:e + 1], axis=0)).then_inc(S(f"over{l}_rows"), 16)
                    pool.wait_ge(S(f"over{l}_y_stored"), 16 * NE * OVF + 16)
                    token_rows(y_dram)
                with pool.Else():
                    token_rows(y_dram[0:NE * P, :])
                pool.nop()

            moe(0)
            for m in range(DC):
                u_ready(pool, "hy", m)
            for dst, src in (
                (embT, A["t_emb"]), (hw1, A["hy_f_w1"][0]), (hw2, A["hy_f_w2"][0]),
                (fprm[:, 0:1], A["hy_f_b1"].rearrange("o (n c) -> (o n) c", c=1)),
                (fprm[:, 1:2], A["hy_f_freq1"].rearrange("o (n c) -> (o n) c", c=1)),
                (fprm[:, 2:3], A["hy_f_b2"].rearrange("o (n c) -> (o n) c", c=1)),
                (fprm[:, 3:4], A["hy_f_freq2"].rearrange("o (n c) -> (o n) c", c=1)),
            ):
                pool.dma_start(dst, src).then_inc(S("hy_small_loaded"), 16)
            pool.dma_start(thy, A["t_hy"]).then_inc(S("dft_loaded"), 16)
            pool.memset(h2T[64:65, :], 0.0).then_inc(S("h2_row"), 1)
            pool.wait_ge(S("h2_row"), 1)
            for a0, _ in SEQS:
                pool.memset(h2T[64:65, a0:a0 + 1], 1.0).then_inc(S("h2_row"), 1)
            full(pool, (0, 0, "G"), NE // 2 - 1)
            pool.memset(ring[64:65, 0, :], 0.0).then_inc(S("w3_row_cleared"), 1)
            pool.wait_ge(S("w3_row_cleared"), 1)
            for od in range(2):
                pool.dma_start(ring[64:65, 0, 2 * od * D:(2 * od + 1) * D], A["hy_f_bias"][0, od:od + 1, :]).then_inc(S("w3_row_loaded"), 16)
            for c in range(2):
                for od in range(2):
                    if c == 0:
                        if od == 1:
                            evacuated(pool, ("filt", 0, 1, NT - 1, 1))
                            pool.wait_ge(S("filters"), 2 * NT)
                        pool.dma_start(dcy, A["t_decay"].rearrange("(j p) n -> p j n", p=P)[:, :, od * 512:(od + 1) * 512]).then_inc(S("decay_loaded"), 16)
                    for pr in range(3):
                        n = (c * 2 + od) * 3 + pr
                        pool.wait_ge(S("products"), n + 1)
                        pool.tensor_tensor(Yf[:, 2 * pr, :], Yf[:, 2 * pr, :], ptmp[:, 2 * pr, :], ALU.subtract).then_inc(S("spectrum"), 1)
                        pool.tensor_tensor(Yf[:, 2 * pr + 1, :], Yf[:, 2 * pr + 1, :], ptmp[:, 2 * pr + 1, :], ALU.add).then_inc(S("spectrum"), 1)
            moe(1)

        @block.scalar
        def _(act):
            nchain = [0]

            def chain(ins):
                nchain[0] += 1
                ins.then_inc(S("act_chain"), 1)
                act.wait_ge(S("act_chain"), nchain[0])

            for dst, src in (
                (vrows[0:8, 0, :], A["c_ctx"].rearrange("(a b) -> a b", b=P)),
                (vrows[8:16, 0, :], A["c"].rearrange("o (a b) -> (o a) b", b=P)),
                (vrows[16:32, 0, :], A["norm1_w"].rearrange("l (a b) -> (l a) b", b=P)),
                (vrows[32:48, 0, :], A["norm2_w"].rearrange("l (a b) -> (l a) b", b=P)),
                (vrows[48:56, 0, :], A["norm_f_w"].rearrange("(a b) -> a b", b=P)),
                (vrows[56:60, 0, :], A["gla_gk_b"].rearrange("o d (a b) -> (o d a) b", b=P)),
                (vrows[0:96, 1, :], A["ada_b"].rearrange("l (a b) -> (l a) b", b=P)),
                (vrows[0:72, 2, :], A["hy_conv_w"].rearrange("o t (a b) -> (o t a) b", b=P)),
            ):
                act.dma_start(dst, src).then_inc(S("vec_rows_loaded"), 16)
            act.dma_start(tc_[:], A["t_common"]).then_inc(S("tables_loaded"), 16)
            act.dma_start(x_in[:, 0, :], A["x_prompt"][0]).then_inc(S("x_loaded"), 16)
            act.dma_start(x_in[:, 1:3, :], A["x_sample"][0].rearrange("(j p) d -> p j d", p=P)).then_inc(S("x_loaded"), 16)
            act.dma_start(pos_in, A["t_pos"].rearrange("(j p) d -> p j d", p=P)).then_inc(S("x_loaded"), 16)
            evacuated(act, "vec")
            act.activation(silc[:].rearrange("p k v -> p v k"), vecT[:, 0:2 * DC].rearrange("p (v k) -> p v k", v=2),
                           ACT.Silu).then_inc(S("silu_c"), 1)
            def ada_rows(l, first, last):
                for j in range(first, last):
                    full(act, ("adam", l, j))
                    if l == 1 and j:
                        full(act, ("adac", j - 1))
                    elif l or j:
                        act.wait_ge(S("ada_rows_read"), 12 * l + j)
                    free(act.copy(adar, bank(("adam", l, j))[0:2, :]), ("adam", l, j))

            def ada_columns(j):
                full(act, ("adac", j))
                free(act.copy(ada[:, 1, 4 * j:4 * j + 4, :], bank(("adac", j))[:, 0:8].rearrange("p (m v) -> p m v", v=2)), ("adac", j))

            def ada_step(j):
                if j:
                    ada_columns(j - 1)
                ada_rows(1, j, j + 1)
                if j == 11:
                    ada_columns(11)

            ada_rows(0, 0, 6)
            for j in range(NT):
                full(act, ("x", j, 0))
                free(act.copy(xT[:, 0:4, j * P:(j + 1) * P], bank(("x", j, 0))[:].rearrange("p (n t) -> p n t", n=4)), ("x", j, 0))

            def square(name):
                for m in range(DC):
                    x_ready(act, name, m)
                    act.activation(squares[name][:, m, :], xT[:, m, :], ACT.Square).then_inc(S("squares"), 1)

            def root(name):
                full(act, ("ss", name))
                act.wait_ge(S("eps_set"), 1)
                free(act.activation(rstd[:], bank(("ss", name))[:, 0:T], ACT.Sqrt, bias=eps[:, 0:1], scale=1.0 / D), ("ss", name))

            def modulate(name):
                root(name)
                for m in range(DC):
                    add_shift(act, name, m)

            square("rec")
            root("rec")
            ada_rows(0, 6, 12)
            evacuated(act, ("ada", 0))
            for m in range(DC):
                add_shift(act, "rec", m)
            for m in range(2):
                full(act, ("qka", m))
                free(act.activation(qka[:, m, :], bank(("qka", m))[:, 0:T], ACT.Copy, scale=DK ** -0.5), ("qka", m))
            for m in range(2):
                full(act, ("qkb", m))
                free(act.activation(qkb[:, m, :], bank(("qkb", m))[:, 0:T], ACT.Copy, scale=DK ** -0.5), ("qkb", m))
            for m in range(4):
                full(act, ("glog", m))
                act.activation(gt[:, m, :], bank(("glog", m))[:, 0:T], ACT.Abs, bias=col(V_GKB + m)).then_inc(S("glog_abs"), 1)
            act.wait_ge(S("mlstm_f"), 1)
            act.wait_ge(S("rec_small_loaded"), 16 * REC_SMALL)
            act.activation(g36[:, 2, :], g36[:, 1, :], ACT.Abs, bias=mcol[0:36, 1:2]).then_inc(S("f_abs"), 1)
            act.wait_ge(S("glog_abs"), 4)
            chain(act.activation(gt, gt, ACT.Exp, scale=-1.0))
            act.activation(gt, gt, ACT.Ln, bias=ones[:, 0:1]).then_inc(S("gla_ln"), 1)
            act.wait_ge(S("f_abs"), 1)
            chain(act.activation(g36[:, 2, :], g36[:, 2, :], ACT.Exp, scale=-1.0))
            act.activation(g36[:, 2, :], g36[:, 2, :], ACT.Ln, bias=ones[0:36, 0:1]).then_inc(S("mlstm_ln"), 1)
            act.wait_ge(S("gla_diff"), 1)
            act.activation(eq, gt, ACT.Exp, scale=1.0 / 16).then_inc(S("gla_exp"), 1)
            act.activation(ek, gt, ACT.Exp, scale=-1.0 / 16).then_inc(S("gla_exp"), 1)
            act.activation(fexp, fcol, ACT.Exp, scale=1.0 / 16).then_inc(S("gla_fexp"), 1)
            for j in range(NT):
                full(act, ("ra", j))
                free(act.activation(mix_tok[:, j, 0:512], bank(("ra", j))[:], ACT.Silu), ("ra", j))
            for j in range(NT):
                full(act, ("ob", j))
                free(act.activation(mix_tok[:, j, 512:], bank(("ob", j))[:], ACT.Sigmoid), ("ob", j))
            for k in range(4):
                full(act, ("keT", k))
                free(act.copy(ke_s[:, 2 * k:2 * k + 2, :], bank(("keT", k))[:, 0:2 * P].rearrange("p (a n) -> p a n", a=2)), ("keT", k))
            act.wait_ge(S("gla_fexp"), 1)
            for d in range(2):
                full(act, ("kv", d, 0))
                for kc in range(2):
                    ins = act.activation(S1[:, d, kc, :], bank(("kv", d, 0))[:, kc * DV:(kc + 1) * DV], ACT.Copy,
                                         scale=fexp[:, 2 * d + kc, 2:3])
                free(ins, ("kv", d, 0))
            for j in range(NT):
                full(act, ("oa", j))
                act.activation(osq[:, j, :], bank(("oa", j))[:], ACT.Square).then_inc(S("gla_squares"), 1)
            full(act, "mtok")
            act.copy(atok, bank("mtok")[:, 0:108].rearrange("p (j c) -> p j c", j=NT)).then_inc(S("atok"), 1)
            free(act.activation(emt, bank("mtok")[:, 108:216].rearrange("p (j c) -> p j c", j=NT), ACT.Exp), "mtok")
            for j in range(NT):
                full(act, ("oa", j))
            full(act, "kbt")
            free(act.copy(kbt, bank("kbt")[:, 0:2 * P].rearrange("p (a n) -> p a n", a=2)), "kbt")
            for h in range(H):
                kc, r0 = h // 2, (h % 2) * DK
                for d in range(2):
                    c = 4 * d + h
                    full(act, ("nM", d, h))
                    act.activation(qin[r0:r0 + DK, d, kc, :], bank(("nM", d, h))[r0:r0 + DK, P:T], ACT.Exp,
                                   bias=m0b[r0:r0 + DK, c:c + 1]).then_inc(S("qin_exp"), 1)
                    evacuated(act, ("nM", d, h))
                    act.activation(Wm[:, c, :], Wm[:, c, :], ACT.Exp).then_inc(S("weights"), 1)
            for d in range(2):
                full(act, ("C", d))
                free(act.copy(Cout[:, d, :], bank(("C", d))[:, 0:258]), ("C", d))
            n = 0
            for j in range(NT):
                for d in range(2):
                    for hp in range(2):
                        key = ("num", j, d, hp)
                        full(act, key)
                        if n >= 4:
                            act.wait_ge(S("den_read"), n - 3)
                        act.activation(dn[:, 2 * (n % 4):2 * (n % 4) + 2], bank(key)[:, DV:258:129], ACT.Abs).then_inc(S("den_abs"), 1)
                        n += 1
                act.wait_ge(S("h_sum"), 2 * (j + 1))
                act.wait_ge(S("gla_sums"), j + 1)
                act.activation(osq[:, j, :], hs[:, j, :], ACT.Square).then_inc(S("h_squares"), 1)
                act.wait_ge(S("sums"), j + 1)
                act.activation(rms[:, 1, j, :], rms[:, 0, j, :], ACT.Sqrt, bias=eps[:, 0:1], scale=1.0 / DV).then_inc(S("head_rms"), 1)
                ada_step(j)
            for j in range(NT):
                for hf in range(2):
                    full(act, ("mixT", j, hf))
                    free(act.copy(uT[:, 4 * hf:4 * hf + 4, j * P:(j + 1) * P], bank(("mixT", j, hf))[:].rearrange("p (n t) -> p n t", n=4)), ("mixT", j, hf))
                if j == 1:
                    ada_step(3)

            def moe(l):
                square(f"moe{l}")
                modulate(f"moe{l}")
                if l == 0:
                    ada_step(4)
                for j in range(NT):
                    for hf in range(2):
                        full(act, ("ut", l, j, hf))
                        free(act.copy(utok[:, j, hf * 512:(hf + 1) * 512], bank(("ut", l, j, hf))[:]), ("ut", l, j, hf))
                act.wait_ge(S("exp_in"), l + 1)
                act.activation(R5[1], R5[0], ACT.Exp).then_inc(S("exp_out"), 1)
                if l == 0:
                    for j in range(ADA1[0], ADA1[2]):
                        ada_step(j)
                for g in range(4):
                    full(act, ("idxT", l, g))
                    free(act.copy(idxT[:, g * 512:(g + 1) * 512], bank(("idxT", l, g))[0:2, :]), ("idxT", l, g))
                if l == 0:
                    for j in range(ADA1[2], ADA1[3]):
                        ada_step(j)

                def rows_in(it, u):
                    full(act, (l, u, "X", 0), it)
                    free(act.copy(xg[:, u, 0:4, :], bank((l, u, "X", 0))[:].rearrange("p (k s) -> p k s", k=4)), (l, u, "X", 0))

                def silu(it, u):
                    full(act, (l, u, "G"), it)
                    free(act.activation(sg[:, u, :], bank((l, u, "G"))[:], ACT.Silu), (l, u, "G"))

                def rows_out(it, u):
                    full(act, (l, u, "Y", 0), it)
                    if not isinstance(it, int) or it + l:
                        act.wait_ge(S(f"y{u}_stored"), it * 16 + l * (NE // 2) * 16)
                    free(act.copy(ysb[:, u, 0:512], bank((l, u, "Y", 0))[:]), (l, u, "Y", 0))

                def two(it):
                    for it_e, u, it_before, it_next in ((it, 1, it, it + 1), (it + 1, 0, it, it + 1)):
                        silu(it_e, u)
                        rows_out(it_before, 1 - u)
                        rows_in(it_next, 1 - u)

                act.wait_ge(S("u_rows_stored"), 16 * NT * (l + 1))
                full(act, ("idx", l))
                rows_in(0, 0)
                silu(0, 0)
                rows_in(0, 1)
                two(0)
                with act.Fori(1, NE // 2 - 1) as it:
                    two(it)
                silu(NE // 2 - 1, 1)
                rows_out(NE // 2 - 1, 0)
                rows_out(NE // 2 - 1, 1)
                act.wait_ge(S("overflow_flag"), l + 1)
                over = act.value_load(flag[0:1, 0:1], min_val=0, max_val=T)
                with act.If(over > P):
                    for c in range(1, NT):
                        with act.Fori(0, NE) as e:
                            n = e + NE * (c - 1)
                            act.wait_ge(S(f"over{l}_x"), n + 1)
                            act.copy(xg[:, 0, 0:4, :], ps[0][:].rearrange("p (k s) -> p k s", k=4)).then_inc(S(f"over{l}_xcopy"), 1)
                            act.wait_ge(S(f"over{l}_gu"), n + 1)
                            act.activation(sg[:, 0, :], ps[2][:], ACT.Silu).then_inc(S(f"over{l}_silu"), 1)
                            act.wait_ge(S(f"over{l}_down"), n + 1)
                            act.copy(ysb[:, 0, 0:512], ps[5][:]).then_inc(S(f"over{l}_ya"), 1)
                    act.wait_ge(S(f"over{l}_y_stored"), 16 * NE * OVF + 16)
                with act.Else():
                    act.nop()
                act.nop()

            moe(0)
            square("hy")
            modulate("hy")
            zdst = [zc[:, m % 2, :] if m < 2 * DC else x2T[:, m - 2 * DC, :] for m in range(3 * DC)]
            for m in range(3 * DC):
                if m in (2, 4):
                    n = m // 2 - 1
                    act.wait_ge(S("sin_in"), n + 1)
                    act.activation((h1T, h2T[0:64])[n], srt[:, 0, :], ACT.Sin).then_inc(S("sin_out"), 1)
                full(act, ("z", m))
                if 2 <= m < 2 * DC:
                    full(act, ("zt", m - 2))
                act.activation(zdst[m], bank(("z", m))[:, 0:T], ACT.Copy, scale=col(V_CONV + 3 * DC + m)).then_inc(S("conv_mid"), 1)
                if 1 <= m <= 2 * DC:
                    q = m - 1
                    full(act, ("zt", q))
                    dst = (v_tok if q < DC else x1_tok)[:, :, (q % DC) * P:(q % DC + 1) * P]
                    free(act.copy(dst, bank(("zt", q))[:, 0:T].rearrange("p (j n) -> p j n", j=NT)), ("zt", q))
            for c in range(2):
                for od in range(2):
                    for q in range(8):
                        full(act, ("K", c, od, q))
                        free(act.copy(Kf[:, q, :], bank(("K", c, od, q))[:]), ("K", c, od, q))
            moe(1)
            square("fin")
            root("fin")
            for j in range(NT):
                full(act, ("out", j, 0))
                free(act.copy(x_out[:, j, 0:512], bank(("out", j, 0))[:]), ("out", j, 0))

        @block.vector
        def _(v):
            nchain = [0]

            def chain(ins):
                nchain[0] += 1
                ins.then_inc(S("dve_chain"), 1)
                v.wait_ge(S("dve_chain"), nchain[0])

            v.memset(ones[:], 1.0).then_inc(S("ones_set"), 1)
            v.memset(eps[:], EPS).then_inc(S("eps_set"), 1)
            full(v, "vec")
            free(v.tensor_copy(vecT[:], bank("vec")[:, 0:V_ALL]), "vec")
            v.wait_ge(S("x_loaded"), 48)
            v.tensor_tensor(x_in[:, 1:3, :], x_in[:, 1:3, :], pos_in, ALU.add).then_inc(S("x_pos"), 1)
            for j in range(NT):
                full(v, ("x", j, 1))
                free(v.tensor_copy(xT[:, 4:8, j * P:(j + 1) * P], bank(("x", j, 1))[:].rearrange("p (n t) -> p n t", n=4)), ("x", j, 1))

            def ada_out(l):
                n = NMOD * DC
                if l == 1:
                    evacuated(v, ("adac", 11))
                    v.tensor_tensor(ada[:, l, :, :], ada[:, l, :, :],
                                    bc(vecT[:, V_ADA + l * n:V_ADA + (l + 1) * n].unsqueeze(2), [P, n, 2]), ALU.add).then_inc(S("ada1_ready"), 1)
                    return
                full(v, ("ada", l))
                free(v.tensor_tensor(ada[:, l, :, :], bank(("ada", l))[:, 0:2 * n].rearrange("p (m v) -> p m v", v=2),
                                     bc(vecT[:, V_ADA + l * n:V_ADA + (l + 1) * n].unsqueeze(2), [P, n, 2]), ALU.add), ("ada", l))

            def modulate(name):
                s = squares[name]
                if name != "fin":
                    l, part = MODV[name]
                    if l == 0:
                        evacuated(v, ("ada", l))
                    else:
                        v.wait_ge(S("ada1_ready"), 1)
                    if name != "rec":
                        v.wait_ge(S("xn"), MODS.index(name) * DC)
                    v.scalar_tensor_tensor(mA[:], ada[:, l, (part + 1) * DC:(part + 2) * DC, :], 1.0,
                                           bc(vecT[:, NVEC[name]:NVEC[name] + DC].unsqueeze(2), [P, DC, 2]),
                                           ALU.add, ALU.mult).then_inc(S("mA_ready"), 1)
                    v.wait_ge(S("mA_ready"), MODS.index(name) + 1)
                evacuated(v, ("ss", name))
                chain(v.reciprocal(rstd[:], rstd[:]))
                for m in range(DC):
                    if name == "fin":
                        v.scalar_tensor_tensor(uT[:, m, :], xT[:, m, :], col(V_NF + m), rstd[:],
                                               ALU.mult, ALU.mult).then_inc(S("fin_u"), 1)
                        continue
                    for q, (a0, a1) in enumerate(SEQS):
                        ins = v.scalar_tensor_tensor(s[:, m, a0:a1], xT[:, m, a0:a1], mA[:, m, q:q + 1], rstd[:, a0:a1],
                                                     ALU.mult, ALU.mult)
                    ins.then_inc(S("xn"), 1)

            def residual(key, m, l, part):
                full(v, key)
                for q, (a0, a1) in enumerate(SEQS):
                    ins = v.scalar_tensor_tensor(xT[:, m, a0:a1], bank(key)[:, a0:a1], mod(l, part, m, q),
                                                 xT[:, m, a0:a1], ALU.mult, ALU.add)
                free(ins, key)

            ada_out(0)
            modulate("rec")
            for m in range(2, 4):
                full(v, ("qka", m))
                free(v.tensor_copy(qka[:, m, :], bank(("qka", m))[:, 0:T]), ("qka", m))
            full(v, "gk")
            v.wait_ge(S("gkw_cleared"), 1)
            free(v.tensor_copy(gkT, bank("gk")[0:32, 0:T]), "gk")
            full(v, "mg")
            v.wait_ge(S("g36_cleared"), 1)
            v.tensor_copy(g36[:, 0, :], bank("mg")[0:36, 0:T])
            v.tensor_copy(g36[:, 1, :], bank("mg")[64:100, 0:T]).then_inc(S("mlstm_f"), 1)
            v.wait_ge(S("mlstm_f"), 1)
            v.wait_ge(S("rec_small_loaded"), 16 * REC_SMALL)
            free(v.tensor_scalar(g36[:, 0, :], g36[:, 0, :], mcol[0:36, 0:1], None, ALU.add), "mg")
            for m in range(2, 4):
                full(v, ("qkb", m))
                free(v.tensor_copy(qkb[:, m, :], bank(("qkb", m))[:, 0:T]), ("qkb", m))
            for m in range(DC):
                u_ready(v, "rec", m)
            for m in range(4):
                full(v, ("glog", m))
                v.wait_ge(S("glog_abs"), m + 1)
                free(v.tensor_scalar(B_[:, m, :], bank(("glog", m))[:, 0:T], col(V_GKB + m), 0.0, ALU.add, ALU.min), ("glog", m))
            v.wait_ge(S("gla_ln"), 1)
            evacuated(v, ("glog", 3))
            chain(v.tensor_tensor(B_, B_, gt, ALU.subtract))
            for m in range(4):
                for a0, a1 in SEQS:
                    src, dst = B_[:, m, a0:a1], gt[:, m, a0:a1]
                    if m >= 2:
                        src, dst = src[:, ::-1], dst[:, ::-1]
                    ins = v.tensor_tensor_scan(dst, bc(ones[:, 0:1], [P, a1 - a0]), src, 0.0, ALU.mult, ALU.add)
            chain(ins)
            v.tensor_copy(refs[:, 0:2, :], gt[:, 0:2, 63::P])
            chain(v.tensor_copy(refs[:, 2:4, :], gt[:, 2:4, 64::P]))
            for d, (first, second, end) in enumerate(((1, 2, LP - 1), (2, 1, 0))):
                r = refs[:, 2 * d:2 * d + 2, :]
                fc = fcol[:, 2 * d:2 * d + 2, :]
                v.tensor_copy(fc[:, :, 0:1], r[:, :, first:first + 1])
                v.tensor_tensor(fc[:, :, 1:2], r[:, :, second:second + 1], r[:, :, first:first + 1], ALU.subtract)
                ins = v.tensor_tensor(fc[:, :, 2:3], gt[:, 2 * d:2 * d + 2, end:end + 1], r[:, :, 0:1], ALU.subtract)
            chain(ins)
            v.tensor_tensor(gt.rearrange("p m (j t) -> p (m j) t", j=NT), gt.rearrange("p m (j t) -> p (m j) t", j=NT),
                            bc(refs.rearrange("p m j -> p (m j)").unsqueeze(2), [P, 4 * NT, P]),
                            ALU.subtract).then_inc(S("gla_diff"), 1)
            for j in range(NT):
                full(v, ("va", j))
                free(v.tensor_copy(va[:, j, :], bank(("va", j))[:]), ("va", j))
            for j in range(NT):
                full(v, ("vb", j))
                free(v.tensor_copy(vb[:, j, :, 0:DV], bank(("vb", j))[:].rearrange("p (h n) -> p h n", h=H)), ("vb", j))
            v.wait_ge(S("mlstm_ln"), 1)
            chain(v.tensor_scalar(g36[:, 1, :], g36[:, 1, :], mcol[0:36, 1:2], 0.0, ALU.add, ALU.min))
            chain(v.tensor_tensor(g36[:, 1, :], g36[:, 1, :], g36[:, 2, :], ALU.subtract))

            def scans(src, dst, op, init):
                for d in range(2):
                    for q, (a0, a1) in enumerate(SEQS):
                        r = slice(32 * d, 32 * d + 4)
                        s_, d_ = g36[r, src, a0:a1], g36[r, dst, a0:a1]
                        if d:
                            s_, d_ = s_[:, ::-1], d_[:, ::-1]
                        ins = v.tensor_tensor_scan(d_, bc(ones[r, 0:1], [4, a1 - a0]), s_, init(r, q), ALU.mult, op)
                chain(ins)

            scans(1, 3, ALU.add, lambda r, q: 0.0)
            chain(v.tensor_tensor(g36[:, 4, :], g36[:, 0, :], g36[:, 3, :], ALU.subtract))
            scans(4, 5, ALU.max, lambda r, q: 0.0 if q == 0 else mcol[r, 2:3])
            chain(v.tensor_scalar(g36[:, 5, :], g36[:, 5, :], -1.0, None, ALU.mult))
            v.tensor_tensor(g36[:, 2, :], g36[:, 3, :], g36[:, 5, :], ALU.subtract)
            v.tensor_tensor(g36[:, 6, :], g36[:, 5, :], g36[:, 3, :], ALU.subtract).then_inc(S("m_rows"), 1)
            v.wait_ge(S("gla_exp"), 1)
            evacuated(v, ("qka", 1))
            for d in range(2):
                v.tensor_tensor(eq[:, 2 * d:2 * d + 2, :], eq[:, 2 * d:2 * d + 2, :], qka[:, 0:2, :], ALU.mult).then_inc(S("qe"), 1)
            v.wait_ge(S("gla_fexp"), 1)
            for d in range(2):
                for kc in range(2):
                    ins = v.tensor_scalar(S0[:, d, kc, :], S0[:, d, kc, :], fexp[:, 2 * d + kc, 0:1], None, ALU.mult)
            ins.then_inc(S("state_first"), 1)
            v.wait_ge(S("A_cleared"), 1)
            v.wait_ge(S("rec_tables_loaded"), 16)
            for d in range(2):
                for j in range(NT):
                    full(v, ("A", d, j))
                    free(v.copy_predicated(A_sb[:, d, j, :].rearrange("p (h t) -> p h t", h=H), bc(amask[d].unsqueeze(1), [P, H, P]),
                                           bank(("A", d, j))[:].rearrange("p (h t) -> p h t", h=H)), ("A", d, j))
            v.wait_ge(S("state_first"), 1)
            for d in range(2):
                full(v, ("kv", d, 1))
                free(v.tensor_tensor(S3[:, d, :, :], bank(("kv", d, 1))[:, 0:2 * DV].rearrange("p (k v) -> p k v", k=2), S0[:, d, :, :], ALU.add), ("kv", d, 1))
                evacuated(v, ("kv", d, 1))
                for kc in range(2):
                    ins = v.tensor_scalar(S3[:, d, kc, :], S3[:, d, kc, :], fexp[:, 2 * d + kc, 1:2], None, ALU.mult)
                ins.then_inc(S("state_second"), 1)
            for j in range(NT):
                v.wait_ge(S("gla_squares"), j + 1)
                v.tensor_reduce(rms[:, 0, j, 0:4], osq[:, j, :].rearrange("p (h n) -> p h n", h=H), AX.X, ALU.add).then_inc(S("gla_sums"), 1)
                evacuated(v, ("ra", j))
                free(v.tensor_tensor(mix_tok[:, j, 0:512], mix_tok[:, j, 0:512], bank(("oa", j))[:], ALU.mult), ("oa", j))
            v.wait_ge(S("atok"), 1)
            evacuated(v, "kbt")
            SPAN = (((0, 0, P), (1, P, 3 * P), (2, 3 * P, 4 * P)), ((0, 0, P), (1, P, 2 * P), (2, 2 * P, 4 * P)))
            FROM = ((0, P, 2 * P), (0, P, P))
            def weigh(h, d):
                c = 4 * d + h
                v.wait_ge(S("qin_exp"), 2 * h + d + 1)
                full(v, ("nM", d, h))
                for (s, o0, o1), t0 in zip(SPAN[d], FROM[d]):
                    ins = v.scalar_tensor_tensor(Wm[:, c, o0:o1], bank(("nM", d, h))[:, t0:t0 + o1 - o0],
                                                 atok[:, s, 32 * d + h:32 * d + h + 1], mneg[d][:, o0:o1], ALU.add, ALU.min)
                free(ins, ("nM", d, h))

            def times_qk(h, d):
                c = 4 * d + h
                kc, r0 = h // 2, (h % 2) * DK
                v.wait_ge(S("weights"), 2 * h + d + 1)
                end = (LP - 1, 0)[d]
                chain(v.tensor_scalar(kw[:, c, :], kbt[:, kc, r0:r0 + DK], Wm[:, c, end:end + 1], None, ALU.mult))
                full(v, "qk0")
                ins = v.tensor_tensor(Wm[:, c, 0:P], Wm[:, c, 0:P], bank("qk0")[:, h * P:(h + 1) * P], ALU.mult)
                if h == H - 1 and d == 1:
                    free(ins, "qk0")
                full(v, ("qk", h))
                for s, o0, o1 in SPAN[d][1:]:
                    q0 = {(0, 1): 0, (0, 2): 384, (1, 1): 0, (1, 2): 256}[(d, s)]
                    ins = v.tensor_tensor(Wm[:, c, o0:o1], Wm[:, c, o0:o1], bank(("qk", h))[:, q0:q0 + o1 - o0], ALU.mult)
                    if d == 0 and s == 2:
                        ins.then_inc(S("P_fwd"), 1)
                    elif d == 1 and s == 2:
                        free(ins, ("qk", h))
            for h in range(H):
                for d in range(2):
                    weigh(h, d)
                for d in range(2):
                    times_qk(h, d)
            n = 0
            for j in range(NT):
                for d in range(2):
                    for hp in range(2):
                        key = ("num", j, d, hp)
                        den = dn[:, 2 * (n % 4):2 * (n % 4) + 2]
                        v.wait_ge(S("den_abs"), n + 1)
                        chain(v.tensor_tensor(den, den, emt[:, j, 32 * d + 2 * hp:32 * d + 2 * hp + 2], ALU.max))
                        chain(v.reciprocal(den, den))
                        full(v, key)
                        for hh_ in range(2):
                            dst = hs[:, j, (2 * hp + hh_) * DV:(2 * hp + hh_ + 1) * DV]
                            src = bank(key)[:, hh_ * 129:hh_ * 129 + DV]
                            if d == 0:
                                ins = v.tensor_scalar(dst, src, den[:, hh_:hh_ + 1], None, ALU.mult)
                            else:
                                ins = v.scalar_tensor_tensor(dst, src, den[:, hh_:hh_ + 1], dst, ALU.mult, ALU.add)
                            if hh_ == 0:
                                chain(ins)
                        free(ins, key)
                        evacuated(v, key)
                        n += 1
                        v.nop().then_inc(S("den_read"), 1)
                    v.nop().then_inc(S("h_sum"), 1)
                v.wait_ge(S("h_squares"), j + 1)
                v.tensor_reduce(rms[:, 0, j, 4:8], osq[:, j, :].rearrange("p (h n) -> p h n", h=H), AX.X, ALU.add).then_inc(S("sums"), 1)
                chain(v.tensor_tensor(mix_tok[:, j, 512:], mix_tok[:, j, 512:], hs[:, j, :], ALU.mult))
                v.wait_ge(S("head_rms"), j + 1)
                chain(v.reciprocal(rms[:, 2, j, :], rms[:, 1, j, :]))
                for h in range(2 * H):
                    w = gnw[:, 0:DV] if h < H else gnw[:, DV:]
                    y = mix_tok[:, j, h * DV:(h + 1) * DV]
                    ins = v.scalar_tensor_tensor(y, y, rms[:, 2, j, h:h + 1], w, ALU.mult, ALU.mult)
                ins.then_inc(S("mix"), 1)
            for m in range(DC):
                residual(("ro", m), m, 0, 2)

            def first_of(out, vals, tmp, top):
                chain(v.tensor_reduce(top, vals, AX.X, ALU.max))
                chain(v.tensor_tensor(tmp, vals, bc(top.unsqueeze(2), [P, NT, 4]), ALU.is_equal))
                chain(v.tensor_tensor(tmp, tmp, bc(w4.unsqueeze(1), [P, NT, 4]), ALU.mult))
                chain(v.tensor_reduce(R1[9], tmp, AX.X, ALU.max))
                chain(v.tensor_tensor(out, tmp, bc(R1[9].unsqueeze(2), [P, NT, 4]), ALU.is_equal))

            def moe(l):
                modulate(f"moe{l}")
                full(v, ("routeT", l))
                free(v.tensor_copy(logitT, bank(("routeT", l))[0:NG + NE, 0:T]), ("routeT", l))
                full(v, ("route", l))
                v.wait_ge(S("router_loaded"), 16 * 8)
                free(v.tensor_tensor(lg, bank(("route", l))[:, 0:60].rearrange("p (j c) -> p j c", j=NT),
                                     bc(b20[:, l, :].unsqueeze(1), [P, NT, 20]), ALU.add), ("route", l))
                evacuated(v, ("route", l))
                goh, tmp, ein, oh1, oh2, e2, gin, gmsk, t4 = R4[:9]
                gmax, m1, m2, esum, pg, w1, w2 = R1[:7]
                pl, mask, gate, o1, o2, posm, t16, rows = R16
                gl = lg[:, :, 0:NG]
                first_of(goh, gl, tmp, gmax)
                chain(v.tensor_tensor(R5[0][:, :, 0:4], gl, bc(gmax.unsqueeze(2), [P, NT, 4]), ALU.subtract))
                el = lg[:, :, NG:].rearrange("p j (g e) -> p j g e", g=NG)
                t44 = t16.rearrange("p j (g e) -> p j g e", g=NG)
                chain(v.tensor_tensor(t44, el, bc(goh.unsqueeze(3), [P, NT, NG, EPG]), ALU.mult))
                chain(v.tensor_reduce(ein, t16.rearrange("p j (g e) -> p j e g", g=NG), AX.X, ALU.add))
                first_of(oh1, ein, tmp, m1)
                chain(v.scalar_tensor_tensor(e2, oh1, NEG, ein, ALU.mult, ALU.add))
                first_of(oh2, e2, tmp, m2)
                v.tensor_tensor(R5[0][:, :, 4:5], m2.unsqueeze(2), m1.unsqueeze(2), ALU.subtract).then_inc(S("exp_in"), 1)
                g4 = goh.unsqueeze(3)
                for oh, dst in ((oh1, o1), (oh2, o2)):
                    chain(v.tensor_tensor(dst.rearrange("p j (g e) -> p j g e", g=NG), bc(g4, [P, NT, NG, EPG]),
                                          bc(oh.unsqueeze(2), [P, NT, NG, EPG]), ALU.mult))
                v.tensor_tensor(mask, o1, o2, ALU.add).then_inc(S("mask"), 1)
                v.wait_ge(S("exp_out"), l + 1)
                chain(v.tensor_reduce(esum, R5[1][:, :, 0:4], AX.X, ALU.add))
                e5 = R5[1][:, :, 4:5]
                chain(v.tensor_scalar(w1.unsqueeze(2), e5, 1.0, None, ALU.add))
                chain(v.tensor_tensor(w1, w1, esum, ALU.mult))
                chain(v.reciprocal(w1, w1))
                chain(v.tensor_tensor(w2.unsqueeze(2), w1.unsqueeze(2), e5, ALU.mult))
                chain(v.tensor_tensor(gate, o1, bc(w1.unsqueeze(2), [P, NT, NE]), ALU.mult))
                chain(v.tensor_tensor(t16, o2, bc(w2.unsqueeze(2), [P, NT, NE]), ALU.mult))
                chain(v.tensor_tensor(gid[:, :, :, 1:2], gate.unsqueeze(3), t16.unsqueeze(3), ALU.add))
                chain(v.tensor_copy(gid[:, :, :, 0:1], bc(tokid.unsqueeze(2).unsqueeze(3), [P, NT, NE, 1])))
                full(v, ("pos", l))
                chain(v.tensor_scalar(posm, mask, -BIG, BIG, ALU.mult, ALU.add))
                chain(v.tensor_copy(pl, bank(("pos", l))[:, 0:48].rearrange("p (j e) -> p j e", j=NT)))
                free(v.tensor_tensor(posm, posm, pl, ALU.add), ("pos", l))
                evacuated(v, ("pos", l))
                full(v, ("cnt", l))
                chain(v.tensor_reduce(cmax[:, 0:1], bank(("cnt", l))[:, 0:NE], AX.X, ALU.max))
                free(v.tensor_copy(flag, cmax[:, 0:1]), ("cnt", l))
                evacuated(v, ("cnt", l))
                v.nop().then_inc(S("overflow_flag"), 1)
                for j in range(NT):
                    v.tensor_tensor(pall[:, j, :, :], bc(iota.unsqueeze(1), [P, NE, P]),
                                    bc(posm[:, j, :].unsqueeze(2), [P, NE, P]), ALU.is_equal).then_inc(S("slot_lists"), 1)
                chain(v.tensor_scalar(rows, pl, float(P), float(NE * P - P), ALU.is_ge, ALU.mult))
                chain(v.tensor_tensor(rows, rows, pl, ALU.add))
                chain(v.tensor_scalar(t16, pl, float(2 * P), float(NE * P - P), ALU.is_ge, ALU.mult))
                chain(v.tensor_tensor(rows, rows, t16, ALU.add))
                chain(v.tensor_tensor(rows, rows, bc(ebase.unsqueeze(1), [P, NT, NE]), ALU.add))
                for q, oh in ((0, o1), (1, o2)):
                    chain(v.tensor_tensor(t16, rows, oh, ALU.mult))
                    chain(v.tensor_reduce(R1[7 + q], t16, AX.X, ALU.add))
                    chain(v.tensor_copy(ridx[:, :, q:q + 1], R1[7 + q].unsqueeze(2)))
                for key, first, last in ((("idx0", l), 0, 2), (("idx", l), 2, NE)):
                    full(v, key)
                    src = bank(key)[:, 2 * first:2 * last].rearrange("p (e c) -> p e c", c=2)
                    chain(v.tensor_copy(gslot[:, first:last].unsqueeze(2), src[:, :, 1:2]))
                    free(v.tensor_copy(idxu[:, first:last].unsqueeze(2), src[:, :, 0:1]), key)

                if l == 0:
                    ada_out(1)

                def rows_in(it, u):
                    full(v, (l, u, "X", 1), it)
                    free(v.tensor_copy(xg[:, u, 4:8, :], bank((l, u, "X", 1))[:].rearrange("p (k s) -> p k s", k=4)), (l, u, "X", 1))
                    v.tensor_copy(gcol[:, u:u + 1], gslot[:, bass.ds(2 * it + u, 1)]).then_inc(S(f"gate{u}_ready"), 1)

                def hidden_t(it, u):
                    full(v, (l, u, "HT"), it)
                    free(v.tensor_copy(hT, bank((l, u, "HT"))[:]), (l, u, "HT"))

                def hidden(it, u):
                    full(v, (l, u, "U"), it)
                    evacuated(v, (l, u, "G"), it)
                    v.wait_ge(S(f"gate{u}_ready"), it + 1 + l * (NE // 2))
                    free(v.scalar_tensor_tensor(hh, bank((l, u, "U"))[:], gcol[:, u:u + 1], sg[:, u, :], ALU.mult, ALU.mult), (l, u, "U"))

                def rows_out(it, u):
                    full(v, (l, u, "Y", 1), it)
                    if not isinstance(it, int) or it + l:
                        v.wait_ge(S(f"y{u}_stored"), it * 16 + l * (NE // 2) * 16)
                    free(v.tensor_copy(ysb[:, u, 512:], bank((l, u, "Y", 1))[:]), (l, u, "Y", 1))

                def two(it):
                    for it_e, u, it_before, it_next in ((it, 1, it, it + 1), (it + 1, 0, it, it + 1)):
                        hidden_t(it_before, 1 - u)
                        hidden(it_e, u)
                        rows_out(it_before, 1 - u)
                        rows_in(it_next, 1 - u)

                v.wait_ge(S("u_rows_stored"), 16 * NT * (l + 1))
                rows_in(0, 0)
                hidden(0, 0)
                rows_in(0, 1)
                two(0)
                with v.Fori(1, NE // 2 - 1) as it:
                    two(it)
                hidden_t(NE // 2 - 1, 0)
                hidden(NE // 2 - 1, 1)
                rows_out(NE // 2 - 1, 0)
                hidden_t(NE // 2 - 1, 1)
                rows_out(NE // 2 - 1, 1)
                over = v.value_load(flag[0:1, 0:1], min_val=0, max_val=T)
                with v.If(over > P):
                    full(v, (l, 1, "Y", 1), NE // 2 - 1)
                    for c in range(1, NT):
                        v.wait_ge(S(f"over{l}_y_stored"), 16 * NE * (c - 1) + 16)
                        v.tensor_scalar(t16, posm, float(-P * c), None, ALU.add).then_inc(S(f"over{l}_pos"), 1)
                        v.wait_ge(S(f"over{l}_pos"), c)
                        for j in range(NT):
                            v.tensor_tensor(pall[:, j, :, :], bc(iota.unsqueeze(1), [P, NE, P]),
                                            bc(t16[:, j, :].unsqueeze(2), [P, NE, P]), ALU.is_equal).then_inc(S(f"over{l}_lists"), 1)
                        v.wait_ge(S(f"over{l}_idx_mm"), c)
                        pi = ps[7][:, 0:32].rearrange("p (e c) -> p e c", c=2)
                        v.tensor_copy(ogate.unsqueeze(2), pi[:, :, 1:2])
                        v.tensor_copy(oidx.unsqueeze(2), pi[:, :, 0:1]).then_inc(S(f"over{l}_idx"), 1)
                        v.wait_ge(S(f"over{l}_idx"), c)
                        with v.Fori(0, NE) as e:
                            n = e + NE * (c - 1)
                            v.wait_ge(S(f"over{l}_x"), n + 1)
                            v.tensor_copy(xg[:, 0, 4:8, :], ps[1][:].rearrange("p (k s) -> p k s", k=4)).then_inc(S(f"over{l}_xcopy"), 1)
                            v.tensor_copy(gcol[:, 0:1], ogate[:, bass.ds(e, 1)]).then_inc(S(f"over{l}_gcol"), 1)
                            v.wait_ge(S(f"over{l}_silu"), n + 1)
                            v.wait_ge(S(f"over{l}_gcol"), n + 1)
                            v.scalar_tensor_tensor(hh, ps[3][:], gcol[:, 0:1], sg[:, 0, :], ALU.mult, ALU.mult).then_inc(S(f"over{l}_h"), 1)
                            v.wait_ge(S(f"over{l}_ht"), n + 1)
                            v.tensor_copy(hT, ps[4][:]).then_inc(S(f"over{l}_hT"), 1)
                            v.wait_ge(S(f"over{l}_ya"), n + 1)
                            v.tensor_copy(ysb[:, 0, 512:], ps[6][:]).then_inc(S(f"over{l}_y"), 1)
                    v.wait_ge(S(f"over{l}_y_stored"), 16 * NE * OVF + 16)
                with v.Else():
                    v.nop()
                for j in range(NT):
                    v.wait_ge(S(f"token_rows_{j}"), 32 * (l + 1))
                    v.tensor_tensor(cmb[:, 0, j, :], cmb[:, 0, j, :], cmb[:, 1, j, :], ALU.add).then_inc(S("y_sum"), 1)
                for j in range(NT):
                    for hf in range(2):
                        key = ("yT", l, j, hf)
                        full(v, key)
                        for n in range(4):
                            m = 4 * hf + n
                            x = xT[:, m, j * P:(j + 1) * P]
                            ins = v.scalar_tensor_tensor(x, bank(key)[:, n * P:(n + 1) * P], mod(l, 5, m, min(j, 1)), x, ALU.mult, ALU.add)
                        free(ins, key)

            moe(0)
            modulate("hy")
            TWO_PI_HI, MAGIC = 6.28125, 1.5 * 2 ** 23
            def sin_argument(n, key):
                full(v, key)
                if n == 1:
                    v.wait_ge(S("sin_out"), 1)
                free(v.tensor_scalar(srt[:, 0, :], bank(key)[0:64, 0:T], fprm[:, 2 * n:2 * n + 1], fprm[:, 2 * n + 1:2 * n + 2],
                                     ALU.add, ALU.mult), key)
                evacuated(v, key)
                chain(v.tensor_scalar(srt[:, 1, :], srt[:, 0, :], 1.0 / (2 * math.pi), MAGIC, ALU.mult, ALU.add))
                chain(v.tensor_scalar(srt[:, 1, :], srt[:, 1, :], MAGIC, None, ALU.subtract))
                chain(v.scalar_tensor_tensor(srt[:, 0, :], srt[:, 1, :], -TWO_PI_HI, srt[:, 0, :], ALU.mult, ALU.add))
                chain(v.scalar_tensor_tensor(srt[:, 0, :], srt[:, 1, :], -(2 * math.pi - TWO_PI_HI), srt[:, 0, :], ALU.mult, ALU.add))
                v.tensor_scalar(srt[:, 0, :], srt[:, 0, :], 3.1415925, -3.1415925, ALU.min, ALU.max).then_inc(S("sin_in"), 1)
            for m in range(3 * DC):
                if m in (2, 4):
                    sin_argument(m // 2 - 1, ("f1", "f2")[m // 2 - 1])
                dst = zc[:, m % 2, :] if m < 2 * DC else x2T[:, m - 2 * DC, :]
                src = bank(("z", m))
                full(v, ("z", m))
                v.wait_ge(S("conv_mid"), m + 1)
                for tap, so, do in ((0, 0, 1), (2, 1, 0)):
                    w = col(V_CONV + tap * 3 * DC + m)
                    for a0, a1 in SEQS:
                        n = a1 - a0 - 1
                        ins = v.scalar_tensor_tensor(dst[:, a0 + do:a0 + do + n], src[:, a0 + so:a0 + so + n], w,
                                                     dst[:, a0 + do:a0 + do + n], ALU.mult, ALU.add)
                    if tap == 0:
                        chain(ins)
                free(ins, ("z", m))
            def filters(c, od):
                v.wait_ge(S("decay_loaded"), 16 * (c + 1))
                if c or od:
                    v.wait_ge(S("spectrum"), 6 * (2 * c + od))
                if c == 0 and od == 0:
                    full(v, ("zt", 2 * DC - 1))
                for j in range(NT):
                    kf, kb_ = ("filt", c, od, j, 0), ("filt", c, od, j, 1)
                    full(v, kf)
                    full(v, kb_)
                    if c or od or j:
                        v.wait_ge(S("filters"), NT * (2 * c + od) + j)
                    free(v.tensor_tensor(htmp, bank(kf)[:], dcy[:, j, :], ALU.mult), kf)
                    free(v.scalar_tensor_tensor(hpm[:, j, 1, :], bank(kb_)[:], notfirst if j < 2 else ones[:, 0:1],
                                                dcy[:, j, :], ALU.mult, ALU.mult), kb_)
                    evacuated(v, kb_)
                    v.tensor_tensor(hpm[:, j, 0, :], htmp, hpm[:, j, 1, :], ALU.add)
                    v.tensor_tensor(hpm[:, j, 1, :], htmp, hpm[:, j, 1, :], ALU.subtract).then_inc(S("filters"), 1)

            filters(0, 0)
            for c in range(2):
                for od in range(2):
                    full(v, ("K", c, od, 7))
                    for q in range(8):
                        evacuated(v, ("K", c, od, q))
                    for pr, (p1, p2, p3) in enumerate(((0, 1, 2), (3, 5, 7), (4, 6, 4))):
                        re, im = ("F", c, od, 2 * pr), ("F", c, od, 2 * pr + 1)
                        full(v, im)
                        v.tensor_tensor(Yf[:, 2 * pr, :], Kf[:, p1, :], bank(re)[:], ALU.mult)
                        free(v.tensor_tensor(Yf[:, 2 * pr + 1, :], Kf[:, p2, :], bank(re)[:], ALU.mult), re)
                        v.tensor_tensor(ptmp[:, 2 * pr, :], Kf[:, p2, :], bank(im)[:], ALU.mult)
                        free(v.tensor_tensor(ptmp[:, 2 * pr + 1, :], Kf[:, p3, :], bank(im)[:], ALU.mult), im)
                        evacuated(v, im)
                        v.nop().then_inc(S("products"), 1)
                    if (c, od) != (1, 1):
                        filters(*NEXT[(c, od)])
                    for q in range(NT if od == 0 else 4):
                        key = ("inv", c, od, q)
                        full(v, key)
                        if od == 0:
                            w = x1_tok[:, q, c * 512:(c + 1) * 512]
                            free(v.tensor_tensor(w, w, bank(key)[:], ALU.mult), key)
                        else:
                            m = 4 * c + q
                            free(v.tensor_tensor(uT[:, m, :], x2T[:, m, :], bank(key)[:, 0:T], ALU.mult), key)
            for m in range(DC):
                residual(("ho", m), m, 1, 2)
            moe(1)
            modulate("fin")
            for j in range(NT):
                full(v, ("out", j, 1))
                free(v.tensor_copy(x_out[:, j, 512:], bank(("out", j, 1))[:]), ("out", j, 1))

        @block.tensor
        def _(pe):
            def transposes(key, blocks):
                opened(pe, key)
                for at, src in blocks:
                    p, n = src.shape
                    ins = pe.transpose(bank(key)[0:n, at:at + p], src, ident[0:p, 0:p])
                done(ins, key)

            def accumulate(key, out, pairs):
                n = len(pairs)
                for i, (lhsT, rhs) in enumerate(pairs):
                    ins = pe.matmul(out, lhsT, rhs, start=(i == 0), stop=(i == n - 1))
                return ins

            pe.wait_ge(S("vec_rows_loaded"), 16 * 8)
            pe.wait_ge(S("tables_loaded"), 16)
            transposes("vec", [(0, vrows[0:60, 0, :]), (V_ADA, vrows[0:96, 1, :]), (V_CONV, vrows[0:72, 2, :])])
            nturn = [0]

            def settle(ins):
                nturn[0] += 1
                ins.then_inc(S("row_half_done"), 1)
                pe.wait_ge(S("row_half_done"), nturn[0])

            def ada_mm(l, first, last):
                for j in range(first, last):
                    key = ("adam", l, j)
                    w = loaded(pe, ("ada", l, j)).rearrange("p (k n) -> p k n", k=DC)
                    opened(pe, key)
                    done(accumulate(key, bank(key)[0:2, :], [(silc[:, k, :], w[:, k, :]) for k in range(DC)]), key)
                    if j:
                        ada_columns(l, j - 1)
                if last == 12:
                    ada_columns(l, 11)

            def ada_columns(l, j):
                key = ("ada", l)
                if j == 0:
                    opened(pe, key)
                evacuated(pe, ("adam", l, j))
                for mm in range(4):
                    m = 4 * j + mm
                    ins = pe.transpose(bank(key)[:, 2 * m:2 * m + 2], adar[:, mm * P:(mm + 1) * P], ident[0:2, 0:2])
                ins.then_inc(S("ada_rows_read"), 1)
                if j == 11:
                    pe.wait_ge(S("ada_rows_read"), 12 * l + 12)
                    done(pe.nop(), key)

            def ada_step(j):
                key = ("adam", 1, j)
                w = loaded(pe, ("ada", 1, j)).rearrange("p (k n) -> p k n", k=DC)
                opened(pe, key)
                done(accumulate(key, bank(key)[0:2, :], [(silc[:, k, :], w[:, k, :]) for k in range(DC)]), key)
                for before in ([j - 1] if j else []) + ([11] if j == 11 else []):
                    key = ("adac", before)
                    opened(pe, key)
                    evacuated(pe, ("adam", 1, before))
                    for mm in range(4):
                        ins = pe.transpose(bank(key)[:, 2 * mm:2 * mm + 2], adar[:, mm * P:(mm + 1) * P], ident[0:2, 0:2])
                    done(ins, key)

            def sumsq_part(name, m):
                key = ("ss", name)
                if m == 0:
                    opened(pe, key)
                    pe.wait_ge(S("ones_set"), 1)
                pe.wait_ge(S("squares"), MODS.index(name) * DC + m + 1)
                ins = pe.matmul(bank(key)[:, 0:T], ones[:], squares[name][:, m, :], start=(m == 0), stop=(m == DC - 1))
                if m == DC - 1:
                    done(ins, key)

            def sumsq(name):
                for m in range(DC):
                    sumsq_part(name, m)

            def all_u(name):
                for m in range(DC):
                    u_ready(pe, name, m)

            def wide(key, w, rows=P, fresh=None):
                opened(pe, key)
                for k in range(DC):
                    if fresh is not None:
                        u_ready(pe, fresh, k)
                    ins = pe.matmul(bank(key)[0:rows, 0:T], w(k), uT[:, k, :], start=(k == 0), stop=(k == DC - 1))
                done(ins, key)

            pe.wait_ge(S("silu_c"), 1)
            ada_mm(0, 0, 6)
            pe.wait_ge(S("x_loaded"), 48)
            for j in range(NT):
                if j == 1:
                    pe.wait_ge(S("x_pos"), 1)
                for hf in range(2):
                    transposes(("x", j, hf), [(n * P, x_in[:, j, (4 * hf + n) * P:(4 * hf + n + 1) * P]) for n in range(4)])
            sumsq("rec")
            ada_mm(0, 6, 12)
            w = loaded(pe, ("rec", 0)).rearrange("p (k n) -> p k n", k=DC)
            for m in range(4):
                wide(("qka", m), lambda k: w[:, k, m * P:(m + 1) * P], fresh="rec" if m == 0 else None)
            pe.wait_ge(S("wg_loaded"), 16 * 5)
            wide("gk", lambda k: wg[:, k, 0:32], 32)
            wide("mg", lambda k: wg[:, k, 32:160])
            w = loaded(pe, ("rec", 3)).rearrange("p (k n) -> p k n", k=DC)
            for m in range(4):
                wide(("qkb", m), lambda k: w[:, k, m * P:(m + 1) * P])
            evacuated(pe, "gk")
            pe.wait_ge(S("rec_small_loaded"), 16 * REC_SMALL)
            for m in range(4):
                opened(pe, ("glog", m))
                done(pe.matmul(bank(("glog", m))[:, 0:T], gkw[:, m * P:(m + 1) * P], gkT, start=True, stop=True), ("glog", m))
            for name, jb in (("va", 1), ("vb", 4), ("ra", 2), ("ob", 5)):
                w = loaded(pe, ("rec", jb)).rearrange("p (k n) -> p k n", k=DC)
                for j in range(NT):
                    key = (name, j)
                    opened(pe, key)
                    done(accumulate(key, bank(key)[:], [(uT[:, k, j * P:(j + 1) * P], w[:, k, :]) for k in range(DC)]), key)
            def head(h):
                return h // 2, (h % 2) * DK
            pe.wait_ge(S("ke"), 2)
            for k in range(4):
                d = k // 2
                j = (0, 1 + d)[k % 2]
                transposes(("keT", k), [(kc * P, ek[:, 2 * d + kc, j * P:(j + 1) * P]) for kc in range(2)])
            pe.wait_ge(S("qe"), 2)
            for d in range(2):
                for j in range(NT):
                    key = ("A", d, j)
                    opened(pe, key)
                    t = slice(j * P, (j + 1) * P)
                    for h in (0, 2, 1, 3):
                        kc, r0 = head(h)
                        if h == 1:
                            settle(ins)
                        ins = pe.matmul(bank(key)[:, h * P:(h + 1) * P], ek[r0:r0 + DK, 2 * d + kc, t],
                                        eq[r0:r0 + DK, 2 * d + kc, t], start=True, stop=True)
                    done(ins, key)
            for w_ in range(2):
                for d in range(2):
                    key = ("kv", d, w_)
                    k = 2 * d + w_
                    j = (0, (1, 2)[d])[w_]
                    evacuated(pe, ("keT", k))
                    evacuated(pe, ("va", j))
                    opened(pe, key)
                    for h in range(H):
                        kc, r0 = head(h)
                        ins = pe.matmul(bank(key)[r0:r0 + DK, kc * DV:(kc + 1) * DV], ke_s[:, 2 * k + kc, r0:r0 + DK],
                                        va[:, j, h * DV:(h + 1) * DV], start=True, stop=True)
                    done(ins, key)
            for j in range(NT):
                key = ("oa", j)
                evacuated(pe, ("va", j))
                for d in range(2):
                    evacuated(pe, ("A", d, j))
                if j:
                    pe.wait_ge(S("state_first"), 1)
                    pe.wait_ge(S("state_second"), 2)
                opened(pe, key)
                for h in (0, 2, 1, 3):
                    kc, r0 = head(h)
                    if h == 1 and j:
                        settle(ins)
                    pairs = [(A_sb[:, d, j, h * P:(h + 1) * P], va[:, j, h * DV:(h + 1) * DV]) for d in range(2)]
                    if j:
                        for d in range(2):
                            first = j == (1, 2)[d]
                            st = (S0 if first else S3)[r0:r0 + DK, d, kc, :]
                            pairs.append((eq[r0:r0 + DK, 2 * d + kc, j * P:(j + 1) * P], st))
                    ins = accumulate(key, bank(key)[:, h * DV:(h + 1) * DV], pairs)
                done(ins, key)
            pe.wait_ge(S("m_rows"), 1)
            transposes("mtok", [((q * NT + j) * 36, g36[:, row, j * P:(j + 1) * P]) for q, row in enumerate((4, 6)) for j in range(NT)])
            for m in range(4):
                evacuated(pe, ("qkb", m))
            opened(pe, "qk0")
            for h in (0, 2, 1, 3):
                kc, r0 = head(h)
                if h == 1:
                    settle(ins)
                ins = pe.matmul(bank("qk0")[:, h * P:(h + 1) * P], qkb[r0:r0 + DK, 2 + kc, 0:P], qkb[r0:r0 + DK, kc, 0:P], start=True, stop=True)
            done(ins, "qk0")
            transposes("kbt", [(kc * P, qkb[:, 2 + kc, 0:P]) for kc in range(2)])
            for h in range(H):
                kc, r0 = head(h)
                opened(pe, ("qk", h))
                for s in range(2):
                    ins = pe.matmul(bank(("qk", h))[:, s * LS:(s + 1) * LS], qkb[r0:r0 + DK, 2 + kc, (s + 1) * P:(s + 2) * P],
                                    qkb[r0:r0 + DK, kc, P:T], start=True, stop=True)
                done(ins, ("qk", h))
                for d in range(2):
                    key = ("nM", d, h)
                    opened(pe, key)
                    r = 32 * d + h
                    done(pe.matmul(bank(key)[:, 0:T], bc(ident[0:36, r:r + 1], [36, P]), g36[:, 5, :], start=True, stop=True), key)
            evacuated(pe, ("qk", H - 1))
            evacuated(pe, ("vb", NT - 1))
            pe.wait_ge(S("vb_ones"), 1)
            for d in range(2):
                key = ("C", d)
                opened(pe, key)
                for h in range(H):
                    kc, r0 = head(h)
                    ins = pe.matmul(bank(key)[r0:r0 + DK, kc * 129:(kc + 1) * 129], kw[:, 4 * d + h, :], vb[:, 0, h, :], start=True, stop=True)
                done(ins, key)
            pe.wait_ge(S("qin"), 2)
            PB = {(0, 0): [(0, 0)], (0, 1): [(1, P)], (0, 2): [(1, 2 * P), (2, 3 * P)],
                  (1, 0): [(0, 0)], (1, 1): [(1, P), (2, 2 * P)], (1, 2): [(2, 3 * P)]}
            for j in range(NT):
                for d in range(2):
                    for hp in range(2):
                        key = ("num", j, d, hp)
                        opened(pe, key)
                        for hh_ in range(2):
                            h = 2 * hp + hh_
                            kc, r0 = head(h)
                            if j and hh_:
                                settle(ins)
                            pairs = [(Wm[:, 4 * d + h, o0:o0 + P], vb[:, s, h, :]) for s, o0 in PB[(d, j)]]
                            if j:
                                pairs.append((qin[r0:r0 + DK, d, kc, (j - 1) * P:j * P], C0[r0:r0 + DK, d, kc, :]))
                            ins = accumulate(key, bank(key)[:, hh_ * 129:(hh_ + 1) * 129], pairs)
                        done(ins, key)
                ada_step(j)
            for j in range(NT):
                pe.wait_ge(S("mix"), j + 1)
                for hf in range(2):
                    transposes(("mixT", j, hf), [(n * P, mix_tok[:, j, (4 * hf + n) * P:(4 * hf + n + 1) * P]) for n in range(4)])
                if j == 1:
                    ada_step(3)
            for j in range(NT):
                for hf in range(2):
                    evacuated(pe, ("mixT", j, hf))
            for jb in range(2):
                w = loaded(pe, ("ro", jb)).rearrange("p (k n) -> p k n", k=DC)
                for mm in range(4):
                    m = 4 * jb + mm
                    wide(("ro", m), lambda k: w[:, k, mm * P:(mm + 1) * P])
                    if m:
                        sumsq_part("moe0", m - 1)
            sumsq_part("moe0", DC - 1)
            ada_step(4)

            def moe(l):
                pe.wait_ge(S("router_loaded"), 16 * 8)
                wide(("routeT", l), lambda k: wr[:, k, l, :], NG + NE, fresh=f"moe{l}")
                for j in range(NT):
                    for hf in range(2):
                        transposes(("ut", l, j, hf), [(n * P, uT[:, 4 * hf + n, j * P:(j + 1) * P]) for n in range(4)])
                    if j == 1:
                        key = ("route", l)
                        opened(pe, key)
                        evacuated(pe, ("routeT", l))
                        for q in range(NT):
                            ins = pe.transpose(bank(key)[:, 20 * q:20 * q + 20], logitT[:, q * P:(q + 1) * P], ident[0:20, 0:20])
                        done(ins, key)
                if l == 0:
                    for j in range(ADA1[0], ADA1[1]):
                        ada_step(j)
                mask = R16[1]
                pe.wait_ge(S("mask"), l + 1)
                key = ("pos", l)
                opened(pe, key)
                for j in range(NT):
                    pairs = [(ones[:], mask[:, q, :]) for q in range(j)] + [(strict, mask[:, j, :])]
                    ins = accumulate(key, bank(key)[:, 16 * j:16 * j + 16], pairs)
                done(ins, key)
                key = ("cnt", l)
                opened(pe, key)
                done(accumulate(key, bank(key)[:, 0:NE], [(ones[:], mask[:, q, :]) for q in range(NT)]), key)
                if l == 0:
                    for j in range(ADA1[1], ADA1[2]):
                        ada_step(j)
                pe.wait_ge(S("slot_lists"), NT * (l + 1))
                for g in range(4):
                    key = ("idxT", l, g)
                    opened(pe, key)
                    for q in range(4):
                        e = 4 * g + q
                        ins = accumulate(key, bank(key)[0:2, q * P:(q + 1) * P], [(gid[:, j, e, :], pall[:, j, e, :]) for j in range(NT)])
                    done(ins, key)
                for key, first, last in ((("idx0", l), 0, 2), (("idx", l), 2, NE)):
                    opened(pe, key)
                    for e in range(first, last):
                        if e % 4 == 0 or e == 2:
                            evacuated(pe, ("idxT", l, e // 4))
                        ins = pe.transpose(bank(key)[:, 2 * e:2 * e + 2], idxT[:, e * P:(e + 1) * P], ident[0:2, 0:2])
                    done(ins, key)
                if l == 0:
                    for j in range(ADA1[2], ADA1[3]):
                        ada_step(j)
                base = moe_base[l]

                def t8(key, it, n0, u):
                    opened(pe, key, it)
                    for n in range(4):
                        ins = pe.transpose(bank(key)[:, n * P:(n + 1) * P], ug[:, u, (n0 + n) * P:(n0 + n + 1) * P], ident)
                    done(ins, key)

                def gathered(it, u):
                    pe.wait_ge(S(f"rows{u}_gathered"), (it + l * (NE // 2)) * 16 + 16)
                    t8((l, u, "X", 0), it, 0, u)
                    t8((l, u, "X", 1), it, 4, u)

                def slot(it, u, kind):
                    n = 3 * u + kind
                    pe.wait_ge(S(f"slot{n}_loaded"), 16 * base[n] + 16 + it * 16)
                    return ring[:, n, :]

                def project(it, u, kind):
                    if kind == 0:
                        evacuated(pe, (l, u, "X", 0), it)
                        evacuated(pe, (l, u, "X", 1), it)
                    key = (l, u, "GU"[kind])
                    w = slot(it, u, kind).rearrange("p (k n) -> p k n", k=DC)
                    opened(pe, key, it)
                    done(accumulate(key, bank(key)[:], [(xg[:, u, k, :], w[:, k, :]) for k in range(DC)]), key)

                def hidden_t(it, u):
                    key = (l, u, "HT")
                    opened(pe, key, it)
                    evacuated(pe, (l, u, "U"), it)
                    for n in range(4):
                        ins = pe.transpose(bank(key)[:, n * P:(n + 1) * P], hh[:, n * P:(n + 1) * P], ident)
                    done(ins, key)

                def down(it, u):
                    evacuated(pe, (l, u, "HT"), it)
                    w = slot(it, u, 2).rearrange("p (k n) -> p k n", k=4)
                    for q in range(2):
                        key = (l, u, "Y", q)
                        opened(pe, key, it)
                        done(accumulate(key, bank(key)[:], [(hT[:, k * P:(k + 1) * P], w[:, k, q * 512:(q + 1) * 512]) for k in range(4)]), key)

                gathered(0, 0)
                project(0, 0, 0)
                project(0, 0, 1)
                gathered(0, 1)
                with pe.Fori(0, NE // 2 - 1) as it:
                    for it_e, u in ((it, 1), (it + 1, 0)):
                        project(it_e, u, 0)
                        hidden_t(it, 1 - u)
                        project(it_e, u, 1)
                        down(it, 1 - u)
                        gathered(it + 1, 1 - u)
                it = NE // 2 - 1
                project(it, 1, 0)
                hidden_t(it, 0)
                project(it, 1, 1)
                down(it, 0)
                hidden_t(it, 1)
                down(it, 1)
                pe.wait_ge(S("overflow_flag"), l + 1)
                over = pe.value_load(flag[0:1, 0:1], min_val=0, max_val=T)
                with pe.If(over > P):
                    for q in range(2):
                        evacuated(pe, (l, 1, "Y", q), NE // 2 - 1)
                    for c in range(1, NT):
                        pe.wait_ge(S(f"over{l}_lists"), NT * c)
                        for e in range(NE):
                            ins = accumulate(None, ps[7][:, 2 * e:2 * e + 2], [(pall[:, j, e, :], gid[:, j, e, :]) for j in range(NT)])
                        ins.then_inc(S(f"over{l}_idx_mm"), 1)
                        with pe.Fori(0, NE) as e:
                            n = e + NE * (c - 1)
                            pe.wait_ge(S(f"over{l}_rows"), 16 * n + 16)
                            for k in range(DC):
                                ins = pe.transpose(ps[k // 4][:, (k % 4) * P:(k % 4 + 1) * P], ug[:, 0, k * P:(k + 1) * P], ident)
                            ins.then_inc(S(f"over{l}_x"), 1)
                            pe.wait_ge(S(f"over{l}_xcopy"), 2 * n + 2)
                            pe.wait_ge(S(f"over{l}_xcopy"), 2 * n + 2)
                            for kind in range(2):
                                pe.wait_ge(S(f"over{l}_loaded"), 48 * n + 48)
                                w = ring[:, kind, :].rearrange("p (k n) -> p k n", k=DC)
                                ins = accumulate(None, ps[2 + kind][:], [(xg[:, 0, k, :], w[:, k, :]) for k in range(DC)])
                            ins.then_inc(S(f"over{l}_gu"), 1)
                            pe.wait_ge(S(f"over{l}_h"), n + 1)
                            for k in range(4):
                                ins = pe.transpose(ps[4][:, k * P:(k + 1) * P], hh[:, k * P:(k + 1) * P], ident)
                            ins.then_inc(S(f"over{l}_ht"), 1)
                            pe.wait_ge(S(f"over{l}_hT"), n + 1)
                            pe.wait_ge(S(f"over{l}_loaded"), 48 * n + 48)
                            w = ring[:, 2, :].rearrange("p (k n) -> p k n", k=4)
                            for q in range(2):
                                ins = accumulate(None, ps[5 + q][:], [(hT[:, k * P:(k + 1) * P], w[:, k, q * 512:(q + 1) * 512]) for k in range(4)])
                            ins.then_inc(S(f"over{l}_down"), 1)
                    pe.wait_ge(S(f"over{l}_y_stored"), 16 * NE * OVF + 16)
                with pe.Else():
                    pe.nop()
                pe.nop()
                for j in range(NT):
                    pe.wait_ge(S("y_sum"), NT * l + j + 1)
                    for hf in range(2):
                        transposes(("yT", l, j, hf), [(n * P, cmb[:, 0, j, (4 * hf + n) * P:(4 * hf + n + 1) * P]) for n in range(4)])

            moe(0)
            sumsq("hy")

            def zt(m):
                evacuated(pe, ("z", m))
                transposes(("zt", m), [(j * P, zc[:, m % 2, j * P:(j + 1) * P]) for j in range(NT)])

            for m in range(3 * DC):
                if m % 4 == 0:
                    w = loaded(pe, ("hin", m // 4)).rearrange("p (k n) -> p k n", k=DC)
                wide(("z", m), lambda k: w[:, k, (m % 4) * P:(m % 4 + 1) * P], fresh="hy" if m == 0 else None)
                if m == 1:
                    pe.wait_ge(S("hy_small_loaded"), 16 * 7)
                    opened(pe, "f1")
                    done(pe.matmul(bank("f1")[0:64, 0:T], hw1, embT, start=True, stop=True), "f1")
                if m == 3:
                    pe.wait_ge(S("sin_out"), 1)
                    opened(pe, "f2")
                    done(pe.matmul(bank("f2")[0:64, 0:T], hw2, h1T, start=True, stop=True), "f2")
                if 1 <= m <= 2 * DC:
                    zt(m - 1)
            CP, SNP, SP, C3P, GRP, GIP = (thy[:, i * P:(i + 1) * P] for i in range(6))
            tab = [thy[:, 768 + 512 * i:1280 + 512 * i].rearrange("p (a f) -> p a f", a=2) for i in range(2)]
            CS, SNS = tab
            SS, C3S = (thy[:, 1792 + 256 * i:2048 + 256 * i].rearrange("p (a f) -> p a f", a=2) for i in range(2))
            GRS, GIS = (thy[:, 2304 + 512 * i:2816 + 512 * i].rearrange("p (a f) -> p a f", a=2) for i in range(2))
            w3 = loaded(pe, "w3")
            pe.wait_ge(S("dft_loaded"), 16)
            pe.wait_ge(S("w3_row_loaded"), 32)
            pe.wait_ge(S("h2_row"), 3)
            pe.wait_ge(S("sin_out"), 2)
            def filters(c, od):
                for j in range(NT):
                    for d in range(2):
                        key = ("filt", c, od, j, d)
                        opened(pe, key)
                        at = (2 * od + d) * D + c * 512
                        done(pe.matmul(bank(key)[:], h2T[:, j * P:(j + 1) * P], w3[0:65, at:at + 512], start=True, stop=True), key)

            filters(0, 0)
            for c in range(2):
                for od in range(2):
                    pe.wait_ge(S("filters"), NT * (2 * c + od + 1))
                    if c or od:
                        pe.wait_ge(S("products"), 3 * (2 * c + od))
                    f1, f0 = slice(P, 2 * P), slice(0, P)
                    for q, (tabs, s) in enumerate((
                        (CP, 0), (SP, 1), (C3P, 0), ((CS, f0), 0), ((CS, f1), 0), ((SS, f0), 1), ((SNS, f1), 1), ((C3S, f0), 0),
                    )):
                        key = ("K", c, od, q)
                        opened(pe, key)
                        if q < 3:
                            pairs = [(tabs, hpm[:, 0, s, :])]
                        else:
                            pairs = [(tabs[0][:, tt, tabs[1]], hpm[:, 1 + tt, s, :]) for tt in range(2)]
                        done(accumulate(key, bank(key)[:], pairs), key)
                    sig = v_tok if od == 0 else x1_tok
                    if od == 0:
                        for m in range(2 * DC):
                            evacuated(pe, ("zt", m))
                    else:
                        for q in range(NT):
                            evacuated(pe, ("inv", c, 0, q))
                    for q in range(6):
                        key = ("F", c, od, q)
                        opened(pe, key)
                        if q < 2:
                            pairs = [((CP, SNP)[q], sig[:, 0, c * 512:(c + 1) * 512])]
                        else:
                            f = (f0, f1)[(q - 2) // 2]
                            pairs = [((CS, SNS)[q % 2][:, tt, f], sig[:, 1 + tt, c * 512:(c + 1) * 512]) for tt in range(2)]
                        done(accumulate(key, bank(key)[:], pairs), key)
                    if (c, od) != (1, 1):
                        filters(*NEXT[(c, od)])
                    pe.wait_ge(S("spectrum"), 6 * (2 * c + od + 1))
                    for q in range(NT if od == 0 else 4):
                        key = ("inv", c, od, q)
                        opened(pe, key)
                        if od == 0:
                            if q == 0:
                                pairs = [(GRP, Yf[:, 0, :]), (GIP, Yf[:, 1, :])]
                            else:
                                t = slice((q - 1) * P, q * P)
                                pairs = [(g[:, ft, t], Yf[:, 2 + 2 * ft + i, :]) for ft in range(2) for i, g in enumerate((GRS, GIS))]
                            done(accumulate(key, bank(key)[:], pairs), key)
                        else:
                            ch = slice(q * P, (q + 1) * P)
                            accumulate(key, bank(key)[:, 0:P], [(Yf[:, 0, ch], GRP), (Yf[:, 1, ch], GIP)])
                            done(accumulate(key, bank(key)[:, P:T], [(Yf[:, 2 + 2 * ft + i, ch], g[:, ft, :]) for ft in range(2)
                                                                     for i, g in enumerate((GRS, GIS))]), key)
            for q in range(4):
                evacuated(pe, ("inv", 0, 1, q))
                evacuated(pe, ("inv", 1, 1, q))
            for jb in range(2):
                w = loaded(pe, ("ho", jb)).rearrange("p (k n) -> p k n", k=DC)
                for mm in range(4):
                    m = 4 * jb + mm
                    wide(("ho", m), lambda k: w[:, k, mm * P:(mm + 1) * P])
                    if m:
                        sumsq_part("moe1", m - 1)
            sumsq_part("moe1", DC - 1)
            moe(1)
            sumsq("fin")
            pe.wait_ge(S("fin_u"), DC)
            for j in range(NT):
                for hf in range(2):
                    transposes(("out", j, hf), [(n * P, uT[:, 4 * hf + n, j * P:(j + 1) * P]) for n in range(4)])


_OUTS = [(1, LP, D), (1, LS, D), (1, 1, 2, H, DK, DV), (1, 1, 2, H, DK, DV), (1, 1, 2, H, DK), (1, 1, 2, H)]


def kernel(**inputs):
    import concourse.bacc as _bacc
    from concourse.bass_utils import run_bass_kernel_spmd as _run

    nc = _bacc.Bacc("TRN2", target_bir_lowering=False, num_devices=1)
    arrays, A = {}, {}
    for name, a in list(inputs.items()) + list(tables().items()):
        a = np.ascontiguousarray(a)
        arrays[f"in_{name}"] = a
        A[name] = nc.dram_tensor(f"in_{name}", a.shape, mybir.dt.from_np(a.dtype), kind="ExternalInput").ap()
    O = [nc.dram_tensor(f"out_{i}", shape, F32, kind="ExternalOutput").ap() for i, shape in enumerate(_OUTS)]
    build(nc, A, O)
    r = _run(nc, [arrays], core_ids=[0])
    return tuple(r.results[0][f"out_{i}"] for i in range(len(_OUTS)))
```
